# Optimizing a Trainium2 kernel written in Bass

```python
import jax, jax.numpy as jnp
from jax import lax
import numpy as np

D_MODEL = 1024
BATCH = 1
SEQ = 512
DEPTH = 1

ATTN_W = D_MODEL // 2
N_ATTN_HEADS = 8
HEAD_DIM = ATTN_W // N_ATTN_HEADS
POOL_W = D_MODEL - ATTN_W
POOL_WINDOWS = (2, 4, 8, 16)
POOL_C = POOL_W // len(POOL_WINDOWS)
IN_COLS = 3 * ATTN_W + N_ATTN_HEADS + POOL_W
D_FF = 2816
CONV_W = 3
Q_BLOCK = 128
EPS = 1e-6


def _rmsnorm(x, g):
    x32 = x.astype(jnp.float32)
    y = x32 * lax.rsqrt(jnp.mean(x32 * x32, axis=-1, keepdims=True) + EPS)
    return (y * g.astype(jnp.float32)).astype(x.dtype)

def _fox_attention(q, k, v, log_f):
    B, S, H, Dh = q.shape
    nb = S // Q_BLOCK
    F = jnp.cumsum(log_f, axis=1)
    Fk = F.transpose(0, 2, 1)
    q32 = q.astype(jnp.float32) * (Dh ** -0.5)
    k32 = k.astype(jnp.float32)
    v32 = v.astype(jnp.float32)
    qb = q32.reshape(B, nb, Q_BLOCK, H, Dh).transpose(1, 0, 2, 3, 4)
    Fq = F.reshape(B, nb, Q_BLOCK, H).transpose(1, 0, 3, 2)
    kpos = jnp.arange(S)

    def one_block(args):
        i, qi, Fi = args
        s = jnp.einsum('bqhd,bkhd->bhqk', qi, k32)
        s = s + Fi[..., None] - Fk[:, :, None, :]
        qpos = i * Q_BLOCK + jnp.arange(Q_BLOCK)
        s = jnp.where(qpos[:, None] >= kpos[None, :], s, -jnp.inf)
        p = jax.nn.softmax(s, axis=-1)
        return jnp.einsum('bhqk,bkhd->bqhd', p, v32)

    o = lax.map(one_block, (jnp.arange(nb), qb, Fq))
    return o.transpose(1, 0, 2, 3, 4).reshape(B, S, H * Dh)

def _multiscale_pool(u, pool_w, pool_scale):
    B, S, _ = u.shape
    u32 = u.astype(jnp.float32)
    count = jnp.arange(1, S + 1, dtype=jnp.float32)
    outs = []
    for g, w in enumerate(POOL_WINDOWS):
        ug = u32[..., g * POOL_C:(g + 1) * POOL_C]
        csp = jnp.concatenate([jnp.zeros((B, 1, POOL_C), jnp.float32),
                               jnp.cumsum(ug, axis=1)], axis=1)
        lo = jnp.concatenate([jnp.zeros((B, w - 1, POOL_C), jnp.float32),
                              csp[:, :S - w + 1]], axis=1)
        mean = (csp[:, 1:] - lo) / jnp.minimum(count, w)[None, :, None]
        outs.append(jnp.einsum('bsc,cd->bsd', mean - ug, pool_w[g].astype(jnp.float32)))
    out = jnp.concatenate(outs, axis=-1) * pool_scale.astype(jnp.float32)
    return out.astype(u.dtype)

def _conv_ffn(h, w_up, conv_w, conv_b, w_down):
    S = h.shape[1]
    a = h @ w_up
    ap = jnp.pad(a, ((0, 0), (CONV_W - 1, 0), (0, 0)))
    conv = conv_b + ap[:, 0:S] * conv_w[0]
    for j in range(1, CONV_W):
        conv = conv + ap[:, j:j + S] * conv_w[j]
    gate, val = jnp.split(conv, 2, axis=-1)
    return (jax.nn.silu(gate) * val) @ w_down

def first_inputs(seed: int = 0) -> dict:
    key = jax.random.key(seed)
    ks = jax.random.split(key, 18)
    f32 = jnp.float32
    nrm = lambda k, shape, s: jax.random.normal(k, shape, f32) * s
    return {
        "x": nrm(ks[0], (BATCH, SEQ, D_MODEL), 1.0),
        "c": nrm(ks[1], (BATCH, D_MODEL), 1.0),
        "mod_w": nrm(ks[2], (DEPTH, D_MODEL, 6 * D_MODEL), 0.5 * D_MODEL ** -0.5),
        "mod_b": nrm(ks[3], (DEPTH, 6 * D_MODEL), 0.02),
        "norm1_g": 1.0 + nrm(ks[4], (DEPTH, D_MODEL), 0.02),
        "norm2_g": 1.0 + nrm(ks[5], (DEPTH, D_MODEL), 0.02),
        "w_in": nrm(ks[6], (DEPTH, D_MODEL, IN_COLS), D_MODEL ** -0.5),
        "b_f": jax.random.uniform(ks[7], (DEPTH, N_ATTN_HEADS), f32, 1.0, 6.0),
        "pool_w": nrm(ks[8], (DEPTH, len(POOL_WINDOWS), POOL_C, POOL_C), POOL_C ** -0.5),
        "pool_scale": 1.0 + nrm(ks[9], (DEPTH, POOL_W), 0.1),
        "w_out": nrm(ks[10], (DEPTH, ATTN_W + POOL_W, D_MODEL), (ATTN_W + POOL_W) ** -0.5),
        "ffn_up": nrm(ks[11], (DEPTH, D_MODEL, 2 * D_FF), D_MODEL ** -0.5),
        "ffn_conv_w": nrm(ks[12], (DEPTH, CONV_W, 2 * D_FF), CONV_W ** -0.5),
        "ffn_conv_b": nrm(ks[13], (DEPTH, 2 * D_FF), 0.02),
        "ffn_down": nrm(ks[14], (DEPTH, D_FF, D_MODEL), D_FF ** -0.5),
        "final_g": 1.0 + nrm(ks[15], (D_MODEL,), 0.02),
    }

def first_block(x, c, mod_w, mod_b, norm1_g, norm2_g, w_in, b_f, pool_w, pool_scale,
              w_out, ffn_up, ffn_conv_w, ffn_conv_b, ffn_down, final_g):
    B, S, _ = x.shape
    c_act = jax.nn.silu(c)
    splits = [ATTN_W, 2 * ATTN_W, 3 * ATTN_W, 3 * ATTN_W + N_ATTN_HEADS]
    for l in range(DEPTH):
        mod = (c_act @ mod_w[l] + mod_b[l])[:, None, :]
        sh1, sc1, g1, sh2, sc2, g2 = jnp.split(mod, 6, axis=-1)

        h = _rmsnorm(x, norm1_g[l]) * (1.0 + sc1) + sh1
        z = h @ w_in[l]
        q, k, v, f_logit, u = jnp.split(z, splits, axis=-1)
        log_f = jax.nn.log_sigmoid((f_logit + b_f[l]).astype(jnp.float32))
        hd = (B, S, N_ATTN_HEADS, HEAD_DIM)
        attn = _fox_attention(q.reshape(hd), k.reshape(hd), v.reshape(hd), log_f)
        pool = _multiscale_pool(u, pool_w[l], pool_scale[l])
        mixed = jnp.concatenate([attn.astype(x.dtype), pool], axis=-1)
        x = x + g1 * (mixed @ w_out[l])

        h = _rmsnorm(x, norm2_g[l]) * (1.0 + sc2) + sh2
        x = x + g2 * _conv_ffn(h, ffn_up[l], ffn_conv_w[l], ffn_conv_b[l], ffn_down[l])
    return _rmsnorm(x, final_g)


GRID_W = 64
WIN_H_MAX = 8
WIN_W = 16
ATTN_HEADS = 8
ATTN_HEAD_DIM = 64
ATTN_WIDTH = ATTN_HEADS * ATTN_HEAD_DIM
DN_HEADS = 4
DN_HEAD_DIM = 128
DN_WIDTH = DN_HEADS * DN_HEAD_DIM
DN_CONV = 5
DN_CHUNK = 64
D_MIX = ATTN_WIDTH + DN_WIDTH
IN_COLS_2 = 3 * ATTN_WIDTH + 4 * DN_WIDTH + 4 * DN_HEADS
N_GROUPS = 8
EXPERTS_PER_GROUP = 8
N_EXPERTS = N_GROUPS * EXPERTS_PER_GROUP
TOP_K_IN_GROUP = 2
D_EXPERT = D_MODEL // 4
MOE_BLOCK = 256


def rms_norm(x, g):
    xf = x.astype(jnp.float32)
    y = xf * lax.rsqrt(jnp.mean(xf * xf, axis=-1, keepdims=True) + EPS)
    return (y * g.astype(jnp.float32)).astype(x.dtype)

def l2_norm(x):
    xf = x.astype(jnp.float32)
    return xf * lax.rsqrt(jnp.sum(xf * xf, axis=-1, keepdims=True) + EPS)

def neighbourhood_attention(q, k, v, rpb):
    b_, s_, h_, dh = q.shape
    rows = s_ // GRID_W
    kh = min(WIN_H_MAX, rows)
    to_grid = lambda t: t.reshape(b_, rows, GRID_W, h_, dh).transpose(1, 0, 3, 2, 4)
    qg, kg, vg = to_grid(q), to_grid(k), to_grid(v)
    cols = jnp.arange(GRID_W)
    col_start = jnp.clip(cols - WIN_W // 2, 0, GRID_W - WIN_W)
    col_idx = col_start[:, None] + jnp.arange(WIN_W)[None, :]
    col_off = col_idx - cols[:, None] + (WIN_W - 1)
    scale = dh ** -0.5

    def row_block(args):
        r, q_row = args
        r0 = jnp.clip(r - kh // 2, 0, rows - kh)
        k_band = lax.dynamic_slice_in_dim(kg, r0, kh, axis=0)
        v_band = lax.dynamic_slice_in_dim(vg, r0, kh, axis=0)
        k_win = k_band[:, :, :, col_idx]
        v_win = v_band[:, :, :, col_idx]
        row_off = r0 + jnp.arange(kh) - r + (WIN_H_MAX - 1)
        bias = rpb[:, row_off[None, :, None], col_off[:, None, :]]
        logits = jnp.einsum('bhqd,rbhqcd->bhqrc', q_row, k_win).astype(jnp.float32) * scale
        logits = logits + bias.astype(jnp.float32)[None]
        p = jax.nn.softmax(logits.reshape(b_, h_, GRID_W, kh * WIN_W), axis=-1)
        p = p.reshape(b_, h_, GRID_W, kh, WIN_W).astype(v.dtype)
        return jnp.einsum('bhqrc,rbhqce->bqhe', p, v_win)

    out = lax.map(row_block, (jnp.arange(rows), qg))
    return out.transpose(1, 0, 2, 3, 4).reshape(b_, s_, h_ * dh)

def gated_delta_rule(q, k, v, g, beta):
    f32 = jnp.float32
    bn, hn, t_, dk = q.shape
    dv = v.shape[-1]
    c = DN_CHUNK
    nc = t_ // c
    q = q.astype(f32).reshape(bn, hn, nc, c, dk)
    k = k.astype(f32).reshape(bn, hn, nc, c, dk)
    v = v.astype(f32).reshape(bn, hn, nc, c, dv)
    beta = beta.astype(f32).reshape(bn, hn, nc, c)
    gc = jnp.cumsum(g.astype(f32).reshape(bn, hn, nc, c), axis=-1)
    incl = jnp.tril(jnp.ones((c, c), bool))
    strict = jnp.tril(jnp.ones((c, c), bool), -1)
    diff = gc[..., :, None] - gc[..., None, :]
    decay = jnp.where(incl, jnp.exp(jnp.where(incl, diff, 0.0)), 0.0)
    kb = k * beta[..., None]
    lower = jnp.where(strict, jnp.einsum('bhnid,bhnjd->bhnij', kb, k) * decay, 0.0)
    a_mat = jnp.eye(c, dtype=f32) + lower
    rhs = jnp.concatenate([v * beta[..., None], kb * jnp.exp(gc)[..., None]], axis=-1)
    sol = lax.linalg.triangular_solve(a_mat, rhs, left_side=True, lower=True, unit_diagonal=True)
    u, w = sol[..., :dv], sol[..., dv:]
    qk = jnp.einsum('bhnid,bhnjd->bhnij', q, k) * decay

    def step(state, inp):
        q_c, k_c, u_c, w_c, g_c, qk_c = inp
        v_new = u_c - jnp.einsum('bhck,bhkv->bhcv', w_c, state)
        o_c = (jnp.einsum('bhck,bhkv->bhcv', q_c * jnp.exp(g_c)[..., None], state)
               + jnp.einsum('bhij,bhjv->bhiv', qk_c, v_new))
        g_last = g_c[..., -1:]
        state = (state * jnp.exp(g_last)[..., None]
                 + jnp.einsum('bhck,bhcv->bhkv', k_c * jnp.exp(g_last - g_c)[..., None], v_new))
        return state, o_c

    xs = tuple(jnp.moveaxis(t, 2, 0) for t in (q, k, u, w, gc, qk))
    state0 = jnp.zeros((bn, hn, dk, dv), f32)
    _, o = lax.scan(step, state0, xs)
    return jnp.moveaxis(o, 0, 2).reshape(bn, hn, t_, dv)

def bidirectional_gated_deltanet(qkv_raw, z, a, b, conv_w, a_log, dt_bias, out_norm_g):
    b_, s_, _ = qkv_raw.shape
    qkv = lax.conv_general_dilated(qkv_raw, conv_w[:, None, :].astype(qkv_raw.dtype),
                                   window_strides=(1,), padding=[(DN_CONV // 2, DN_CONV // 2)],
                                   dimension_numbers=('NWC', 'WIO', 'NWC'),
                                   feature_group_count=3 * DN_WIDTH)
    qkv = jax.nn.silu(qkv)
    q, k, v = jnp.split(qkv.reshape(b_, s_, 3, DN_HEADS, DN_HEAD_DIM), 3, axis=2)
    q = l2_norm(q[:, :, 0]) * (DN_HEAD_DIM ** -0.5)
    k = l2_norm(k[:, :, 0])
    v = v[:, :, 0].astype(jnp.float32)
    g = -jnp.exp(a_log.astype(jnp.float32)) * jax.nn.softplus(a.astype(jnp.float32) + dt_bias.astype(jnp.float32))
    beta = jax.nn.sigmoid(b.astype(jnp.float32))
    bht = lambda t: t.transpose(0, 2, 1, 3)
    both = lambda t: jnp.concatenate([t, jnp.flip(t, axis=2)], axis=1)
    q2, k2, v2 = both(bht(q)), both(bht(k)), both(bht(v))
    g2 = jnp.concatenate([g[:, :, 0].transpose(0, 2, 1), jnp.flip(g[:, :, 1].transpose(0, 2, 1), axis=-1)], axis=1)
    beta2 = jnp.concatenate([beta[:, :, 0].transpose(0, 2, 1), jnp.flip(beta[:, :, 1].transpose(0, 2, 1), axis=-1)], axis=1)
    o2 = gated_delta_rule(q2, k2, v2, g2, beta2)
    o = o2[:, :DN_HEADS] + jnp.flip(o2[:, DN_HEADS:], axis=2)
    o = o.transpose(0, 2, 1, 3)
    zf = z.reshape(b_, s_, DN_HEADS, DN_HEAD_DIM).astype(jnp.float32)
    o = rms_norm(o, out_norm_g) * jax.nn.silu(zf)
    return o.reshape(b_, s_, DN_WIDTH).astype(qkv_raw.dtype)

def hierarchical_moe(h, wg_r, bg_r, we_r, be_r, w_gate, w_up, w_down):
    b_, s_, d_ = h.shape
    n = b_ * s_
    hf = h.reshape(n, d_)
    group_logits = (hf @ wg_r + bg_r).astype(jnp.float32)
    group_prob = jax.nn.softmax(group_logits, axis=-1)
    gsel = jnp.argmax(group_logits, axis=-1)
    gp = jnp.take_along_axis(group_prob, gsel[:, None], axis=-1)
    exp_logits = (hf @ we_r + be_r).astype(jnp.float32).reshape(n, N_GROUPS, EXPERTS_PER_GROUP)
    in_group = jnp.take_along_axis(exp_logits, gsel[:, None, None], axis=1)[:, 0]
    top_val, top_idx = lax.top_k(in_group, TOP_K_IN_GROUP)
    gates = gp * jax.nn.softmax(top_val, axis=-1)
    eid = (gsel[:, None] * EXPERTS_PER_GROUP + top_idx).reshape(-1).astype(jnp.int32)
    gate_flat = gates.reshape(-1)
    tok_flat = jnp.repeat(jnp.arange(n, dtype=jnp.int32), TOP_K_IN_GROUP)
    nk = n * TOP_K_IN_GROUP
    p_rows = -(-nk // MOE_BLOCK) * MOE_BLOCK + N_EXPERTS * MOE_BLOCK
    nb = p_rows // MOE_BLOCK
    order = jnp.argsort(eid)
    e_sorted = eid[order]
    counts = jnp.bincount(eid, length=N_EXPERTS)
    starts = jnp.cumsum(counts) - counts
    padded = -(-counts // MOE_BLOCK) * MOE_BLOCK
    pends = jnp.cumsum(padded)
    pstarts = pends - padded
    dest = pstarts[e_sorted] + (jnp.arange(nk) - starts[e_sorted])
    buf_tok = jnp.full((p_rows,), n, jnp.int32).at[dest].set(tok_flat[order])
    buf_gate = jnp.zeros((p_rows,), jnp.float32).at[dest].set(gate_flat[order])
    block_expert = jnp.clip(jnp.searchsorted(pends, jnp.arange(nb) * MOE_BLOCK, side='right'),
                            0, N_EXPERTS - 1).astype(jnp.int32)
    h_pad = jnp.concatenate([hf, jnp.zeros((1, d_), hf.dtype)], axis=0)

    def expert_block(args):
        tok, e = args
        xb = h_pad[tok]
        hid = jax.nn.silu(xb @ w_gate[e]) * (xb @ w_up[e])
        return hid @ w_down[e]

    out = lax.map(expert_block, (buf_tok.reshape(nb, MOE_BLOCK), block_expert))
    out = (out.reshape(p_rows, d_).astype(jnp.float32) * buf_gate[:, None]).astype(h.dtype)
    y = jnp.zeros((n + 1, d_), h.dtype).at[buf_tok].add(out)[:n]
    return y.reshape(b_, s_, d_)

def hybrid_layer(x, ln1_g, w_in, q_norm_g, k_norm_g, rpb, attn_out_g, conv_w, a_log, dt_bias,
                 dn_out_g, w_out, ln2_g, wg_r, bg_r, we_r, be_r, w_gate, w_up, w_down):
    b_, s_, _ = x.shape
    h = rms_norm(x, ln1_g)
    proj = h @ w_in
    a3 = 3 * ATTN_WIDTH
    aq, ak, av, dqkv, dz, dab = jnp.split(
        proj, [ATTN_WIDTH, 2 * ATTN_WIDTH, a3, a3 + 3 * DN_WIDTH, a3 + 4 * DN_WIDTH], axis=-1)
    hs = lambda t: t.reshape(b_, s_, ATTN_HEADS, ATTN_HEAD_DIM)
    aq = rms_norm(hs(aq), q_norm_g)
    ak = rms_norm(hs(ak), k_norm_g)
    attn = rms_norm(neighbourhood_attention(aq, ak, hs(av), rpb), attn_out_g)
    dab = dab.reshape(b_, s_, 2, 2, DN_HEADS)
    dn = bidirectional_gated_deltanet(dqkv, dz, dab[:, :, 0], dab[:, :, 1], conv_w, a_log,
                                      dt_bias, dn_out_g)
    x = x + jnp.concatenate([attn, dn], axis=-1) @ w_out
    x = x + hierarchical_moe(rms_norm(x, ln2_g), wg_r, bg_r, we_r, be_r, w_gate, w_up, w_down)
    return x

def second_inputs(seed: int = 0) -> dict:
    key = jax.random.key(seed)
    ks = jax.random.split(key, 24)
    f32 = jnp.float32
    nrm = lambda k, shape, s: jax.random.normal(k, shape, f32) * s
    gain = lambda k, shape: 1.0 + 0.01 * jax.random.normal(k, shape, f32)
    L = DEPTH
    dt = jnp.exp(jax.random.uniform(ks[9], (L, 2, DN_HEADS), f32, np.log(1e-3), np.log(1e-1)))
    return {
        'x': nrm(ks[0], (BATCH, SEQ, D_MODEL), 1.0),
        'ln1_g': gain(ks[1], (L, D_MODEL)),
        'w_in': nrm(ks[2], (L, D_MODEL, IN_COLS_2), D_MODEL ** -0.5),
        'attn_q_norm_g': gain(ks[3], (L, ATTN_HEAD_DIM)),
        'attn_k_norm_g': gain(ks[4], (L, ATTN_HEAD_DIM)),
        'attn_rpb': nrm(ks[5], (L, ATTN_HEADS, 2 * WIN_H_MAX - 1, 2 * WIN_W - 1), 0.1),
        'attn_out_norm_g': gain(ks[6], (L, ATTN_WIDTH)),
        'dn_conv_w': nrm(ks[7], (L, DN_CONV, 3 * DN_WIDTH), DN_CONV ** -0.5),
        'dn_a_log': jnp.log(jax.random.uniform(ks[8], (L, 2, DN_HEADS), f32, 1.0, 16.0)),
        'dn_dt_bias': dt + jnp.log(-jnp.expm1(-dt)),
        'dn_out_norm_g': gain(ks[10], (L, DN_HEAD_DIM)),
        'w_out': nrm(ks[11], (L, D_MIX, D_MODEL), D_MIX ** -0.5),
        'ln2_g': gain(ks[12], (L, D_MODEL)),
        'router_group_w': nrm(ks[13], (L, D_MODEL, N_GROUPS), D_MODEL ** -0.5),
        'router_group_b': nrm(ks[14], (L, N_GROUPS), 0.01),
        'router_expert_w': nrm(ks[15], (L, D_MODEL, N_EXPERTS), D_MODEL ** -0.5),
        'router_expert_b': nrm(ks[16], (L, N_EXPERTS), 0.01),
        'expert_w_gate': nrm(ks[17], (L, N_EXPERTS, D_MODEL, D_EXPERT), D_MODEL ** -0.5),
        'expert_w_up': nrm(ks[18], (L, N_EXPERTS, D_MODEL, D_EXPERT), D_MODEL ** -0.5),
        'expert_w_down': nrm(ks[19], (L, N_EXPERTS, D_EXPERT, D_MODEL), D_EXPERT ** -0.5),
    }

def second_block(x, ln1_g, w_in, attn_q_norm_g, attn_k_norm_g, attn_rpb, attn_out_norm_g, dn_conv_w,
              dn_a_log, dn_dt_bias, dn_out_norm_g, w_out, ln2_g, router_group_w, router_group_b,
              router_expert_w, router_expert_b, expert_w_gate, expert_w_up, expert_w_down):
    for l in range(DEPTH):
        x = hybrid_layer(x, ln1_g[l], w_in[l], attn_q_norm_g[l], attn_k_norm_g[l], attn_rpb[l],
                         attn_out_norm_g[l], dn_conv_w[l], dn_a_log[l], dn_dt_bias[l],
                         dn_out_norm_g[l], w_out[l], ln2_g[l], router_group_w[l], router_group_b[l],
                         router_expert_w[l], router_expert_b[l], expert_w_gate[l], expert_w_up[l],
                         expert_w_down[l])
    return x


def setup_inputs(seed=0):
    out = dict(first_inputs(seed))
    for name, value in second_inputs(seed + 1).items():
        if name != "x":
            out[name + "_2"] = value
    return out


def reference(
    x, c, mod_w, mod_b, norm1_g, norm2_g, w_in, b_f, pool_w, pool_scale, w_out, ffn_up,
    ffn_conv_w, ffn_conv_b, ffn_down, final_g, ln1_g_2, w_in_2, attn_q_norm_g_2,
    attn_k_norm_g_2, attn_rpb_2, attn_out_norm_g_2, dn_conv_w_2, dn_a_log_2, dn_dt_bias_2,
    dn_out_norm_g_2, w_out_2, ln2_g_2, router_group_w_2, router_group_b_2, router_expert_w_2,
    router_expert_b_2, expert_w_gate_2, expert_w_up_2, expert_w_down_2,
):
    x = first_block(
        x, c, mod_w, mod_b, norm1_g, norm2_g, w_in, b_f, pool_w, pool_scale, w_out, ffn_up,
        ffn_conv_w, ffn_conv_b, ffn_down, final_g,
    )
    return second_block(
        x, ln1_g_2, w_in_2, attn_q_norm_g_2, attn_k_norm_g_2, attn_rpb_2, attn_out_norm_g_2,
        dn_conv_w_2, dn_a_log_2, dn_dt_bias_2, dn_out_norm_g_2, w_out_2, ln2_g_2,
        router_group_w_2, router_group_b_2, router_expert_w_2, router_expert_b_2,
        expert_w_gate_2, expert_w_up_2, expert_w_down_2,
    )


_drawn_inputs = setup_inputs


def setup_inputs(seed=0):
    import zlib

    import numpy as np

    out = dict(_drawn_inputs(seed))
    spreads = {}
    factors = {'norm1_g': 4.707,
     'norm2_g': 4.164,
     'ffn_conv_b': 2.978,
     'ln1_g_2': 3.853,
     'attn_q_norm_g_2': 4.893,
     'attn_k_norm_g_2': 5.811,
     'attn_out_norm_g_2': 19.995,
     'dn_out_norm_g_2': 5.848,
     'ln2_g_2': 3.363,
     'router_group_b_2': 5.992,
     'router_expert_b_2': 14.339,
     'attn_rpb_2': 3.208}
    for name, (base, spread) in spreads.items():
        noise = np.random.default_rng([zlib.crc32(name.encode()), seed]).standard_normal(out[name].shape)
        drawn = base * np.exp(spread * noise) if base else spread * noise
        out[name] = __import__('jax').numpy.asarray(drawn.astype(out[name].dtype))
    for name, factor in factors.items():
        out[name] = (out[name] * factor).astype(out[name].dtype)
    return out
```

```python
from contextlib import ExitStack

import numpy as np

import concourse.bass as bass
from concourse import mybir

ALU = mybir.AluOpType
ACT = mybir.ActivationFunctionType
AXIS_X = mybir.AxisListType.X
F32 = mybir.dt.float32
U32 = mybir.dt.uint32

P = 128
D = 1024
DC = D // P
T = 512
TT = T // P
HEADS = 8
DH = 64
QW = HEADS * DH
POOL_WINDOWS = (2, 4, 8, 16)
FF = 2816
FC = FF // P
EPS = 1e-6
GRID = 64
ROWS = T // GRID
WIN_W = 16
WIN_H = 8
DN_HEADS = 4
DN_TAPS = 5
CHUNK = 64
GROUPS = 8
PER_GROUP = 8
EXPERTS = GROUPS * PER_GROUP
DE = 256
CAP = 64
TOP_K = 2
PICKS = TOP_K * T
PICK_TILES = PICKS // P
MORE = T // CAP - 1
OVER = 16
FAR = 1.0e6
NEG = -1.0e30

SLAB = 4096
SLABS = 3
EXPERT = 6144

VEC = {}
_at = 0
for _name, _rows in (("mod_b", 48), ("c", DC), ("norm1_g", DC), ("norm2_g", DC), ("final_g", DC),
                     ("ln1_g", DC), ("ln2_g", DC), ("pool_scale", 4), ("conv_b", 2 * FC),
                     ("conv_w", 3 * 2 * FC), ("dn_conv_w", DN_TAPS * 12), ("q_gain", 1),
                     ("k_gain", 1)):
    VEC[_name] = (_at, _rows)
    _at += _rows
VEC_TILES = -(-_at // P)

ROW = {}
_at = 0
for _name, _cols in (("attn_out_g", QW), ("dn_out_g", P), ("b_f", HEADS), ("router_b", 72),
                     ("dt_bias", 8), ("a_log", 8)):
    ROW[_name] = (_at, _cols)
    _at += _cols
ROW_W = _at


def constants():
    i = np.arange(P)[:, None]
    j = np.arange(P)[None, :]
    same = i // CHUNK == j // CHUNK
    f = np.float32
    out = {
        "ident": (i == j).astype(f),
        "ones": np.ones((P, P), f),
        "ones64": same.astype(f),
        "upto": (i <= j).astype(f),
        "before": (i < j).astype(f),
        "causal": np.where(j <= i, 0, NEG).astype(f),
        "cum0": (same & (i <= j)).astype(f), "cum1": (same & (i >= j)).astype(f),
        "bar0": np.where(same & (j <= i), 0, -NEG).astype(f),
        "bar1": np.where(same & (j >= i), 0, -NEG).astype(f),
        "strict0": (same & (j < i)).astype(f), "strict1": (same & (j > i)).astype(f),
        "in16": (i // 16 == j // 16).astype(f),
        "join32": ((i // 32 == j // 32) & (i // 16 != j // 16)).astype(f),
        "join64": (same & (i // 32 != j // 32)).astype(f),
    }
    out["head_row"] = np.concatenate([np.repeat(i == h, P, 1) for h in range(HEADS)], 1).astype(f)
    t = np.arange(16)
    out["pool_count"] = np.tile(np.concatenate([1 / np.minimum(t + 1, w) for w in POOL_WINDOWS]), (P, 1)).astype(f)
    col, key = np.arange(P)[:, None] % GRID, np.arange(GRID)[None, :]
    first = np.clip(col - WIN_W // 2, 0, GRID - WIN_W)
    out["window"] = np.where((key >= first) & (key < first + WIN_W), 0, NEG).astype(f)[:, ::-1]
    out["rev8"] = np.tile(8 - np.arange(8), (P, 1)).astype(f)
    out["pick"] = (np.arange(PICK_TILES)[None, :] * P + i + 1).astype(f)
    out["slot"] = np.tile(np.arange(P) % CAP, (P, 1)).astype(f)
    out["block"] = np.tile(np.arange(OVER), (P, 1)).astype(f)
    out["expert"] = np.tile(np.arange(EXPERTS) + 1, (P, 1)).astype(f)
    out["caps"] = np.tile((np.arange(MORE) + 1) * CAP, (P, 1)).astype(f)
    out["part"] = (i - P).astype(f)
    out["eps"] = np.full((P, 1), EPS, f)
    return out


CONST = {}
_at = 0
for _name, _table in constants().items():
    CONST[_name] = (_at, _table.shape[1])
    _at += _table.shape[1]
CONST_W = _at


class Queues:

    ENGINES = ("tensor", "vector", "scalar", "gpsimd", "sync")

    def __init__(self, nc, ctx):
        self.queue = {e: [] for e in self.ENGINES}
        self.done = {e: ctx.enter_context(nc.semaphore(f"{e}_done")) for e in self.ENGINES}
        self.count = dict.fromkeys(self.ENGINES, 0)
        self.waited = {e: {} for e in self.ENGINES}

    def wait(self, engine, marks):
        for mark in marks:
            if mark is None:
                continue
            if isinstance(mark, list):
                self.wait(engine, mark)
                continue
            sem, value = mark
            if self.waited[engine].get(sem.name, 0) < value:
                self.waited[engine][sem.name] = value
                self.queue[engine].append(lambda e, sem=sem, value=value: e.wait_ge(sem, value))

    def do(self, engine, after, instruction, signal=True):
        self.wait(engine, after)
        if not signal:
            self.queue[engine].append(instruction)
            return None
        sem = self.done[engine]
        self.count[engine] += 1
        self.queue[engine].append(lambda e: instruction(e).then_inc(sem, 1))
        return (sem, self.count[engine])

    def last(self, engine):
        return (self.done[engine], self.count[engine]) if self.count[engine] else None

    def stage(self):
        marks = [self.last(e) for e in ("tensor", "vector", "scalar", "gpsimd")]
        for e in ("tensor", "vector", "scalar", "gpsimd"):
            self.wait(e, marks)
        return marks

    def play(self, block):
        for name in self.ENGINES:
            def run(engine, name=name):
                for step in self.queue[name]:
                    step(engine)
            {"tensor": block.tensor, "vector": block.vector, "scalar": block.scalar,
             "gpsimd": block.gpsimd, "sync": block.sync}[name](run)


class Buffer:

    def __init__(self, ap):
        self.ap, self.free, self.busy = ap, [], False

    def release(self, *marks):
        self.free, self.busy = list(marks), False


class Rotation:
    def __init__(self, aps):
        self.buffers, self.next = [Buffer(a) for a in aps], 0

    def take(self):
        for _ in self.buffers:
            b = self.buffers[self.next]
            self.next = (self.next + 1) % len(self.buffers)
            if not b.busy:
                b.busy = True
                return b
        raise ValueError("no buffer is free")


class Lane:

    def __init__(self, nc, ctx, q, name):
        self.q, self.sem, self.count = q, ctx.enter_context(nc.semaphore(name)), 0

    def copy(self, engine, after, out, in_):
        self.q.wait(engine, after)
        self.count += 16
        self.q.queue[engine].append(lambda e: e.dma_start(out, in_).then_inc(self.sem, 16))
        return (self.sem, self.count)

    def indirect(self, after, **how):
        self.q.wait("gpsimd", after)
        self.count += 16
        self.q.queue["gpsimd"].append(lambda e: e.indirect_dma_start(**how).then_inc(self.sem, 16))
        return (self.sem, self.count)


class Kernel:
    def __init__(self, nc, ctx, dram):
        self.nc, self.ctx, self.dram = nc, ctx, dram
        self.q = q = Queues(nc, ctx)

        def sbuf(name, cols, dtype=F32):
            return ctx.enter_context(nc.sbuf_tensor(name, [P, cols], dtype))

        self.const = sbuf("constants", CONST_W)
        self.vec = sbuf("channel_vectors", VEC_TILES * P)
        self.row = sbuf("row_vectors", ROW_W)
        self.small = sbuf("small", 1400)
        self.index = sbuf("indices", 64, U32)
        self.xT = sbuf("residual_T", DC * T)
        self.ring = sbuf("weight_ring", SLABS * SLAB)
        self.WORK = 30900
        self.work = sbuf("work", self.WORK)
        self.work_at = self.small_at = 0
        banks = [ctx.enter_context(nc.psum_tensor(f"bank{i}", [P, 512], F32)) for i in range(8)]
        self.banks = Rotation([b[:, :] for b in banks])
        self.slabs = Rotation([self.ring[:, i * SLAB:(i + 1) * SLAB] for i in range(SLABS)])
        self.slab_lanes = [Lane(nc, ctx, q, f"slab{i}_in") for i in range(SLABS)]
        self.lanes = 0
        self.flip = 0

    def lane(self, name):
        return Lane(self.nc, self.ctx, self.q, name)

    def area(self, *shape):
        n = int(np.prod(shape))
        ap = self.work[:, self.work_at:self.work_at + n]
        self.work_at += n
        assert self.work_at <= self.WORK, self.work_at
        return self.shaped(ap, shape)

    @staticmethod
    def shaped(ap, shape):
        if len(shape) == 2:
            return ap.rearrange("p (a b) -> p a b", a=shape[0])
        if len(shape) == 3:
            return ap.rearrange("p (a b c) -> p a b c", a=shape[0], b=shape[1])
        return ap

    def tiny(self, *shape):
        n = int(np.prod(shape))
        ap = self.small[:, self.small_at:self.small_at + n]
        self.small_at += n
        assert self.small_at <= 1400
        return self.shaped(ap, shape)

    def c(self, name, rows=P):
        at, n = CONST[name]
        return self.const[0:rows, at:at + n]

    def v(self, name, i=0, n=1):
        at = VEC[name][0] + i
        return self.vec[:, at:at + n]

    def r(self, name):
        at, n = ROW[name]
        return self.row[:, at:at + n]

    def mm(self, after, out, lhsT, rhs, start, stop, signal=None):
        signal = stop if signal is None else signal
        return self.q.do("tensor", after, lambda e: e.matmul(out, lhsT, rhs, start=start, stop=stop), signal)

    def turn(self, after, out, in_, signal=True):
        ident = self.c("ident")[0:in_.shape[0], 0:in_.shape[0]]
        return self.q.do("tensor", after, lambda e: e.transpose(out, in_, ident), signal)

    def act(self, after, out, in_, func, bias=0.0, scale=1.0, accum=None):
        more = {} if accum is None else {"accum_out": accum}
        if func == ACT.Copy:
            return self.q.do("scalar", after, lambda e: e.activation(out, in_, func, scale=scale, **more))
        return self.q.do("scalar", after,
                         lambda e: e.activation(out, in_, func, bias=bias, scale=scale, **more))

    def tt(self, after, out, a, b, op, engine="vector"):
        return self.q.do(engine, after, lambda e: e.tensor_tensor(out, a, b, op))

    def ts(self, after, out, a, s1, op0, s2=None, op1=None, engine="vector"):
        if op1 is None:
            return self.q.do(engine, after, lambda e: e.tensor_scalar(out, a, s1, None, op0))
        return self.q.do(engine, after, lambda e: e.tensor_scalar(out, a, s1, s2, op0, op1))

    def stt(self, after, out, a, s, b, op0, op1):
        return self.q.do("vector", after, lambda e: e.scalar_tensor_tensor(
            out=out, in0=a, scalar=s, in1=b, op0=op0, op1=op1))

    def reduce(self, after, out, in_, op, negate=False):
        return self.q.do("vector", after, lambda e: e.tensor_reduce(out, in_, AXIS_X, op, negate=negate))

    def copy(self, after, out, in_, engine=None):
        if engine is None:
            self.flip ^= 1
            engine = "vector" if self.flip else "scalar"
        if engine == "scalar":
            return self.act(after, out, in_, ACT.Copy)
        return self.q.do(engine, after, lambda e: e.tensor_copy(out, in_))

    def recip(self, after, out, in_):
        return self.q.do("vector", after, lambda e: e.reciprocal(out, in_))

    def slab(self, *parts):
        i = self.slabs.next
        b = self.slabs.take()
        for at, shape, source in parts:
            n = int(np.prod(shape))
            mark = self.slab_lanes[i].copy("sync", b.free, self.shaped(b.ap[:, at:at + n], shape), source)
        b.landed = mark
        return b

    def columns(self, weight, first, n=512):
        b = self.slab((0, (DC, n), weight.rearrange("(k p) n -> p k n", p=P)[:, :, first:first + n]))
        b.view = self.shaped(b.ap[:, 0:DC * n], (DC, n))
        return b

    def project(self, after, slab_view, landed, src, cols, n=T):
        bank = self.banks.take()
        for k in range(src.shape[1]):
            mark = self.mm([bank.free, after, landed], bank.ap[:, 0:n], slab_view[:, k, cols], src[:, k, :],
                           k == 0, k == src.shape[1] - 1)
        return bank, mark

    def load_small(self):
        lane = self.lane("small_in")
        d = self.dram
        lane.copy("scalar", [], self.const[:, :], d["constants"])
        stage = self.work[:, 0:VEC_TILES * P].rearrange("p (a b) -> p a b", b=P)
        lane.copy("scalar", [], stage, d["channel_vectors"].rearrange("(a p) n -> p a n", p=P))
        self.small_in = lane.copy("scalar", [], self.row[:, :],
                                  d["row_vectors"].to_broadcast([P, ROW_W]))
        bank = self.banks.take()
        for a in range(VEC_TILES):
            m = self.turn([self.small_in], bank.ap[:, a * P:(a + 1) * P], stage[:, a, :])
        self.vec_done = self.copy([m, self.small_in], self.vec[:, :], bank.ap[:, 0:VEC_TILES * P], "vector")
        bank.release(self.vec_done)

    def load_x(self):
        self.work_at = 4096
        lane = self.lane("x_in")
        x = self.area(TT, D)
        landed = lane.copy("scalar", [], x, self.dram["x"].rearrange("(i p) d -> p i d", p=P))
        xT = self.shaped(self.xT[:, :], (DC, T))
        marks = []
        for k in range(DC):
            bank = self.banks.take()
            for i in range(TT):
                m = self.turn([landed, self.small_in, bank.free], bank.ap[:, i * P:(i + 1) * P],
                              x[:, i, k * P:(k + 1) * P], signal=i == TT - 1)
            marks.append(self.copy([m], xT[:, k, :], bank.ap))
            bank.release(marks[-1])
        self.xT3 = xT
        self.x_done = marks

    def modulation_start(self):
        self.c_act = self.tiny(DC)
        self.c_done = self.act([self.vec_done], self.c_act, self.v("c", 0, DC), ACT.Silu)
        self.mod = self.tiny(48)

    def modulation(self, first, last):
        bank = self.banks.take()
        for s in range(first, last):
            w = self.columns(self.dram["mod_w"], s * 512)
            for j in range(4):
                for k in range(DC):
                    m = self.mm([w.landed, self.c_done, bank.free], bank.ap[:, (s * 4 + j):(s * 4 + j) + 1],
                                w.view[:, k, j * P:(j + 1) * P], self.c_act[:, k:k + 1], k == 0, k == DC - 1)
            w.release(m)
        a, b = first * 4, last * 4
        done = self.tt([m, self.vec_done], self.mod[:, a:b], bank.ap[:, a:b], self.v("mod_b", a, b - a), ALU.add)
        bank.release(done)
        return done

    def rms(self, after, out, gain, shift=None):
        squares = Rotation([self.rms_tmp[:, i, :] for i in range(2)])
        bank = self.banks.take()
        for k in range(DC):
            s = squares.take()
            sq = self.act([after, s.free], s.ap, self.xT3[:, k, :], ACT.Square)
            m = self.mm([sq, bank.free], bank.ap, self.c("ones"), s.ap, k == 0, k == DC - 1, signal=True)
            s.release(m)
        root = self.act([m, self.small_in], self.rms_tmp[:, 2, :], bank.ap, ACT.Sqrt, bias=self.c("eps"), scale=1.0 / D)
        bank.release(root)
        inv = self.recip([root], self.rms_tmp[:, 3, :], self.rms_tmp[:, 2, :])
        marks = []
        for k in range(DC):
            m = self.stt([inv, after], out[:, k, :], self.xT3[:, k, :], gain[:, k:k + 1], self.rms_tmp[:, 3, :],
                         ALU.mult, ALU.mult)
            if shift is not None:
                m = self.act([m], out[:, k, :], out[:, k, :], ACT.Identity, bias=shift[:, k:k + 1])
            marks.append(m)
        return marks

    def gain_of(self, after, scale_at, norm):
        g = self.tiny(DC)
        return g, self.stt([after], g, self.mod[:, scale_at:scale_at + DC], 1.0, self.v(norm, 0, DC), ALU.add, ALU.mult)

    def attend(self, qT, kT, v, width, logits, out_row, ready, outs):
        n_buf = 3
        probs = Rotation([self.area(T) for _ in range(n_buf)])
        turned = Rotation([self.area(T) for _ in range(n_buf)])
        neg_max = self.tiny(TT, HEADS)
        total = self.tiny(TT, HEADS)
        inverse = self.tiny(TT, HEADS)
        state = {}

        def scores(i, h):
            w = width(i)
            rows = slice(64 * (h % 2), 64 * (h % 2) + 64)
            bank = self.banks.take()
            m = self.mm([bank.free, ready], bank.ap[:, 0:w], qT[rows, h // 2, i * P:(i + 1) * P],
                        kT[rows, h // 2, 0:w], True, True)
            p = probs.take()
            m = logits(i, h, bank, m, p)
            m = self.reduce([m], neg_max[:, i, h:h + 1], p.ap[:, 0:w], ALU.max, negate=True)
            m = self.act([m], p.ap[:, 0:w], p.ap[:, 0:w], ACT.Exp, bias=neg_max[:, i, h:h + 1],
                         accum=total[:, i, h:h + 1])
            state[i, h] = [p, m]

        def transposed(i, h):
            w = width(i)
            p, m = state[i, h]
            bank = self.banks.take()
            t = turned.take()
            for j in range(w // P):
                mark = self.turn([m, bank.free], bank.ap[:, j * P:(j + 1) * P], p.ap[:, j * P:(j + 1) * P],
                                 signal=j == w // P - 1)
            p.release(mark)
            mark = self.copy([mark, t.free], t.ap[:, 0:w], bank.ap[:, 0:w])
            bank.release(mark)
            state[i, h] = [t, mark, m]

        def values(i, h):
            t, mark, exp = state.pop((i, h))
            if h == 0:
                state["o"] = self.banks.take()
            o = state["o"]
            for j in range(width(i) // P):
                m = self.mm([mark, ready, o.free], o.ap[:, h * DH:(h + 1) * DH], t.ap[:, j * P:(j + 1) * P],
                            v[:, j, h * DH:(h + 1) * DH], j == 0, j == width(i) // P - 1)
            t.release(m)
            if h == HEADS - 1:
                inv = self.recip([exp], inverse[:, i, :], total[:, i, :])
                b = outs.take()
                o3 = o.ap.rearrange("p (h d) -> p h d", h=HEADS)
                m = self.tt([m, inv, b.free], b.ap.rearrange("p (h d) -> p h d", h=HEADS), o3,
                            inverse[:, i, :].unsqueeze(2).to_broadcast([P, HEADS, DH]), ALU.mult)
                o.release(m)
                out_row(i, b, m)

        units = [(i, h) for i in range(TT) for h in range(HEADS)]
        for n in range(len(units) + 2):
            if n < len(units):
                scores(*units[n])
            if 1 <= n <= len(units):
                transposed(*units[n - 1])
            if n >= 2:
                values(*units[n - 2])

    def turn_row(self, b, mark, mixed, first, i):
        bank = self.banks.take()
        for j in range(4):
            m = self.turn([mark, bank.free], bank.ap[:, j * P:(j + 1) * P], b.ap[:, j * P:(j + 1) * P], signal=j == 3)
        b.release(m)
        out = mixed[:, first:first + 4, i * P:(i + 1) * P]
        m = self.copy([m], out, bank.ap.rearrange("p (a b) -> p a b", a=4))
        bank.release(m)
        self.mixed_marks.append(m)

    def block1_mixer(self):
        d, q = self.dram, self.q
        self.load_small()
        self.modulation_start()
        self.load_x()
        self.work_at = 0
        wf_lane = self.lane("wf_in")
        mod_a = self.modulation(0, 4)
        gain, gain_done = self.gain_of(mod_a, DC, "norm1_g")
        stage = q.stage()
        hT = self.area(DC, T)
        self.rms_tmp = self.area(4, T)
        h = self.rms(self.x_done + [gain_done], hT, gain, self.mod[:, 0:DC])

        qT, kT, v, mixed = self.area(4, T), self.area(4, T), self.area(TT, QW), self.area(DC, T)
        w_in = d["w_in"]
        ready = []
        for first, out, scale in ((0, qT, DH ** -0.5), (QW, kT, 1.0)):
            w = self.columns(w_in, first)
            for j in range(4):
                bank, m = self.project(h, w.view, w.landed, hT, slice(j * P, (j + 1) * P))
                done = self.act([m], out[:, j, :], bank.ap, ACT.Copy, scale=scale)
                bank.release(done)
                ready.append(done)
            w.release(m)
        w = self.columns(w_in, 2 * QW)
        for i in range(TT):
            bank = self.banks.take()
            for k in range(DC):
                m = self.mm([bank.free, w.landed, h], bank.ap, hT[:, k, i * P:(i + 1) * P], w.view[:, k, :],
                            k == 0, k == DC - 1)
            done = self.copy([m], v[:, i, :], bank.ap)
            bank.release(done)
            ready.append(done)
        w.release(m)

        wf = self.tiny(DC, HEADS)
        wf_in = wf_lane.copy("scalar", [], wf, w_in.rearrange("(k p) n -> p k n", p=P)[:, :, 3 * QW:3 * QW + HEADS])
        bank = self.banks.take()
        for i in range(TT):
            for k in range(DC):
                m = self.mm([bank.free, wf_in, h], bank.ap[:, i * 8:i * 8 + 8], hT[:, k, i * P:(i + 1) * P],
                            wf[:, k, :], k == 0, k == DC - 1)
        y, a, log_f, F = self.tiny(TT, 8), self.tiny(TT, 8), self.tiny(TT, 8), self.tiny(TT, 8)
        m = self.tt([m], y, bank.ap[:, 0:32].rearrange("p (i h) -> p i h", i=TT),
                    self.r("b_f").unsqueeze(1).to_broadcast([P, TT, 8]), ALU.add)
        bank.release(m)
        e = self.softplus_part([m], a, y)
        m = self.stt([e], log_f, y, 0.0, a, ALU.min, ALU.subtract)
        bank = self.banks.take()
        for i in range(TT):
            for j in range(i + 1):
                c = self.c("upto") if j == i else self.c("ones")
                self.mm([bank.free, m], bank.ap[:, i * 8:i * 8 + 8], c, log_f[:, j, :], j == 0, j == i)
        F_done = self.copy([q.last("tensor")], F, bank.ap[:, 0:32].rearrange("p (i h) -> p i h", i=TT), "vector")
        bank.release(F_done)
        bank = self.banks.take()
        for i in range(TT):
            for j in range(i + 1):
                c = self.c("upto") if j == i else self.c("ones")
                self.mm([bank.free, m], bank.ap[0:8, i * P:(i + 1) * P], log_f[:, j, :], c, j == 0, j == i)
        minus_F = self.area(T)
        rows_done = self.act([q.last("tensor")], minus_F[0:8, :], bank.ap[0:8, :], ACT.Copy, scale=-1.0)
        bank.release(rows_done)
        F_rows = self.area(HEADS, T)
        for hd in range(HEADS):
            bank = self.banks.take()
            m = self.mm([bank.free, rows_done], bank.ap, self.c("head_row", 8)[:, hd * P:(hd + 1) * P],
                        minus_F[0:8, :], True, True)
            done = self.copy([m], F_rows[:, hd, :], bank.ap)
            bank.release(done)
            ready.append(done)
        ready.append(F_done)

        self.mixed_marks = []
        w = self.columns(w_in, 3 * QW + HEADS)
        pool_lane = self.lane("pool_w_in")
        pool_w = self.shaped(self.rms_tmp.rearrange("p a b -> p (a b)")[:, 0:4 * P], (4, P))
        pool_in = pool_lane.copy("scalar", [h], pool_w, d["pool_w"].rearrange("g c d -> c g d"))
        u_bufs = [self.area(T) for _ in range(3)]
        u_free = []
        counts = self.c("pool_count").rearrange("p (g n) -> p g n", g=4)
        for g, window in enumerate(POOL_WINDOWS):
            bank, m = self.project(h, w.view, w.landed, hT, slice(g * P, (g + 1) * P))
            u, s, s2 = u_bufs
            m = self.copy([m, u_free], u, bank.ap, "scalar")
            bank.release(m)
            u_done = m
            src, reach = u, 1
            while reach < window:
                dst = s2 if src is s else s
                m1 = self.tt([m], dst[:, reach:], src[:, reach:], src[:, :T - reach], ALU.add)
                m2 = self.copy([m], dst[:, 0:reach], src[:, 0:reach], "vector")
                m, src, reach = [m1, m2], dst, 2 * reach
            other = s2 if src is s else s
            m = [self.stt([m, u_done], other, src, 1.0 / window, u, ALU.mult, ALU.subtract)]
            m = self.tt([m], other[:, 0:16], src[:, 0:16], counts[:, g, :], ALU.mult)
            m = self.tt([m], other[:, 0:16], other[:, 0:16], u[:, 0:16], ALU.subtract)
            bank = self.banks.take()
            mp = self.mm([m, pool_in, bank.free], bank.ap, pool_w[:, g, :], other, True, True)
            m = self.act([mp], mixed[:, 4 + g, :], bank.ap, ACT.Copy, scale=self.v("pool_scale", g))
            bank.release(m)
            self.mixed_marks.append(m)
            u_free = [mp]
        w.release(q.last("tensor"))

        def logits(i, hd, bank, m, p):
            n = (i + 1) * P
            m = self.stt([m, ready, p.free], p.ap[:, 0:n], bank.ap[:, 0:n], F[:, i, hd:hd + 1],
                         F_rows[:, hd, 0:n], ALU.add, ALU.add)
            bank.release(m)
            return self.tt([m], p.ap[:, i * P:n], p.ap[:, i * P:n], self.c("causal"), ALU.add)

        self.attend(qT, kT, v, lambda i: (i + 1) * P, logits,
                    lambda i, b, m: self.turn_row(b, m, mixed, 0, i), ready,
                    Rotation([self.area(QW) for _ in range(2)]))

        self.mod_b_done = self.modulation(4, 12)
        self.residual_add(d["w_out"], mixed, self.mod[:, 2 * DC:3 * DC])

    def softplus_part(self, after, out, y):
        m = self.act(after, out, y, ACT.Abs)
        m = self.act([m], out, out, ACT.Exp, scale=-1.0)
        return self.act([m], out, out, ACT.Ln, bias=self.c("ones")[:, 0:1])

    def residual_add(self, weight, mixed, gate=None):
        self.x_done = []
        for s in range(2):
            w = self.columns(weight, s * 512)
            for j in range(4):
                k = s * 4 + j
                bank, m = self.project(self.mixed_marks, w.view, w.landed, mixed, slice(j * P, (j + 1) * P))
                x = self.xT3[:, k, :]
                if gate is None:
                    m = self.tt([m], x, bank.ap, x, ALU.add)
                else:
                    m = self.stt([m, self.mod_b_done], x, bank.ap, gate[:, k:k + 1], x, ALU.mult, ALU.add)
                bank.release(m)
                self.x_done.append(m)
            w.release(self.q.last("tensor"))

    def block1_mlp(self):
        d, q = self.dram, self.q
        q.stage()
        self.work_at = 0
        hT = self.area(DC, T)
        self.rms_tmp = self.area(4, T)
        gain, gain_done = self.gain_of(self.mod_b_done, 4 * DC, "norm2_g")
        h = self.rms(self.x_done + [gain_done], hT, gain, self.mod[:, 3 * DC:4 * DC])
        hidden = self.area(FC, T)
        convs = Rotation([self.area(T) for _ in range(4)])
        up = d["ffn_up"].rearrange("(k p) n -> p k n", p=P)
        hidden_marks = []
        for s in range(FC // 2):
            n = 2 * P
            w = self.slab((0, (DC, n), up[:, :, s * n:(s + 1) * n]),
                          (DC * n, (DC, n), up[:, :, FF + s * n:FF + (s + 1) * n]))
            views = [self.shaped(w.ap[:, i * DC * n:(i + 1) * DC * n], (DC, n)) for i in range(2)]
            for j in range(2):
                pair = []
                for side in range(2):
                    ch = side * FC + 2 * s + j
                    bank, m = self.project(h, views[side], w.landed, hT, slice(j * P, (j + 1) * P))
                    c = convs.take()
                    tap = [self.v("conv_w", t * 2 * FC + ch) for t in range(3)]
                    m = self.act([m, c.free], c.ap, bank.ap, ACT.Identity, bias=self.v("conv_b", ch), scale=tap[2])
                    m = self.stt([m], c.ap[:, 1:], bank.ap[:, 0:T - 1], tap[1], c.ap[:, 1:], ALU.mult, ALU.add)
                    m = self.stt([m], c.ap[:, 2:], bank.ap[:, 0:T - 2], tap[0], c.ap[:, 2:], ALU.mult, ALU.add)
                    bank.release(m)
                    pair.append((c, m))
                (cg, mg), (cv, mv) = pair
                mg = self.act([mg], cg.ap, cg.ap, ACT.Silu)
                m = self.tt([mg, mv], hidden[:, 2 * s + j, :], cg.ap, cv.ap, ALU.mult, "gpsimd")
                cg.release(m)
                cv.release(m)
                hidden_marks.append(m)
            w.release(q.last("tensor"))
        down = d["ffn_down"].rearrange("(k p) n -> p k n", p=P)
        self.x_done = []
        for k in range(DC):
            w = self.slab((0, (FC, P), down[:, :, k * P:(k + 1) * P]))
            view = self.shaped(w.ap[:, 0:FC * P], (FC, P))
            bank, m = self.project(hidden_marks, view, w.landed, hidden, slice(0, P))
            w.release(m)
            x = self.xT3[:, k, :]
            m = self.stt([m], x, bank.ap, self.mod[:, 5 * DC + k:5 * DC + k + 1], x, ALU.mult, ALU.add)
            bank.release(m)
            self.x_done.append(m)
        self.x_done = self.rms(self.x_done, self.xT3, self.v("final_g", 0, DC))

    def head_norm(self, after, out, src, ones, n, gain, scale=None, eps_inside=True):
        t = self.norm_tmp.take()
        m = self.act([after, t.free], t.ap[:, 0, :], src, ACT.Square)
        bank = self.banks.take()
        m = self.mm([m, bank.free], bank.ap, ones, t.ap[:, 0, :], True, True)
        m = self.act([m], t.ap[:, 1, :], bank.ap, ACT.Sqrt, bias=self.c("eps"), scale=1.0 / n)
        bank.release(m)
        m = self.recip([m], t.ap[:, 1, :], t.ap[:, 1, :])
        m = self.stt([m], out, src, gain, t.ap[:, 1, :], ALU.mult, ALU.mult)
        t.release(m)
        return m

    def block2_attention(self):
        d, q = self.dram, self.q
        entry = q.stage()
        self.work_at = 0
        self.hT2 = hT = self.area(DC, T)
        self.mixed2 = mixed = self.area(DC, T)
        self.rms_tmp = self.area(4, T)
        h = self.h2 = self.rms(self.x_done, hT, self.v("ln1_g", 0, DC))
        qT, kT, v = self.area(4, T), self.area(4, T), self.area(TT, QW)
        self.norm_tmp = Rotation([self.area(2, T) for _ in range(2)])
        raws = Rotation([self.area(T) for _ in range(2)])
        w_in = d["w_in_2"]
        ready = []
        q_gain = self.tiny(1)
        gain_done = self.ts([self.vec_done], q_gain, self.v("q_gain"), DH ** -0.5, ALU.mult)
        for first, out, gain in ((0, qT, q_gain), (QW, kT, self.v("k_gain"))):
            w = self.columns(w_in, first)
            for j in range(4):
                bank, m = self.project(h, w.view, w.landed, hT, slice(j * P, (j + 1) * P))
                raw = raws.take()
                c = self.copy([m, raw.free], raw.ap, bank.ap)
                bank.release(c)
                done = self.head_norm([c, gain_done], out[:, j, :], raw.ap, self.c("ones64"), DH, gain)
                raw.release(done)
                ready.append(done)
            w.release(m)
        w = self.columns(w_in, 2 * QW)
        for i in range(TT):
            bank = self.banks.take()
            for k in range(DC):
                m = self.mm([bank.free, w.landed, h], bank.ap, hT[:, k, i * P:(i + 1) * P], w.view[:, k, :],
                            k == 0, k == DC - 1)
            done = self.copy([m], v[:, i, :], bank.ap)
            bank.release(done)
            ready.append(done)
        w.release(m)

        n_m = 2 * WIN_H - 2
        lane = self.lane("rpb_in")
        table = [self.area(n_m, GRID) for _ in range(HEADS)]
        table_done = []
        rpb = d["rpb"]
        for hd in range(HEADS):
            for r2 in range(2):
                in_ = rpb[hd, 1 - r2:1 - r2 + n_m, :]
                source = bass.AP(in_.tensor, in_.offset, [[1, GRID], [2 * GRID - 1, n_m], [1, GRID]])
                landed = lane.copy("gpsimd", entry, table[hd][r2 * GRID:(r2 + 1) * GRID, :, :],
                                   source)
        for hd in range(HEADS):
            table_done.append(self.tt([landed], table[hd], table[hd],
                                      self.c("window").unsqueeze(1).to_broadcast([P, n_m, GRID]), ALU.add, "gpsimd"))

        def logits(i, hd, bank, m, p):
            at = table[hd][:, 6 - 2 * i:6 - 2 * i + ROWS, :]
            forwards = bass.AP(at.tensor, at.offset + GRID - 1, [list(at.ap[0]), [GRID, ROWS], [-1, GRID]])
            by_row = lambda ap: ap.rearrange("p (r c) -> p r c", r=ROWS)
            m = self.tt([m, table_done[hd], p.free], by_row(p.ap), by_row(bank.ap), forwards, ALU.add)
            bank.release(m)
            return m

        square, stats = self.rms_tmp[:, 0, :], self.tiny(TT, 3)
        self.mixed_marks = []
        last = []

        def out_row(i, b, m):
            m = self.act([m] + last, square, b.ap, ACT.Square, accum=stats[:, i, 0:1])
            last[:] = [m]
            m = self.act([m], stats[:, i, 1:2], stats[:, i, 0:1], ACT.Sqrt, bias=self.c("eps"), scale=1.0 / QW)
            m = self.recip([m], stats[:, i, 2:3], stats[:, i, 1:2])
            m = self.stt([m], b.ap, b.ap, stats[:, i, 2:3], self.r("attn_out_g"), ALU.mult, ALU.mult)
            self.turn_row(b, m, mixed, 0, i)

        self.attend(qT, kT, v, lambda i: T, logits, out_row, ready, raws)

    def deltanet(self):
        d, q = self.dram, self.q
        q.stage()
        hT, mixed, h = self.hT2, self.mixed2, self.h2
        self.work_at = 2 * DC * T
        qkvT = self.area(12, T)
        z = self.area(TT, QW)
        self.norm_tmp = Rotation([self.area(2, T) for _ in range(2)])
        convs = Rotation([self.area(T) for _ in range(3)])
        w_in = d["w_in_2"]
        base = 3 * QW
        done = []
        for s in range(3):
            w = self.columns(w_in, base + s * 512)
            for j in range(4):
                ch = s * 4 + j
                bank, m = self.project(h, w.view, w.landed, hT, slice(j * P, (j + 1) * P))
                c = convs.take()
                tap = [self.v("dn_conv_w", t * 12 + ch) for t in range(DN_TAPS)]
                m = self.act([m, c.free], c.ap, bank.ap, ACT.Copy, scale=tap[2])
                for t in (0, 1, 3, 4):
                    s_ = t - DN_TAPS // 2
                    to = slice(max(0, -s_), T - max(0, s_))
                    of = slice(max(0, s_), T - max(0, -s_))
                    m = self.stt([m], c.ap[:, to], bank.ap[:, of], tap[t], c.ap[:, to], ALU.mult, ALU.add)
                bank.release(m)
                m = self.act([m], qkvT[:, ch, :], c.ap, ACT.Silu)
                c.release(m)
                done.append(m)
            w.release(q.last("tensor"))
        for ch in range(8):
            done[ch] = self.head_norm(done[ch], qkvT[:, ch, :], qkvT[:, ch, :], self.c("ones"), 1.0,
                                      float(P) ** -0.5 if ch < 4 else 1.0)
        w = self.columns(w_in, base + 3 * 512)
        z_done = []
        for i in range(TT):
            bank = self.banks.take()
            for k in range(DC):
                m = self.mm([bank.free, w.landed, h], bank.ap, hT[:, k, i * P:(i + 1) * P], w.view[:, k, :],
                            k == 0, k == DC - 1)
            z_done.append(self.act([m], z[:, i, :], bank.ap, ACT.Silu))
            bank.release(z_done[-1])
        w.release(m)
        lane = self.lane("gates_in")
        wg = self.tiny(DC, 16)
        gates_in = lane.copy("scalar", [], wg, w_in.rearrange("(k p) n -> p k n", p=P)[:, :, base + 4 * 512:base + 4 * 512 + 16])
        bank = self.banks.take()
        for i in range(TT):
            for k in range(DC):
                m = self.mm([bank.free, gates_in, h], bank.ap[:, i * 16:i * 16 + 16], hT[:, k, i * P:(i + 1) * P],
                            wg[:, k, :], k == 0, k == DC - 1)
        ab = bank.ap[:, 0:64].rearrange("p (i n) -> p i n", i=TT)
        y, a, g, beta = (self.tiny(TT, 8) for _ in range(4))
        rate = self.tiny(8)
        m1 = self.tt([m], y, ab[:, :, 0:8], self.r("dt_bias").unsqueeze(1).to_broadcast([P, TT, 8]), ALU.add)
        m2 = self.act([m1], beta, ab[:, :, 8:16], ACT.Exp, scale=-1.0)
        bank.release(m1, m2)
        m2 = self.ts([m2], beta, beta, 1.0, ALU.add)
        beta_done = self.recip([m2], beta, beta)
        m = self.softplus_part([m1], a, y)
        m = self.stt([m], a, y, 0.0, a, ALU.max, ALU.add)
        r = self.act([], rate, self.r("a_log"), ACT.Exp)
        m = self.stt([m, r], g, a, -1.0, rate.unsqueeze(1).to_broadcast([P, TT, 8]), ALU.mult, ALU.mult)
        g_done = m
        cum, whole = self.tiny(2, TT, 4), self.tiny(2, TT, 4)
        bank = self.banks.take()
        for dr in range(2):
            gd = g[:, :, dr * 4:dr * 4 + 4]
            self.mm([bank.free, g_done], bank.ap[:, dr * 16:dr * 16 + 16], self.c(f"cum{dr}"), gd, True, True)
            m = self.mm([], bank.ap[:, 32 + dr * 16:48 + dr * 16], self.c("ones64"), gd, True, True)
        m1 = self.copy([m], cum.rearrange("p a b c -> p (a b c)"), bank.ap[:, 0:32], "vector")
        m2 = self.copy([m], whole.rearrange("p a b c -> p (a b c)"), bank.ap[:, 32:64], "vector")
        bank.release(m2)
        k_scale, w_scale = self.tiny(2, TT, 4), self.tiny(2, TT, 4)
        m = self.tt([m1, m2], k_scale, whole, cum, ALU.subtract)
        k_scale_done = self.act([m], k_scale, k_scale, ACT.Exp)
        m = self.act([m1], w_scale, cum, ACT.Exp)
        for dr in range(2):
            m = self.tt([m, beta_done], w_scale[:, dr], w_scale[:, dr], beta[:, :, dr * 4:dr * 4 + 4], ALU.mult)
        scales = [k_scale_done, m, beta_done, m1]

        free_h = [q.last("tensor")]
        k_tok = hT[:, 0:4, :]
        v_tok = hT[:, 4:8, :]
        tok_done = {}
        for i in range(TT):
            for dst, off in ((k_tok, 4), (v_tok, 8)):
                bank = self.banks.take()
                for hd in range(4):
                    m = self.turn([bank.free, done[off + hd]], bank.ap[:, hd * P:(hd + 1) * P],
                                  qkvT[:, off + hd, i * P:(i + 1) * P], signal=hd == 3)
                m = self.copy([m, free_h], dst[:, i, :], bank.ap)
                bank.release(m)
                tok_done[off, i] = m

        turned = [q.last("tensor"), q.last("scalar"), q.last("vector")]
        self.work_at = 2 * DC * T + 12 * T + TT * QW
        o_acc = self.area(TT, QW)
        states = [self.area(4, P) for _ in range(2)]
        bufs = []
        while self.work_at + 512 <= self.WORK:
            bufs.append(self.area(512))
        bufs += [qkvT[:, 8 + i, :] for i in range(4)] + [mixed[:, 4 + i, :] for i in range(3)]
        pool = Rotation(bufs)
        for b in pool.buffers:
            b.free = turned
        state_done = [[self.q.do("gpsimd", [turned], lambda e, s=s: e.memset(s, 0.0))] for s in states]
        o_done = {}
        heads = lambda ap: ap.rearrange("p (h d) -> p h d", h=4)
        spread = lambda col: col.unsqueeze(2).to_broadcast([P, 4, P])
        over_heads = lambda c: c.unsqueeze(1).to_broadcast([P, 4, P])

        def per_head(after, pairs, out=None, bank=None, rows=slice(0, P)):
            bank = self.banks.take()
            for hd in range(4):
                lhsT, rhs = pairs(hd)
                m = self.mm([after, bank.free], bank.ap[:, hd * P:(hd + 1) * P], lhsT, rhs, True, True)
            return bank, m

        def unit(dr, i):
            tile = slice(i * P, (i + 1) * P)
            col = lambda t: t[:, dr, i, :]
            by_head = lambda b: (lambda hd: b.ap[:, hd * P:(hd + 1) * P])
            tt, ts, stt, act = self.tt, self.ts, self.stt, self.act
            g_col = g[:, i, dr * 4:dr * 4 + 4]
            b_col = beta[:, i, dr * 4:dr * 4 + 4]
            bg = pool.take()
            m = tt([g_done, bg.free], heads(bg.ap), over_heads(self.c(f"cum{dr}")), spread(g_col), ALU.mult)
            bank = self.banks.take()
            m = self.mm([m, bank.free], bank.ap, self.c("ones"), bg.ap, True, True)
            bg.release(m)
            yield
            eg, decay = pool.take(), pool.take()
            eg_done = act([m, eg.free], eg.ap, bank.ap, ACT.Exp)
            m = tt([eg_done, decay.free], heads(decay.ap), heads(bank.ap), over_heads(self.c(f"bar{dr}")), ALU.add)
            bank.release(m, eg_done)
            for hd in range(4):
                s = slice(hd * P, (hd + 1) * P)
                m = act([m, scales], decay.ap[:, s], decay.ap[:, s], ACT.Exp, bias=cum[:, dr, i, hd:hd + 1], scale=-1.0)
            decay_done = m
            yield
            kT = lambda hd: qkvT[:, 4 + hd, tile]
            qT = lambda hd: qkvT[:, hd, tile]
            kk, m_kk = per_head(done, lambda hd: (kT(hd), kT(hd)))
            qk, m_qk = per_head(done, lambda hd: (qT(hd), kT(hd)))
            L, QK = pool.take(), pool.take()
            yield
            m = tt([decay_done, m_qk, QK.free], QK.ap, qk.ap, decay.ap, ALU.mult)
            qk.release(m)
            qk_done = m
            for hd in range(4):
                s = slice(hd * P, (hd + 1) * P)
                m = stt([qk_done, scales], decay.ap[:, s], decay.ap[:, s], b_col[:, hd:hd + 1], self.c(f"strict{dr}"),
                        ALU.mult, ALU.mult)
            L_done = tt([m, m_kk, L.free], L.ap, kk.ap, decay.ap, ALU.mult)
            kk.release(L_done)
            decay.release(L_done)
            yield
            LT, QKT = pool.take(), pool.take()
            out = []
            for src, dst, ready in ((L, LT, L_done), (QK, QKT, qk_done)):
                bank = self.banks.take()
                for hd in range(4):
                    m = self.turn([ready, bank.free], bank.ap[:, hd * P:(hd + 1) * P], src.ap[:, hd * P:(hd + 1) * P],
                                  signal=hd == 3)
                if src is QK:
                    QK.release(m)
                m = self.copy([m, dst.free], dst.ap, bank.ap, "scalar")
                bank.release(m)
                out.append(m)
            LT_done, QKT_done = out
            qe, kd, vb, kb = (pool.take() for _ in range(4))
            qe_done = tt([eg_done, qe.free, done], heads(qe.ap), qkvT[:, 0:4, tile], heads(eg.ap), ALU.mult, "gpsimd")
            kd_done = tt([scales, kd.free, tok_done[4, i]], heads(kd.ap), heads(k_tok[:, i, :]), spread(col(k_scale)), ALU.mult, "gpsimd")
            vb_done = tt([scales, vb.free, tok_done[8, i]], heads(vb.ap), heads(v_tok[:, i, :]), spread(b_col), ALU.mult, "gpsimd")
            kb_done = tt([scales, kb.free, tok_done[4, i]], heads(kb.ap), heads(k_tok[:, i, :]), spread(col(w_scale)), ALU.mult, "gpsimd")
            yield
            N, NT, X, XT = (pool.take() for _ in range(4))
            in16, eye = over_heads(self.c("in16")), over_heads(self.c("ident"))
            mN = tt([L_done, N.free], heads(N.ap), heads(L.ap), in16, ALU.mult)
            mNT = tt([LT_done, NT.free], heads(NT.ap), heads(LT.ap), in16, ALU.mult)
            mX = tt([mN, X.free], heads(X.ap), eye, heads(N.ap), ALU.subtract)
            mXT = tt([mNT, XT.free], heads(XT.ap), eye, heads(NT.ap), ALU.subtract)
            power, powerT, mp, mpT = N, NT, mN, mNT
            for level in range(3):
                yield
                b1, m1 = per_head([mp, mpT], lambda hd: (by_head(powerT)(hd), by_head(power)(hd)))
                nxt = pool.take()
                n1 = self.copy([m1, nxt.free], nxt.ap, b1.ap, "vector")
                b1.release(n1)
                if level < 2:
                    b2, m2 = per_head([], lambda hd: (by_head(power)(hd), by_head(powerT)(hd)))
                    nxtT = pool.take()
                    n2 = self.copy([m2, nxtT.free], nxtT.ap, b2.ap, "scalar")
                    b2.release(n2)
                else:
                    nxtT, n2, m2 = None, None, m1
                power.release(m1, m2, mX, mXT)
                powerT.release(m1, m2, mX, mXT)
                power, powerT, mp, mpT = nxt, nxtT, n1, n2
                yield
                bX, m1 = per_head([mp, mX, mXT], lambda hd: (by_head(XT)(hd), by_head(power)(hd)))
                bT, m2 = per_head([], lambda hd: (by_head(power)(hd), by_head(XT)(hd)))
                mX = tt([m2], X.ap, bX.ap, X.ap, ALU.add)
                mXT = tt([m2], XT.ap, bT.ap, XT.ap, ALU.add)
                bX.release(mX)
                bT.release(mXT)
                last_use = m2
            power.release(last_use)
            for level, join in enumerate(("join32", "join64")):
                yield
                J = pool.take()
                mJ = tt([LT_done, J.free], heads(J.ap), heads(LT.ap), over_heads(self.c(join)), ALU.mult, "gpsimd")
                b1, m1 = per_head([mJ, mX], lambda hd: (by_head(J)(hd), by_head(X)(hd)))
                J.release(m1)
                W = pool.take()
                mW = self.copy([m1, W.free], W.ap, b1.ap, "scalar")
                b1.release(mW)
                yield
                if level == 0:
                    bX, m1 = per_head([mW, mXT, mX], lambda hd: (by_head(XT)(hd), by_head(W)(hd)))
                bT, m2 = per_head([mW, mXT, mX], lambda hd: (by_head(W)(hd), by_head(XT)(hd)))
                if level == 0:
                    mX = tt([m2], X.ap, X.ap, bX.ap, ALU.subtract)
                    bX.release(mX)
                mXT = tt([m2], XT.ap, XT.ap, bT.ap, ALU.subtract)
                bT.release(mXT)
                W.release(m2)
            L.release(mN)
            LT.release(mJ, mNT)
            X.release(m2, mX)
            yield
            U, WT = pool.take(), pool.take()
            b1, m1 = per_head([mXT, vb_done], lambda hd: (by_head(XT)(hd), by_head(vb)(hd)))
            b2, m2 = per_head([kb_done], lambda hd: (by_head(kb)(hd), by_head(XT)(hd)))
            U_done = self.copy([m1, U.free], U.ap, b1.ap, "scalar")
            WT_done = self.copy([m2, WT.free], WT.ap, b2.ap, "vector")
            b1.release(U_done)
            b2.release(WT_done)
            XT.release(m2)
            vb.release(m2)
            kb.release(m2)
            yield
            S = states[dr]
            new = pool.take()
            o_bank = self.banks.take()
            for half in ((0, 1) if dr == 0 else (1, 0)):
                rows = slice(half * CHUNK, (half + 1) * CHUNK)
                end = half * CHUNK + (CHUNK - 1 if dr == 0 else 0)
                bank = self.banks.take()
                for hd in range(4):
                    lhs = WT.ap[:, hd * P + half * CHUNK:hd * P + (half + 1) * CHUNK]
                    m = self.mm([state_done[dr], WT_done, bank.free], bank.ap[rows, hd * P:(hd + 1) * P], lhs, S[:, hd, :], True, True)
                m_new = self.tt([m, U_done, new.free], new.ap[rows, :], U.ap[rows, :], bank.ap[rows, :], ALU.subtract)
                bank.release(m_new)
                yield
                for hd in range(4):
                    c = slice(hd * P + half * CHUNK, hd * P + (half + 1) * CHUNK)
                    out = o_bank.ap[rows, hd * P:(hd + 1) * P]
                    self.mm([qe_done, o_bank.free, QKT_done, m_new], out, qe.ap[:, c], S[:, hd, :], True, False)
                    m_o = self.mm([], out, QKT.ap[rows, c], new.ap[rows, hd * P:(hd + 1) * P], False, True)
                bank = self.banks.take()
                for hd in range(4):
                    m = self.mm([kd_done, bank.free], bank.ap[:, hd * P:(hd + 1) * P], kd.ap[rows, hd * P:(hd + 1) * P],
                                new.ap[rows, hd * P:(hd + 1) * P], True, True)
                ms = self.tt([m_o, eg_done, state_done[dr]], S, S, heads(eg.ap)[:, :, end:end + 1].to_broadcast([P, 4, P]), ALU.mult, "vector")
                ms = self.tt([ms, m], S, S, heads(bank.ap), ALU.add)
                bank.release(ms)
                state_done[dr] = [ms]
                yield
            for b in (WT, new, qe, QKT, kd):
                b.release(m)
            U.release(m_new)
            eg.release(ms, qe_done)
            first = i not in o_done
            if first:
                mo = self.copy([m_o], o_acc[:, i, :], o_bank.ap, "vector")
            else:
                mo = self.tt([m_o, o_done[i]], o_acc[:, i, :], o_acc[:, i, :], o_bank.ap, ALU.add)
            o_bank.release(mo)
            o_done[i] = mo

        for step in range(TT):
            running = [unit(0, step), unit(1, TT - 1 - step)]
            while running:
                for u in list(running):
                    try:
                        next(u)
                    except StopIteration:
                        running.remove(u)

        q.stage()
        sq = [pool.buffers[n].ap for n in range(2)]
        outs = Rotation([pool.buffers[n].ap for n in range(2, 4)])
        ss = self.tiny(TT, 4)
        for i in range(TT):
            m = self.act([], sq[i % 2], o_acc[:, i, :], ACT.Square) if i < 2 else \
                self.act([last_reduce[i - 2]], sq[i % 2], o_acc[:, i, :], ACT.Square)
            if i == 0:
                last_reduce = []
            m = self.reduce([m], ss[:, i, :], heads(sq[i % 2]), ALU.add)
            last_reduce.append(m)
        m = self.act([m], ss, ss, ACT.Sqrt, bias=self.c("eps"), scale=1.0 / P)
        inv = self.recip([m], ss, ss)
        for i in range(TT):
            b = outs.take()
            m = self.tt([inv, b.free], heads(b.ap), heads(o_acc[:, i, :]), spread(ss[:, i, :]), ALU.mult)
            m = self.tt([m], heads(b.ap), heads(b.ap), over_heads(self.r("dn_out_g")), ALU.mult)
            m = self.tt([m, z_done[i]], b.ap, b.ap, z[:, i, :], ALU.mult)
            self.turn_row(b, m, mixed, 4, i)
        self.residual_add(d["w_out_2"], mixed)

    def moe(self):
        d, q = self.dram, self.q
        entry = q.stage()
        self.work_at = 0
        x_tok = self.area(TT, D)
        expert_slots = [self.ring[:, 0:EXPERT], self.ring[:, EXPERT:2 * EXPERT], self.area(EXPERT), self.area(EXPERT)]
        hT = self.area(DC, T)
        self.rms_tmp = self.area(4, T)
        staging = Rotation([self.area(D) for _ in range(2)])
        h = self.rms(self.x_done, hT, self.v("ln2_g", 0, DC))

        ring_free = [m for b in self.slabs.buffers for m in b.free]
        slots = Rotation(expert_slots)
        for n, s in enumerate(slots.buffers):
            s.free = ring_free if n < 2 else entry
            s.lane = self.lane(f"expert{n}_in")
            s.over_lane = self.lane(f"overflow{n}_in")
        names = ("w_gate", "w_up", "w_down")
        part = {n: d[n] for n in names}
        pieces = [(0, 2048, "w_gate"), (2048, 2048, "w_up"), (4096, 2048, "w_down")]

        def load_expert(e):
            s = slots.take()
            for at, n, name in pieces:
                s.landed = s.lane.copy("sync", s.free, s.ap[:, at:at + n], part[name][e * P:(e + 1) * P, :])
            return s

        def load_overflow(n, w_index, ready):
            s = slots.take()
            for at, width, name in pieces:
                s.landed = s.over_lane.indirect([s.free, ready], out=s.ap[:, at:at + width], out_offset=None,
                                           in_=part[name], in_offset=bass.IndirectOffsetOnAxis(ap=w_index[:, n:n + 1], axis=0),
                                           bounds_check=EXPERTS * P - 1, oob_is_err=False)
            return s

        router_lane = self.lane("router_in")
        wr = self.shaped(self.rms_tmp.rearrange("p a b -> p (a b)")[:, 0:DC * 72], (DC, 72))
        router_in = router_lane.copy("scalar", [h], wr, d["router_w"].rearrange("(k p) n -> p k n", p=P))
        bank = self.banks.take()
        for i in range(TT):
            for k in range(DC):
                m = self.mm([bank.free, router_in, h], bank.ap[:, i * 72:(i + 1) * 72], hT[:, k, i * P:(i + 1) * P],
                            wr[:, k, :], k == 0, k == DC - 1)
        lg = self.shaped(self.rms_tmp.rearrange("p a b -> p (a b)")[:, 640:640 + 288], (TT, 72))
        m = self.tt([m], lg, bank.ap[:, 0:288].rearrange("p (i n) -> p i n", i=TT),
                    self.r("router_b").unsqueeze(1).to_broadcast([P, TT, 72]), ALU.add)
        bank.release(m)
        lg_done = m

        h_rows = self.nc.dram_tensor("h_rows", [PICKS, D], F32, kind="Internal").ap()
        y_rows = self.nc.dram_tensor("y_rows", [PICKS, D], F32, kind="Internal").ap()
        rows_lane = [self.lane(f"h_rows_out{i}") for i in range(2)]
        rows_out = []
        x_rows = []
        for i in range(TT):
            b = staging.take()
            marks = []
            for src, dst, free, rdy in ((hT, b.ap, b.free, h), (self.xT3, x_tok[:, i, :], [], self.x_done)):
                for half in range(2):
                    bank = self.banks.take()
                    for j in range(4):
                        m = self.turn([rdy, bank.free], bank.ap[:, j * P:(j + 1) * P],
                                      src[:, half * 4 + j, i * P:(i + 1) * P], signal=j == 3)
                    m = self.copy([m, free], dst[:, half * 512:(half + 1) * 512], bank.ap,
                                  "scalar" if src is hT else "vector")
                    bank.release(m)
                    marks.append(m)
            x_rows += marks[2:]
            for c in range(TOP_K):
                out = rows_lane[i % 2].copy("scalar", marks[:2], h_rows[c * T + i * P:c * T + (i + 1) * P, :], b.ap)
            b.release(out)
            rows_out.append(out)

        R = self.tiny
        gmax, gsum, m1c, m2c = R(TT), R(TT), R(TT), R(TT)
        t8, oh_g, ing, oh1, oh2 = R(TT, 8), R(TT, 8), R(TT, 8), R(TT, 8), R(TT, 8)
        cm = R(TT)
        gates = R(TOP_K, TT)
        wide = lambda c, n=8: c.unsqueeze(2).to_broadcast([P, TT, n])
        rev = self.c("rev8").unsqueeze(1).to_broadcast([P, TT, 8])
        tt, ts, red = self.tt, self.ts, self.reduce

        def first_max(m, src, top, out):
            m = red([m], top, src, ALU.max)
            m = tt([m], t8, src, wide(top), ALU.is_equal)
            m = tt([m], t8, t8, rev, ALU.mult)
            m = red([m], cm, t8, ALU.max)
            return tt([m], out, t8, wide(cm), ALU.is_equal)

        m = first_max(lg_done, lg[:, :, 0:8], gmax, oh_g)
        m = tt([m], t8, lg[:, :, 0:8], wide(gmax), ALU.subtract)
        m = self.act([m], t8, t8, ACT.Exp)
        m = red([m], gsum, t8, ALU.add)
        m = self.recip([m], gsum, gsum)
        big = self.shaped(self.rms_tmp.rearrange("p a b -> p (a b)")[:, 1024:1024 + 256], (TT, 64))
        el = lg[:, :, 8:72].rearrange("p i (g e) -> p i g e", g=8)
        big4 = big.rearrange("p i (g e) -> p i g e", g=8)
        m = tt([m], big4, el, oh_g.unsqueeze(3).to_broadcast([P, TT, 8, 8]), ALU.mult)
        m = red([m], ing, big.rearrange("p i (g e) -> p i e g", g=8), ALU.add)
        m = first_max(m, ing, m1c, oh1)
        m = self.stt([m], ing, oh1, NEG, ing, ALU.mult, ALU.add)
        m = first_max(m, ing, m2c, oh2)
        m = tt([m], m2c, m2c, m1c, ALU.subtract)
        m = self.act([m], m2c, m2c, ACT.Exp)
        m = ts([m], m1c, m2c, 1.0, ALU.add)
        m = self.recip([m], m1c, m1c)
        m = tt([m], gates[:, 0, :], m1c, gsum, ALU.mult)
        m = tt([m], gates[:, 1, :], gates[:, 0, :], m2c, ALU.mult)
        gates_done = m
        rest = self.area(3 * 512 + 1024)
        A = self.shaped(rest[:, 0:512], (PICK_TILES, EXPERTS))
        prod = self.shaped(rest[:, 512:1024], (PICK_TILES, EXPERTS))
        A_main = self.shaped(rest[:, 1024:1536], (PICK_TILES, EXPERTS))
        who = self.shaped(rest[:, 1536:2560], (PICK_TILES, P))
        for c, oh in enumerate((oh1, oh2)):
            for i in range(TT):
                m = tt([m], A[:, c * TT + i, :].rearrange("p (g e) -> p g e", g=8),
                       oh_g[:, i, :].unsqueeze(2).to_broadcast([P, 8, 8]),
                       oh[:, i, :].unsqueeze(1).to_broadcast([P, 8, 8]), ALU.mult)
        A_done = m
        bank = self.banks.take()
        for n in range(PICK_TILES):
            for j in range(n + 1):
                m = self.mm([A_done, bank.free], bank.ap[:, n * 64:(n + 1) * 64],
                            self.c("before") if j == n else self.c("ones"), A[:, j, :], j == 0, j == n)
        bank2 = self.banks.take()
        for n in range(PICK_TILES):
            m_c = self.mm([bank2.free], bank2.ap[0:64, 0:1], A[:, n, :], self.c("ones")[:, 0:1], n == 0, n == PICK_TILES - 1)
        rank, blk, off, who_e, q_blk = (R(PICK_TILES) for _ in range(5))
        m = tt([m], prod, bank.ap.rearrange("p (n e) -> p n e", n=PICK_TILES), A, ALU.mult)
        bank.release(m)
        m = red([m], rank, prod, ALU.add)
        over = R(MORE + 1)
        counts = R(1)
        m_x = self.copy([m_c], counts[0:64, :], bank2.ap[0:64, 0:1], "vector")
        bank2.release(m_x)
        m_x = ts([m_x], over[0:64, 0:MORE], self.c("caps", 64), counts[0:64, 0:1], ALU.is_lt)
        m_x = red([m_x], over[0:64, MORE:MORE + 1], over[0:64, 0:MORE], ALU.add)
        m_x = ts([m_x], who[0:64, 0, :], self.c("ones", 64), over[0:64, MORE:MORE + 1], ALU.mult)
        bank = self.banks.take()
        m_x = self.mm([m_x, bank.free], bank.ap[:, 0:64], who[0:64, 0, :], self.c("before", 64)[:, 0:64], True, True)
        spread_e = lambda ap: ap.unsqueeze(1).to_broadcast([P, PICK_TILES, EXPERTS])
        m = tt([m, m_x], prod, A, spread_e(bank.ap[:, 0:64]), ALU.mult)
        bank.release(m)
        m = red([m], off, prod, ALU.add)
        m = tt([m], prod, A, spread_e(self.c("expert")), ALU.mult)
        m = red([m], who_e, prod, ALU.add)
        scr = R(PICK_TILES, OVER)
        m = tt([m], scr[:, :, 0:MORE], rank.unsqueeze(2).to_broadcast([P, PICK_TILES, MORE]),
               self.c("caps").unsqueeze(1).to_broadcast([P, PICK_TILES, MORE]), ALU.is_ge)
        m = red([m], blk, scr[:, :, 0:MORE], ALU.add)
        m = self.stt([m], rank, blk, -float(CAP), rank, ALU.mult, ALU.add)
        main = R(PICK_TILES)
        m = ts([m], main, blk, 0.0, ALU.is_equal)
        m = tt([m], A_main, A, main.unsqueeze(2).to_broadcast([P, PICK_TILES, EXPERTS]), ALU.mult)
        m = tt([m], q_blk, off, blk, ALU.add)
        m = self.stt([m], main, main, -1.0, self.c("ones")[:, 0:8], ALU.mult, ALU.add)
        m = tt([m], q_blk, q_blk, main, ALU.mult)
        m = ts([m], q_blk, q_blk, -1.0, ALU.add)
        m = tt([m], scr, q_blk.unsqueeze(2).to_broadcast([P, PICK_TILES, OVER]),
               self.c("block").unsqueeze(1).to_broadcast([P, PICK_TILES, OVER]), ALU.is_equal)
        for n in range(PICK_TILES):
            m = ts([m, m_x], who[:, n, :], self.c("slot"), rank[:, n:n + 1], ALU.is_equal,
                   self.c("pick")[:, n:n + 1], ALU.mult)
        bank = self.banks.take()
        for n in range(PICK_TILES):
            self.mm([m, bank.free], bank.ap[:, 0:EXPERTS], who[:, n, :], A_main[:, n, :], n == 0, n == PICK_TILES - 1)
        for n in range(PICK_TILES):
            m_t = self.mm([], bank.ap[:, 64:64 + OVER], who[:, n, :], scr[:, n, :], n == 0, n == PICK_TILES - 1)
        zero = R(PICK_TILES)
        m = ts([m], zero, rank, 0.0, ALU.is_equal)
        m = tt([m], zero, zero, who_e, ALU.mult)
        for n in range(PICK_TILES):
            m = ts([m, m_t], who[:, n, :], self.c("ones"), zero[:, n:n + 1], ALU.mult)
        bank_e = self.banks.take()
        for n in range(PICK_TILES):
            m_e = self.mm([m, bank_e.free], bank_e.ap[:, 0:OVER], who[:, n, :], scr[:, n, :], n == 0, n == PICK_TILES - 1)
        pairs = EXPERTS // 2 + OVER // 2
        val, none = R(pairs), R(pairs)
        for par in range(2):
            rows = slice(par * 64, par * 64 + 64)
            m = self.copy([m_t], val[rows, 0:32], bank.ap[rows, par:64:2], "vector")
            m = self.copy([m_t], val[rows, 32:40], bank.ap[rows, 64 + par:80:2], "vector")
        m = ts([m], none, val, 0.0, ALU.is_equal, FAR, ALU.mult)
        m = self.stt([m], val, val, -1.0, none, ALU.add, ALU.add)
        row_index = self.index[:, 0:pairs]
        m = self.copy([m], row_index, val, "vector")
        index_done = m
        v2, n2 = R(OVER), R(OVER)
        m = ts([m_e], n2, bank_e.ap[:, 0:OVER], 0.0, ALU.is_equal, FAR, ALU.mult)
        m = self.stt([m], v2, bank_e.ap[:, 0:OVER], float(P), n2, ALU.mult, ALU.add)
        bank.release(index_done)
        bank_e.release(m)
        m = ts([m], v2, v2, self.c("part"), ALU.add)
        w_index = self.index[:, pairs:pairs + OVER]
        m = self.copy([m], w_index, v2, "vector")
        w_index_done = m

        marks = q.stage()
        keep = self.work_at
        self.work_at = TT * D + 2 * EXPERT
        gathered = Rotation([self.area(D) for _ in range(3)])
        slot_T = Rotation([self.area(DC, P) for _ in range(2)])
        y_buf = Rotation([self.area(D) for _ in range(2)])
        hid = Rotation([self.area(4, CAP) for _ in range(2)])
        y_lane = [self.lane(f"y_out{i}") for i in range(2)]
        g_lane = [self.lane(f"gather{i}") for i in range(3)]
        for n, b in enumerate(gathered.buffers):
            b.free = [q.do("gpsimd", [], lambda e, b=b: e.memset(b.ap, 0.0)), rows_out[-2], rows_out[-1]]
            b.lane = g_lane[n]
        for n, b in enumerate(y_buf.buffers):
            b.lane = y_lane[n]
        gather_of, turned_of, y_out = {}, {}, []

        def gather(pr):
            b = gathered.take()
            m = b.lane.indirect([b.free, index_done], out=b.ap, out_offset=None, in_=h_rows,
                                in_offset=bass.IndirectOffsetOnAxis(ap=row_index[:, pr:pr + 1], axis=0),
                                bounds_check=PICKS - 1, oob_is_err=False)
            gather_of[pr] = b, m

        def turn_slots(pr):
            b, landed = gather_of.pop(pr)
            s = slot_T.take()
            out = []
            for half in range(2):
                bank = self.banks.take()
                for j in range(4):
                    m = self.turn([landed, bank.free], bank.ap[:, j * P:(j + 1) * P],
                                  b.ap[:, half * 4 + j:D:DC], signal=j == 3)
                m = self.copy([m, s.free], s.ap[:, half * 4:half * 4 + 4, :], bank.ap.rearrange("p (a b) -> p a b", a=4),
                              "scalar" if half else "vector")
                bank.release(m)
                out.append(m)
            b.release(*out)
            turned_of[pr] = s, out

        def up(s, half, w):
            sT, ready = s
            bank = self.banks.take()
            for part_ in range(4):
                side, fc = part_ // 2, part_ % 2
                wv = self.shaped(w.ap[:, side * 2048:(side + 1) * 2048], (DC, DE))
                for k in range(DC):
                    m = self.mm([bank.free, w.landed, ready], bank.ap[:, part_ * CAP:(part_ + 1) * CAP],
                                wv[:, k, fc:DE:2], sT.ap[:, k, half * CAP:(half + 1) * CAP], k == 0, k == DC - 1)
            hb = hid.take()
            gate, upv = hb.ap[:, 0:2, :], bank.ap[:, 2 * CAP:4 * CAP].rearrange("p (a b) -> p a b", a=2)
            a = self.act([m, hb.free], gate, bank.ap[:, 0:2 * CAP].rearrange("p (a b) -> p a b", a=2), ACT.Silu)
            a = self.tt([a], hb.ap[:, 2:4, :], gate, upv, ALU.mult)
            bank.release(a)
            return hb, a, m

        def down(banks, half, hb, ready, w, free):
            wd = self.shaped(w.ap[:, 4096:6144], (2, D))
            for n in range(2):
                for fc in range(2):
                    m = self.mm([free, ready], banks[n].ap[half * CAP:(half + 1) * CAP, :], hb.ap[:, 2 + fc, :],
                                wd[:, fc, n * 512:(n + 1) * 512], fc == 0, fc == 1)
            hb.release(m)
            w.release(m)
            return m

        n_pairs = EXPERTS // 2 + OVER // 2
        blocks = list(range(EXPERTS + OVER))
        gather(0)
        gather(1)
        turn_slots(0)
        for pr in range(n_pairs):
            if pr + 2 < n_pairs:
                gather(pr + 2)
            if pr + 1 < n_pairs:
                turn_slots(pr + 1)
            s, ready = turned_of.pop(pr)
            weights, ups = [], []
            for half in range(2):
                n = 2 * pr + half
                w = load_expert(n) if n < EXPERTS else load_overflow(n - EXPERTS, w_index, w_index_done)
                weights.append(w)
                hb, hb_done, m = up((s, ready), half, w)
                ups.append((hb, hb_done))
            s.release(m)
            banks = [self.banks.take() for _ in range(2)]
            free = [banks[0].free, banks[1].free]
            for half in range(2):
                m = down(banks, half, *ups[half], weights[half], free)
            y = y_buf.take()
            out = []
            for n in range(2):
                mc = self.copy([m, y.free], y.ap[:, n * 512:(n + 1) * 512], banks[n].ap, "scalar" if n else "vector")
                banks[n].release(mc)
                out.append(mc)
            done = y.lane.indirect(out, out=y_rows, out_offset=bass.IndirectOffsetOnAxis(ap=row_index[:, pr:pr + 1], axis=0),
                                   in_=y.ap, in_offset=None, bounds_check=PICKS - 1, oob_is_err=False)
            y.release(done)
            y_out.append(done)

        for e in ("scalar",):
            q.wait(e, [y_out[-2], y_out[-1]])
        marks = q.stage()
        self.work_at = TT * D
        ys = [self.area(D) for _ in range(2 * TT)] if self.work_at + 2 * TT * D <= self.WORK else None
        lanes = [self.lane(f"y_in{i}") for i in range(TT)]
        out_lane = self.lane("out")
        for i in range(TT):
            for c in range(TOP_K):
                landed = lanes[i].copy("scalar", [marks], ys[2 * i + c], y_rows[c * T + i * P:c * T + (i + 1) * P, :])
            m = x_rows
            for c in range(TOP_K):
                m = [self.stt([landed, m, gates_done], x_tok[:, i, :], ys[2 * i + c], gates[:, c, i:i + 1], x_tok[:, i, :],
                              ALU.mult, ALU.add)]
            final = out_lane.copy("sync", m, d["out"][i * P:(i + 1) * P, :], x_tok[:, i, :])
        q.wait("sync", [final])


STAGES = ("block1_mixer", "block1_mlp", "block2_attention", "deltanet", "moe")


def build(nc, dram, stages=STAGES):
    with ExitStack() as ctx:
        k = Kernel(nc, ctx, dram)
        for s in stages:
            {"block1_mixer": k.block1_mixer, "block1_mlp": k.block1_mlp, "block2_attention": k.block2_attention,
             "deltanet": k.deltanet, "moe": k.moe}[s]()
        block = ctx.enter_context(nc.Block())
        k.q.play(block)
    return k


def pack(x):
    f = np.float32
    a = {k: np.asarray(v) for k, v in x.items()}
    flat = lambda n: a[n].reshape(-1)
    gain = lambda n: np.concatenate([flat(n), flat(n)])
    vec = np.concatenate([
        flat("mod_b"), flat("c"), flat("norm1_g"), flat("norm2_g"), flat("final_g"), flat("ln1_g_2"),
        flat("ln2_g_2"), flat("pool_scale"), flat("ffn_conv_b"), flat("ffn_conv_w"), flat("dn_conv_w_2"),
        gain("attn_q_norm_g_2"), gain("attn_k_norm_g_2")]).reshape(-1, P)
    vec = np.concatenate([vec, np.zeros((VEC_TILES * P - len(vec), P), f)])
    row = np.concatenate([
        flat("attn_out_norm_g_2"), flat("dn_out_norm_g_2"), flat("b_f"), flat("router_group_b_2"),
        flat("router_expert_b_2"), flat("dn_dt_bias_2"), flat("dn_a_log_2")])[None, :]
    rpb = a["attn_rpb_2"][0]
    side = GRID - WIN_W
    return {
        "x": a["x"][0], "mod_w": a["mod_w"][0], "w_in": a["w_in"][0], "w_out": a["w_out"][0],
        "ffn_up": a["ffn_up"][0], "ffn_down": a["ffn_down"][0], "pool_w": a["pool_w"][0],
        "w_in_2": a["w_in_2"][0], "w_out_2": a["w_out_2"][0],
        "router_w": np.concatenate([a["router_group_w_2"][0], a["router_expert_w_2"][0]], 1),
        "w_gate": a["expert_w_gate_2"].reshape(EXPERTS * P, DC * DE),
        "w_up": a["expert_w_up_2"].reshape(EXPERTS * P, DC * DE),
        "w_down": a["expert_w_down_2"].reshape(EXPERTS * P, 2 * D),
        "rpb": np.pad(rpb, ((0, 0), (0, 0), (side, side)))[:, :, ::-1],
        "channel_vectors": vec, "row_vectors": row,
        "constants": np.concatenate(list(constants().values()), 1),
    }


def kernel(**inputs):
    from concourse import bacc
    from concourse.bass_utils import run_bass_kernel_spmd

    arrays = {n: np.ascontiguousarray(v) for n, v in pack(inputs).items()}
    nc = bacc.Bacc("TRN2", target_bir_lowering=False, num_devices=1)
    dram = {n: nc.dram_tensor(f"{n}_dram", v.shape, mybir.dt.from_np(v.dtype), kind="ExternalInput").ap()
            for n, v in arrays.items()}
    dram["out"] = nc.dram_tensor("out_dram", (T, D), F32, kind="ExternalOutput").ap()
    build(nc, dram)
    r = run_bass_kernel_spmd(nc, [{f"{n}_dram": v for n, v in arrays.items()}], core_ids=[0])
    return r.results[0]["out_dram"].reshape(1, T, D)
```

```python
from contextlib import ExitStack

import numpy as np

import concourse.bass as bass
from concourse import mybir

ALU = mybir.AluOpType
ACT = mybir.ActivationFunctionType
AXIS_X = mybir.AxisListType.X
F32 = mybir.dt.float32
U32 = mybir.dt.uint32

P = 128
D = 1024
DC = D // P
T = 512
TT = T // P
HEADS = 8
DH = 64
QW = HEADS * DH
POOL_WINDOWS = (2, 4, 8, 16)
FF = 2816
FC = FF // P
EPS = 1e-6
GRID = 64
ROWS = T // GRID
WIN_W = 16
WIN_H = 8
DN_HEADS = 4
DN_TAPS = 5
CHUNK = 64
GROUPS = 8
PER_GROUP = 8
EXPERTS = GROUPS * PER_GROUP
DE = 256
CAP = 64
TOP_K = 2
PICKS = TOP_K * T
PICK_TILES = PICKS // P
MORE = T // CAP - 1
OVER = 16
FAR = 1.0e6
NEG = -1.0e30

MOD_W = 2048
SLAB = 4096
SLABS = 3
DOWN_W = 2048
UP_W = 2 * DOWN_W

VEC = {}
_at = 0
for _name, _rows in (("mod_b", 48), ("c", DC), ("norm1_g", DC), ("norm2_g", DC), ("final_g", DC),
                     ("ln1_g", DC), ("ln2_g", DC), ("pool_scale", 4), ("conv_b", 2 * FC),
                     ("conv_w", 3 * 2 * FC), ("dn_conv_w", DN_TAPS * 12), ("q_gain", 1),
                     ("k_gain", 1)):
    VEC[_name] = (_at, _rows)
    _at += _rows
VEC_TILES = -(-_at // P)

ROW = {}
_at = 0
for _name, _cols in (("attn_out_g", QW), ("dn_out_g", P), ("b_f", HEADS), ("router_b", 72),
                     ("dt_bias", 8), ("a_log", 8)):
    ROW[_name] = (_at, _cols)
    _at += _cols
ROW_W = _at


def constants():
    i = np.arange(P)[:, None]
    j = np.arange(P)[None, :]
    same = i // CHUNK == j // CHUNK
    f = np.float32
    out = {
        "ident": (i == j).astype(f),
        "ones": np.ones((P, P), f),
        "ones64": same.astype(f),
        "upto": (i <= j).astype(f),
        "before": (i < j).astype(f),
        "causal": np.where(j <= i, 0, NEG).astype(f),
        "cum0": (same & (i <= j)).astype(f), "cum1": (same & (i >= j)).astype(f),
        "bar0": np.where(same & (j <= i), 0, -NEG).astype(f),
        "bar1": np.where(same & (j >= i), 0, -NEG).astype(f),
        "strict0": (same & (j < i)).astype(f), "strict1": (same & (j > i)).astype(f),
        "in16": (i // 16 == j // 16).astype(f),
        "join32": ((i // 32 == j // 32) & (i // 16 != j // 16)).astype(f),
        "join64": (same & (i // 32 != j // 32)).astype(f),
    }
    out["head_row"] = np.concatenate([np.repeat(i == h, P, 1) for h in range(HEADS)], 1).astype(f)
    t = np.arange(16)
    out["pool_count"] = np.tile(np.concatenate([1 / np.minimum(t + 1, w) for w in POOL_WINDOWS]), (P, 1)).astype(f)
    col, key = np.arange(P)[:, None] % GRID, np.arange(GRID)[None, :]
    first = np.clip(col - WIN_W // 2, 0, GRID - WIN_W)
    out["window"] = np.where((key >= first) & (key < first + WIN_W), 0, NEG).astype(f)[:, ::-1]
    out["rev8"] = np.tile(8 - np.arange(8), (P, 1)).astype(f)
    out["pick"] = (np.arange(PICK_TILES)[None, :] * P + i + 1).astype(f)
    out["slot"] = np.tile(np.arange(P) % CAP, (P, 1)).astype(f)
    out["block"] = np.tile(np.arange(OVER), (P, 1)).astype(f)
    out["expert"] = np.tile(np.arange(EXPERTS) + 1, (P, 1)).astype(f)
    out["caps"] = np.tile((np.arange(MORE) + 1) * CAP, (P, 1)).astype(f)
    out["part"] = (i - P).astype(f)
    out["eps"] = np.full((P, 1), EPS, f)
    return out


CONST = {}
_at = 0
for _name, _table in constants().items():
    CONST[_name] = (_at, _table.shape[1])
    _at += _table.shape[1]
CONST_W = _at


class Queues:

    ENGINES = ("tensor", "vector", "scalar", "gpsimd", "sync")

    def __init__(self, nc, ctx):
        self.queue = {e: [] for e in self.ENGINES}
        self.done = {e: ctx.enter_context(nc.semaphore(f"{e}_done")) for e in self.ENGINES}
        self.count = dict.fromkeys(self.ENGINES, 0)
        self.waited = {e: {} for e in self.ENGINES}

    def wait(self, engine, marks):
        for mark in marks:
            if mark is None:
                continue
            if isinstance(mark, list):
                self.wait(engine, mark)
                continue
            sem, value = mark
            if self.waited[engine].get(sem.name, 0) < value:
                self.waited[engine][sem.name] = value
                self.queue[engine].append(lambda e, sem=sem, value=value: e.wait_ge(sem, value))

    def do(self, engine, after, instruction, signal=True):
        self.wait(engine, after)
        if not signal:
            self.queue[engine].append(instruction)
            return None
        sem = self.done[engine]
        self.count[engine] += 1
        self.queue[engine].append(lambda e: instruction(e).then_inc(sem, 1))
        return (sem, self.count[engine])

    def last(self, engine):
        return (self.done[engine], self.count[engine]) if self.count[engine] else None

    def stage(self):
        marks = [self.last(e) for e in ("tensor", "vector", "scalar", "gpsimd")]
        for e in ("tensor", "vector", "scalar", "gpsimd"):
            self.wait(e, marks)
        return marks

    def guard(self, value):
        self.before = {e: dict(w) for e, w in self.waited.items()}
        self.guards = {}
        for name in self.ENGINES[:4]:
            def begin(e, name=name):
                self.guards[name] = e.If(e.value_load(value) != 0)
                self.guards[name].__enter__()
            self.queue[name].append(begin)

    def end_guard(self, nc, ctx, marks):
        marks = marks + [self.last(e) for e in self.ENGINES[:4]]
        for name in self.ENGINES[:4]:
            self.wait(name, marks)
            self.queue[name].append(lambda e, name=name: self.guards[name].__exit__(None, None, None))
        self.waited = self.before
        for name in self.ENGINES[:4]:
            self.done[name] = ctx.enter_context(nc.semaphore(f"{name}_done_after"))
            self.count[name] = 1
            self.queue[name].append(lambda e, sem=self.done[name]: e.sem_inc(sem, 1))

    def play(self, block):
        for name in self.ENGINES:
            def run(engine, name=name):
                for step in self.queue[name]:
                    step(engine)
            {"tensor": block.tensor, "vector": block.vector, "scalar": block.scalar,
             "gpsimd": block.gpsimd, "sync": block.sync}[name](run)


class Buffer:

    def __init__(self, ap):
        self.ap, self.free, self.busy = ap, [], False

    def release(self, *marks):
        self.free, self.busy = list(marks), False


class Rotation:
    def __init__(self, aps):
        self.buffers, self.next = [Buffer(a) for a in aps], 0

    def take(self):
        for _ in self.buffers:
            b = self.buffers[self.next]
            self.next = (self.next + 1) % len(self.buffers)
            if not b.busy:
                b.busy = True
                return b
        raise ValueError("no buffer is free")


class Lane:

    def __init__(self, nc, ctx, q, name):
        self.q, self.sem, self.count = q, ctx.enter_context(nc.semaphore(name)), 0

    def copy(self, engine, after, out, in_):
        self.q.wait(engine, after)
        self.count += 16
        self.q.queue[engine].append(lambda e: e.dma_start(out, in_).then_inc(self.sem, 16))
        return (self.sem, self.count)

    def indirect(self, after, **how):
        self.q.wait("gpsimd", after)
        self.count += 16
        self.q.queue["gpsimd"].append(lambda e: e.indirect_dma_start(**how).then_inc(self.sem, 16))
        return (self.sem, self.count)


class Kernel:
    def __init__(self, nc, ctx, dram):
        self.nc, self.ctx, self.dram = nc, ctx, dram
        self.q = q = Queues(nc, ctx)

        def sbuf(name, cols, dtype=F32):
            return ctx.enter_context(nc.sbuf_tensor(name, [P, cols], dtype))

        self.const = sbuf("constants", CONST_W)
        self.vec = sbuf("channel_vectors", VEC_TILES * P)
        self.row = sbuf("row_vectors", ROW_W)
        self.small = sbuf("small", 1400)
        self.index = sbuf("indices", 64, U32)
        self.xT = sbuf("residual_T", DC * T)
        self.ring = sbuf("weight_ring", SLABS * SLAB)
        self.WORK = 30900
        self.work = sbuf("work", self.WORK)
        self.work_at = self.small_at = 0
        banks = [ctx.enter_context(nc.psum_tensor(f"bank{i}", [P, 512], F32)) for i in range(8)]
        self.banks = Rotation([b[:, :] for b in banks])
        self.slabs = Rotation([self.ring[:, i * SLAB:(i + 1) * SLAB] for i in range(SLABS)])
        self.slab_lanes = [Lane(nc, ctx, q, f"slab{i}_in") for i in range(SLABS)]
        self.lanes = 0
        self.flip = 0

    def lane(self, name):
        return Lane(self.nc, self.ctx, self.q, name)

    def area(self, *shape):
        n = int(np.prod(shape))
        ap = self.work[:, self.work_at:self.work_at + n]
        self.work_at += n
        assert self.work_at <= self.WORK, self.work_at
        return self.shaped(ap, shape)

    @staticmethod
    def shaped(ap, shape):
        if len(shape) == 2:
            return ap.rearrange("p (a b) -> p a b", a=shape[0])
        if len(shape) == 3:
            return ap.rearrange("p (a b c) -> p a b c", a=shape[0], b=shape[1])
        return ap

    def tiny(self, *shape):
        n = int(np.prod(shape))
        ap = self.small[:, self.small_at:self.small_at + n]
        self.small_at += n
        assert self.small_at <= 1400
        return self.shaped(ap, shape)

    def c(self, name, rows=P):
        at, n = CONST[name]
        return self.const[0:rows, at:at + n]

    def v(self, name, i=0, n=1):
        at = VEC[name][0] + i
        return self.vec[:, at:at + n]

    def r(self, name):
        at, n = ROW[name]
        return self.row[:, at:at + n]

    def mm(self, after, out, lhsT, rhs, start, stop, signal=None):
        signal = stop if signal is None else signal
        return self.q.do("tensor", after, lambda e: e.matmul(out, lhsT, rhs, start=start, stop=stop), signal)

    def turn(self, after, out, in_, signal=True):
        ident = self.c("ident")[0:in_.shape[0], 0:in_.shape[0]]
        return self.q.do("tensor", after, lambda e: e.transpose(out, in_, ident), signal)

    def act(self, after, out, in_, func, bias=0.0, scale=1.0, accum=None):
        more = {} if accum is None else {"accum_out": accum}
        if func == ACT.Copy:
            return self.q.do("scalar", after, lambda e: e.activation(out, in_, func, scale=scale, **more))
        return self.q.do("scalar", after,
                         lambda e: e.activation(out, in_, func, bias=bias, scale=scale, **more))

    def tt(self, after, out, a, b, op, engine="vector"):
        return self.q.do(engine, after, lambda e: e.tensor_tensor(out, a, b, op))

    def ts(self, after, out, a, s1, op0, s2=None, op1=None, engine="vector"):
        if op1 is None:
            return self.q.do(engine, after, lambda e: e.tensor_scalar(out, a, s1, None, op0))
        return self.q.do(engine, after, lambda e: e.tensor_scalar(out, a, s1, s2, op0, op1))

    def stt(self, after, out, a, s, b, op0, op1):
        return self.q.do("vector", after, lambda e: e.scalar_tensor_tensor(
            out=out, in0=a, scalar=s, in1=b, op0=op0, op1=op1))

    def reduce(self, after, out, in_, op, negate=False):
        return self.q.do("vector", after, lambda e: e.tensor_reduce(out, in_, AXIS_X, op, negate=negate))

    def copy(self, after, out, in_, engine=None):
        if engine is None:
            self.flip ^= 1
            engine = "vector" if self.flip else "scalar"
        if engine == "scalar":
            return self.act(after, out, in_, ACT.Copy)
        return self.q.do(engine, after, lambda e: e.tensor_copy(out, in_))

    def recip(self, after, out, in_):
        return self.q.do("vector", after, lambda e: e.reciprocal(out, in_))

    def slab(self, *parts):
        i = self.slabs.next
        b = self.slabs.take()
        for at, shape, source in parts:
            n = int(np.prod(shape))
            mark = self.slab_lanes[i].copy("sync", b.free, self.shaped(b.ap[:, at:at + n], shape), source)
        b.landed = mark
        return b

    def columns(self, weight, first, n=512):
        b = self.slab((0, (DC, n), weight.rearrange("(k p) n -> p k n", p=P)[:, :, first:first + n]))
        b.view = self.shaped(b.ap[:, 0:DC * n], (DC, n))
        return b

    def project(self, after, slab_view, landed, src, cols, n=T):
        bank = self.banks.take()
        for k in range(src.shape[1]):
            mark = self.mm([bank.free, after, landed], bank.ap[:, 0:n], slab_view[:, k, cols], src[:, k, :],
                           k == 0, k == src.shape[1] - 1)
        return bank, mark

    def load_small(self):
        lane = self.lane("small_in")
        d = self.dram
        lane.copy("scalar", [], self.const[:, :], d["constants"])
        stage = self.work[:, 0:VEC_TILES * P].rearrange("p (a b) -> p a b", b=P)
        lane.copy("scalar", [], stage, d["channel_vectors"].rearrange("(a p) n -> p a n", p=P))
        self.small_in = lane.copy("scalar", [], self.row[:, :],
                                  d["row_vectors"].to_broadcast([P, ROW_W]))
        bank = self.banks.take()
        for a in range(VEC_TILES):
            m = self.turn([self.small_in], bank.ap[:, a * P:(a + 1) * P], stage[:, a, :])
        self.vec_done = self.copy([m, self.small_in], self.vec[:, :], bank.ap[:, 0:VEC_TILES * P], "vector")
        bank.release(self.vec_done)

    def load_x(self):
        self.work_at = 4096
        lane = self.lane("x_in")
        x = self.area(TT, D)
        landed = lane.copy("scalar", [], x, self.dram["x"].rearrange("(i p) d -> p i d", p=P))
        xT = self.shaped(self.xT[:, :], (DC, T))
        marks = []
        for k in range(DC):
            bank = self.banks.take()
            for i in range(TT):
                m = self.turn([landed, self.small_in, bank.free], bank.ap[:, i * P:(i + 1) * P],
                              x[:, i, k * P:(k + 1) * P], signal=i == TT - 1)
            marks.append(self.copy([m], xT[:, k, :], bank.ap))
            bank.release(marks[-1])
        self.xT3 = xT
        self.x_done = marks

    def modulation_start(self):
        self.c_act = self.tiny(DC)
        self.c_done = self.act([self.vec_done], self.c_act, self.v("c", 0, DC), ACT.Silu)
        self.mod = self.tiny(48)

    def modulation(self, part, first, last):
        acc = self.mod_acc
        for s in range(first, last):
            w = self.slab((0, (2, MOD_W), self.dram["mod_w"].rearrange("(k p) n -> p k n", p=P)[
                :, 2 * s:2 * s + 2, part * MOD_W:(part + 1) * MOD_W]))
            view = self.shaped(w.ap, (2, MOD_W))
            for k in range(2):
                col = self.c_act[:, 2 * s + k:2 * s + k + 1]
                if s + k == 0:
                    m = self.ts([w.landed, self.c_done, self.mod_free], acc, view[:, 0, :], col, ALU.mult)
                else:
                    m = self.stt([w.landed, m if s + k > first else self.mod_last], acc, view[:, k, :], col, acc,
                                 ALU.mult, ALU.add)
            self.mod_last = m
            w.release(m)

    def modulation_sum(self, part):
        for g in range(4):
            bank = self.banks.take()
            for j in range(4):
                at = (4 * g + j) * P
                m = self.mm([self.mod_last, bank.free], bank.ap[:, j * P:(j + 1) * P], self.mod_acc[:, at:at + P],
                            self.c("ones"), True, True)
            col = part * 16 + g * 4
            done = self.tt([m, self.vec_done], self.mod[:, col:col + 4], bank.ap[:, 0:512:P],
                           self.v("mod_b", col, 4), ALU.add)
            bank.release(done)
        self.mod_free = m
        return done

    def narrow(self, after, weight, landed, n, src, tmp):
        bank = self.banks.take()
        for k in range(DC):
            m = self.mm([bank.free, landed, after], bank.ap[0:n, :], weight[:, k, 0:n], src[:, k, :], k == 0, k == DC - 1)
        m = self.copy([m], tmp[0:n, :], bank.ap[0:n, :], "scalar")
        bank.release(m)
        bank = self.banks.take()
        for i in range(TT):
            m2 = self.turn([m, bank.free], bank.ap[:, i * n:(i + 1) * n], tmp[0:n, i * P:(i + 1) * P], signal=i == TT - 1)
        return bank, bank.ap[:, 0:TT * n].rearrange("p (i n) -> p i n", i=TT), m2

    def rms(self, after, out, gain, shift=None):
        squares = Rotation([self.rms_tmp[:, i, :] for i in range(2)])
        bank = self.banks.take()
        for k in range(DC):
            s = squares.take()
            sq = self.act([after, s.free], s.ap, self.xT3[:, k, :], ACT.Square)
            m = self.mm([sq, bank.free], bank.ap, self.c("ones"), s.ap, k == 0, k == DC - 1, signal=True)
            s.release(m)
        root = self.act([m, self.small_in], self.rms_tmp[:, 2, :], bank.ap, ACT.Sqrt, bias=self.c("eps"), scale=1.0 / D)
        bank.release(root)
        inv = self.recip([root], self.rms_tmp[:, 3, :], self.rms_tmp[:, 2, :])
        marks = []
        for k in range(DC):
            m = self.stt([inv, after], out[:, k, :], self.xT3[:, k, :], gain[:, k:k + 1], self.rms_tmp[:, 3, :],
                         ALU.mult, ALU.mult)
            if shift is not None:
                m = self.act([m], out[:, k, :], out[:, k, :], ACT.Identity, bias=shift[:, k:k + 1])
            marks.append(m)
        return marks

    def gain_of(self, after, scale_at, norm):
        g = self.tiny(DC)
        return g, self.stt([after], g, self.mod[:, scale_at:scale_at + DC], 1.0, self.v(norm, 0, DC), ALU.add, ALU.mult)

    def attend(self, qT, kT, v, width, logits, out_row, ready, outs):
        n_buf = 3
        probs = Rotation([self.area(T) for _ in range(n_buf)])
        turned = Rotation([self.area(T) for _ in range(n_buf)])
        neg_max = self.tiny(TT, HEADS)
        total = self.tiny(TT, HEADS)
        inverse = self.tiny(TT, HEADS)
        state = {}

        def scores(i, h):
            w = width(i)
            rows = slice(64 * (h % 2), 64 * (h % 2) + 64)
            bank = self.banks.take()
            m = self.mm([bank.free, ready], bank.ap[:, 0:w], qT[rows, h // 2, i * P:(i + 1) * P],
                        kT[rows, h // 2, 0:w], True, True)
            p = probs.take()
            m = logits(i, h, bank, m, p)
            m = self.reduce([m], neg_max[:, i, h:h + 1], p.ap[:, 0:w], ALU.max, negate=True)
            m = self.act([m], p.ap[:, 0:w], p.ap[:, 0:w], ACT.Exp, bias=neg_max[:, i, h:h + 1],
                         accum=total[:, i, h:h + 1])
            state[i, h] = [p, m]

        def transposed(i, h):
            w = width(i)
            p, m = state[i, h]
            bank = self.banks.take()
            t = turned.take()
            for j in range(w // P):
                mark = self.turn([m, bank.free], bank.ap[:, j * P:(j + 1) * P], p.ap[:, j * P:(j + 1) * P],
                                 signal=j == w // P - 1)
            p.release(mark)
            mark = self.copy([mark, t.free], t.ap[:, 0:w], bank.ap[:, 0:w])
            bank.release(mark)
            state[i, h] = [t, mark, m]

        def values(i, h):
            t, mark, exp = state.pop((i, h))
            if h == 0:
                state["o"] = self.banks.take()
            o = state["o"]
            for j in range(width(i) // P):
                for half in range(2):
                    m = self.mm([mark, ready, o.free], o.ap[half * DH:(half + 1) * DH, h * DH:(h + 1) * DH],
                                t.ap[:, j * P + half * DH:j * P + (half + 1) * DH],
                                v[:, j, h * DH:(h + 1) * DH], j == 0, j == width(i) // P - 1)
            t.release(m)
            if h == HEADS - 1:
                inv = self.recip([exp], inverse[:, i, :], total[:, i, :])
                b = outs.take()
                o3 = o.ap.rearrange("p (h d) -> p h d", h=HEADS)
                m = self.tt([m, inv, b.free], b.ap.rearrange("p (h d) -> p h d", h=HEADS), o3,
                            inverse[:, i, :].unsqueeze(2).to_broadcast([P, HEADS, DH]), ALU.mult)
                o.release(m)
                out_row(i, b, m)

        units = [(i, h) for i in range(TT) for h in range(HEADS)]
        for n in range(len(units) + 2):
            if n < len(units):
                scores(*units[n])
            if 1 <= n <= len(units):
                transposed(*units[n - 1])
            if n >= 2:
                values(*units[n - 2])

    def turn_row(self, b, mark, mixed, first, i):
        bank = self.banks.take()
        for j in range(4):
            m = self.turn([mark, bank.free], bank.ap[:, j * P:(j + 1) * P], b.ap[:, j * P:(j + 1) * P], signal=j == 3)
        b.release(m)
        out = mixed[:, first:first + 4, i * P:(i + 1) * P]
        m = self.copy([m], out, bank.ap.rearrange("p (a b) -> p a b", a=4))
        bank.release(m)
        self.mixed_marks.append(m)

    def block1_mixer(self):
        d, q = self.dram, self.q
        self.load_small()
        self.modulation_start()
        self.load_x()
        self.mod_acc, self.mod_free = self.area(MOD_W), None
        wf_lane = self.lane("wf_in")
        wf = self.tiny(DC, HEADS)
        wf_in = wf_lane.copy("scalar", [], wf, d["w_in"].rearrange("(k p) n -> p k n", p=P)[:, :, 3 * QW:3 * QW + HEADS])
        self.modulation(0, 0, 4)
        mod_a = self.modulation_sum(0)
        gain, gain_done = self.gain_of(mod_a, DC, "norm1_g")
        q.stage()
        self.work_at = 0
        hT = self.area(DC, T)
        self.rms_tmp = self.area(4, T)
        self.mod_acc = self.area(MOD_W)
        h = self.rms(self.x_done + [gain_done], hT, gain, self.mod[:, 0:DC])

        qT, kT, v, mixed = self.area(4, T), self.area(4, T), self.area(TT, QW), self.area(DC, T)
        w_in = d["w_in"]
        ready = []
        for first, out, scale in ((0, qT, DH ** -0.5), (QW, kT, 1.0)):
            w = self.columns(w_in, first)
            for j in range(4):
                bank, m = self.project(h, w.view, w.landed, hT, slice(j * P, (j + 1) * P))
                done = self.act([m], out[:, j, :], bank.ap, ACT.Copy, scale=scale)
                bank.release(done)
                ready.append(done)
            w.release(m)
            self.modulation(1, 2 * (first // QW), 2 * (first // QW) + 2)
        F_rows, minus_F = self.area(HEADS, T), self.area(T)
        bank, logit, m = self.narrow(h, wf, wf_in, HEADS, hT, minus_F)
        y, a, log_f, F = self.tiny(TT, 8), self.tiny(TT, 8), self.tiny(TT, 8), self.tiny(TT, 8)
        m = self.tt([m], y, logit, self.r("b_f").unsqueeze(1).to_broadcast([P, TT, 8]), ALU.add)
        bank.release(m)
        e = self.softplus_part([m], a, y)
        log_f_done = self.stt([e], log_f, y, 0.0, a, ALU.min, ALU.subtract)
        w = self.columns(w_in, 2 * QW)
        for i in range(TT):
            bank = self.banks.take()
            for k in range(DC):
                m = self.mm([bank.free, w.landed, h], bank.ap, hT[:, k, i * P:(i + 1) * P], w.view[:, k, :],
                            k == 0, k == DC - 1)
            done = self.copy([m], v[:, i, :], bank.ap)
            bank.release(done)
            ready.append(done)
        w.release(m)

        self.mod_b_done = self.modulation_sum(1)
        self.modulation(2, 0, 4)
        bank = self.banks.take()
        for i in range(TT):
            for j in range(i + 1):
                c = self.c("upto") if j == i else self.c("ones")
                self.mm([bank.free, log_f_done], bank.ap[:, i * 8:i * 8 + 8], c, log_f[:, j, :], j == 0, j == i)
        F_done = self.copy([q.last("tensor")], F, bank.ap[:, 0:32].rearrange("p (i h) -> p i h", i=TT), "vector")
        bank.release(F_done)
        bank = self.banks.take()
        for i in range(TT):
            for j in range(i + 1):
                c = self.c("upto") if j == i else self.c("ones")
                self.mm([bank.free, log_f_done], bank.ap[0:8, i * P:(i + 1) * P], log_f[:, j, :], c, j == 0, j == i)
        rows_done = self.act([q.last("tensor")], minus_F[0:8, :], bank.ap[0:8, :], ACT.Copy, scale=-1.0)
        bank.release(rows_done)
        for hd in range(HEADS):
            bank = self.banks.take()
            m = self.mm([bank.free, rows_done], bank.ap, self.c("head_row", 8)[:, hd * P:(hd + 1) * P],
                        minus_F[0:8, :], True, True)
            done = self.copy([m], F_rows[:, hd, :], bank.ap)
            bank.release(done)
            ready.append(done)
        ready.append(F_done)

        self.mixed_marks = []
        w = self.columns(w_in, 3 * QW + HEADS)
        pool_lane = self.lane("pool_w_in")
        pool_w = self.shaped(self.rms_tmp.rearrange("p a b -> p (a b)")[:, 0:4 * P], (4, P))
        pool_in = pool_lane.copy("scalar", [h], pool_w, d["pool_w"].rearrange("g c d -> c g d"))
        u_bufs = [self.area(T) for _ in range(3)]
        u_free = []
        counts = self.c("pool_count").rearrange("p (g n) -> p g n", g=4)
        for g, window in enumerate(POOL_WINDOWS):
            bank, m = self.project(h, w.view, w.landed, hT, slice(g * P, (g + 1) * P))
            u, s, s2 = u_bufs
            m = self.copy([m, u_free], u, bank.ap, "scalar")
            bank.release(m)
            u_done = m
            src, reach = u, 1
            while reach < window:
                dst = s2 if src is s else s
                m1 = self.tt([m], dst[:, reach:], src[:, reach:], src[:, :T - reach], ALU.add)
                m2 = self.copy([m], dst[:, 0:reach], src[:, 0:reach], "vector")
                m, src, reach = [m1, m2], dst, 2 * reach
            other = s2 if src is s else s
            m = [self.stt([m, u_done], other, src, 1.0 / window, u, ALU.mult, ALU.subtract)]
            m = self.tt([m], other[:, 0:16], src[:, 0:16], counts[:, g, :], ALU.mult)
            m = self.tt([m], other[:, 0:16], other[:, 0:16], u[:, 0:16], ALU.subtract)
            bank = self.banks.take()
            mp = self.mm([m, pool_in, bank.free], bank.ap, pool_w[:, g, :], other, True, True)
            m = self.act([mp], mixed[:, 4 + g, :], bank.ap, ACT.Copy, scale=self.v("pool_scale", g))
            bank.release(m)
            self.mixed_marks.append(m)
            u_free = [mp]
        w.release(q.last("tensor"))

        def logits(i, hd, bank, m, p):
            n = (i + 1) * P
            m = self.stt([m, ready, p.free], p.ap[:, 0:n], bank.ap[:, 0:n], F[:, i, hd:hd + 1],
                         F_rows[:, hd, 0:n], ALU.add, ALU.add)
            bank.release(m)
            return self.tt([m], p.ap[:, i * P:n], p.ap[:, i * P:n], self.c("causal"), ALU.add)

        self.attend(qT, kT, v, lambda i: (i + 1) * P, logits,
                    lambda i, b, m: self.turn_row(b, m, mixed, 0, i), ready,
                    Rotation([self.area(QW) for _ in range(2)]))

        self.mod_b_done = self.modulation_sum(2)
        self.residual_add(d["w_out"], mixed, self.mod[:, 2 * DC:3 * DC])

    def softplus_part(self, after, out, y):
        m = self.act(after, out, y, ACT.Abs)
        m = self.act([m], out, out, ACT.Exp, scale=-1.0)
        return self.act([m], out, out, ACT.Ln, bias=self.c("ones")[:, 0:1])

    def residual_add(self, weight, mixed, gate=None):
        self.x_done = []
        for s in range(2):
            w = self.columns(weight, s * 512)
            for j in range(4):
                k = s * 4 + j
                bank, m = self.project(self.mixed_marks, w.view, w.landed, mixed, slice(j * P, (j + 1) * P))
                x = self.xT3[:, k, :]
                if gate is None:
                    m = self.tt([m], x, bank.ap, x, ALU.add)
                else:
                    m = self.stt([m, self.mod_b_done], x, bank.ap, gate[:, k:k + 1], x, ALU.mult, ALU.add)
                bank.release(m)
                self.x_done.append(m)
            w.release(self.q.last("tensor"))

    def block1_mlp(self):
        d, q = self.dram, self.q
        q.stage()
        self.work_at = 0
        hT = self.area(DC, T)
        self.rms_tmp = self.area(4, T)
        gain, gain_done = self.gain_of(self.mod_b_done, 4 * DC, "norm2_g")
        h = self.rms(self.x_done + [gain_done], hT, gain, self.mod[:, 3 * DC:4 * DC])
        hidden = self.area(FC, T)
        convs = Rotation([self.area(T) for _ in range(4)])
        up = d["ffn_up"].rearrange("(k p) n -> p k n", p=P)
        hidden_marks = []
        for s in range(FC // 2):
            n = 2 * P
            w = self.slab((0, (DC, n), up[:, :, s * n:(s + 1) * n]),
                          (DC * n, (DC, n), up[:, :, FF + s * n:FF + (s + 1) * n]))
            views = [self.shaped(w.ap[:, i * DC * n:(i + 1) * DC * n], (DC, n)) for i in range(2)]
            for j in range(2):
                pair = []
                for side in range(2):
                    ch = side * FC + 2 * s + j
                    bank, m = self.project(h, views[side], w.landed, hT, slice(j * P, (j + 1) * P))
                    c = convs.take()
                    tap = [self.v("conv_w", t * 2 * FC + ch) for t in range(3)]
                    m = self.act([m, c.free], c.ap, bank.ap, ACT.Identity, bias=self.v("conv_b", ch), scale=tap[2])
                    m = self.stt([m], c.ap[:, 1:], bank.ap[:, 0:T - 1], tap[1], c.ap[:, 1:], ALU.mult, ALU.add)
                    m = self.stt([m], c.ap[:, 2:], bank.ap[:, 0:T - 2], tap[0], c.ap[:, 2:], ALU.mult, ALU.add)
                    bank.release(m)
                    pair.append((c, m))
                (cg, mg), (cv, mv) = pair
                mg = self.act([mg], cg.ap, cg.ap, ACT.Silu)
                m = self.tt([mg, mv], hidden[:, 2 * s + j, :], cg.ap, cv.ap, ALU.mult, "gpsimd")
                cg.release(m)
                cv.release(m)
                hidden_marks.append(m)
            w.release(q.last("tensor"))
        down = d["ffn_down"].rearrange("(k p) n -> p k n", p=P)
        self.x_done = []
        for k in range(DC):
            w = self.slab((0, (FC, P), down[:, :, k * P:(k + 1) * P]))
            view = self.shaped(w.ap[:, 0:FC * P], (FC, P))
            bank, m = self.project(hidden_marks, view, w.landed, hidden, slice(0, P))
            w.release(m)
            x = self.xT3[:, k, :]
            m = self.stt([m], x, bank.ap, self.mod[:, 5 * DC + k:5 * DC + k + 1], x, ALU.mult, ALU.add)
            bank.release(m)
            self.x_done.append(m)
        self.x_done = self.rms(self.x_done, self.xT3, self.v("final_g", 0, DC))

    def head_norm(self, after, out, src, ones, n, gain, scale=None, eps_inside=True):
        t = self.norm_tmp.take()
        m = self.act([after, t.free], t.ap[:, 0, :], src, ACT.Square)
        bank = self.banks.take()
        m = self.mm([m, bank.free], bank.ap, ones, t.ap[:, 0, :], True, True)
        m = self.act([m], t.ap[:, 1, :], bank.ap, ACT.Sqrt, bias=self.c("eps"), scale=1.0 / n)
        bank.release(m)
        m = self.recip([m], t.ap[:, 1, :], t.ap[:, 1, :])
        m = self.stt([m], out, src, gain, t.ap[:, 1, :], ALU.mult, ALU.mult)
        t.release(m)
        return m

    def block2_attention(self):
        d, q = self.dram, self.q
        entry = q.stage()
        self.work_at = 0
        self.hT2 = hT = self.area(DC, T)
        self.mixed2 = mixed = self.area(DC, T)
        self.rms_tmp = self.area(4, T)
        h = self.h2 = self.rms(self.x_done, hT, self.v("ln1_g", 0, DC))
        qT, kT, v = self.area(4, T), self.area(4, T), self.area(TT, QW)
        self.norm_tmp = Rotation([self.area(2, T) for _ in range(2)])
        raws = Rotation([self.area(T) for _ in range(2)])
        w_in = d["w_in_2"]
        ready = []
        q_gain = self.tiny(1)
        gain_done = self.ts([self.vec_done], q_gain, self.v("q_gain"), DH ** -0.5, ALU.mult)
        for first, out, gain in ((0, qT, q_gain), (QW, kT, self.v("k_gain"))):
            w = self.columns(w_in, first)
            for j in range(4):
                bank, m = self.project(h, w.view, w.landed, hT, slice(j * P, (j + 1) * P))
                raw = raws.take()
                c = self.copy([m, raw.free], raw.ap, bank.ap)
                bank.release(c)
                done = self.head_norm([c, gain_done], out[:, j, :], raw.ap, self.c("ones64"), DH, gain)
                raw.release(done)
                ready.append(done)
            w.release(m)
        w = self.columns(w_in, 2 * QW)
        for i in range(TT):
            bank = self.banks.take()
            for k in range(DC):
                m = self.mm([bank.free, w.landed, h], bank.ap, hT[:, k, i * P:(i + 1) * P], w.view[:, k, :],
                            k == 0, k == DC - 1)
            done = self.copy([m], v[:, i, :], bank.ap)
            bank.release(done)
            ready.append(done)
        w.release(m)

        n_m = 2 * WIN_H - 2
        lane = self.lane("rpb_in")
        table = [self.area(n_m, GRID) for _ in range(HEADS)]
        table_done = []
        rpb = d["rpb"]
        for hd in range(HEADS):
            for r2 in range(2):
                in_ = rpb[hd, 1 - r2:1 - r2 + n_m, :]
                source = bass.AP(in_.tensor, in_.offset, [[1, GRID], [2 * GRID - 1, n_m], [1, GRID]])
                landed = lane.copy("gpsimd", entry, table[hd][r2 * GRID:(r2 + 1) * GRID, :, :],
                                   source)
        for hd in range(HEADS):
            table_done.append(self.tt([landed], table[hd], table[hd],
                                      self.c("window").unsqueeze(1).to_broadcast([P, n_m, GRID]), ALU.add, "gpsimd"))

        def logits(i, hd, bank, m, p):
            at = table[hd][:, 6 - 2 * i:6 - 2 * i + ROWS, :]
            forwards = bass.AP(at.tensor, at.offset + GRID - 1, [list(at.ap[0]), [GRID, ROWS], [-1, GRID]])
            by_row = lambda ap: ap.rearrange("p (r c) -> p r c", r=ROWS)
            m = self.tt([m, table_done[hd], p.free], by_row(p.ap), by_row(bank.ap), forwards, ALU.add)
            bank.release(m)
            return m

        square, stats = self.rms_tmp[:, 0, :], self.tiny(TT, 3)
        self.mixed_marks = []
        last = []

        def out_row(i, b, m):
            m = self.act([m] + last, square, b.ap, ACT.Square, accum=stats[:, i, 0:1])
            last[:] = [m]
            m = self.act([m], stats[:, i, 1:2], stats[:, i, 0:1], ACT.Sqrt, bias=self.c("eps"), scale=1.0 / QW)
            m = self.recip([m], stats[:, i, 2:3], stats[:, i, 1:2])
            m = self.stt([m], b.ap, b.ap, stats[:, i, 2:3], self.r("attn_out_g"), ALU.mult, ALU.mult)
            self.turn_row(b, m, mixed, 0, i)

        self.attend(qT, kT, v, lambda i: T, logits, out_row, ready, raws)

    def deltanet(self):
        d, q = self.dram, self.q
        q.stage()
        hT, mixed, h = self.hT2, self.mixed2, self.h2
        self.work_at = 2 * DC * T
        qkvT = self.area(12, T)
        z = self.area(TT, QW)
        self.norm_tmp = Rotation([self.area(2, T) for _ in range(2)])
        convs = Rotation([self.area(T) for _ in range(3)])
        w_in = d["w_in_2"]
        base = 3 * QW
        done = []
        for s in range(3):
            w = self.columns(w_in, base + s * 512)
            for j in range(4):
                ch = s * 4 + j
                bank, m = self.project(h, w.view, w.landed, hT, slice(j * P, (j + 1) * P))
                c = convs.take()
                tap = [self.v("dn_conv_w", t * 12 + ch) for t in range(DN_TAPS)]
                m = self.act([m, c.free], c.ap, bank.ap, ACT.Copy, scale=tap[2])
                for t in (0, 1, 3, 4):
                    s_ = t - DN_TAPS // 2
                    to = slice(max(0, -s_), T - max(0, s_))
                    of = slice(max(0, s_), T - max(0, -s_))
                    m = self.stt([m], c.ap[:, to], bank.ap[:, of], tap[t], c.ap[:, to], ALU.mult, ALU.add)
                bank.release(m)
                m = self.act([m], qkvT[:, ch, :], c.ap, ACT.Silu)
                c.release(m)
                done.append(m)
            w.release(q.last("tensor"))
        for ch in range(8):
            done[ch] = self.head_norm(done[ch], qkvT[:, ch, :], qkvT[:, ch, :], self.c("ones"), 1.0,
                                      float(P) ** -0.5 if ch < 4 else 1.0)
        w = self.columns(w_in, base + 3 * 512)
        z_done = []
        for i in range(TT):
            bank = self.banks.take()
            for k in range(DC):
                m = self.mm([bank.free, w.landed, h], bank.ap, hT[:, k, i * P:(i + 1) * P], w.view[:, k, :],
                            k == 0, k == DC - 1)
            z_done.append(self.act([m], z[:, i, :], bank.ap, ACT.Silu))
            bank.release(z_done[-1])
        w.release(m)
        lane = self.lane("gates_in")
        wg = self.tiny(DC, 16)
        gates_in = lane.copy("scalar", [], wg, w_in.rearrange("(k p) n -> p k n", p=P)[:, :, base + 4 * 512:base + 4 * 512 + 16])
        tmp = convs.take()
        bank, ab, m = self.narrow([h, tmp.free], wg, gates_in, 16, hT, tmp.ap)
        tmp.release(m)
        y, a, g, beta = (self.tiny(TT, 8) for _ in range(4))
        rate = self.tiny(8)
        m1 = self.tt([m], y, ab[:, :, 0:8], self.r("dt_bias").unsqueeze(1).to_broadcast([P, TT, 8]), ALU.add)
        m2 = self.act([m1], beta, ab[:, :, 8:16], ACT.Exp, scale=-1.0)
        bank.release(m1, m2)
        m2 = self.ts([m2], beta, beta, 1.0, ALU.add)
        beta_done = self.recip([m2], beta, beta)
        m = self.softplus_part([m1], a, y)
        m = self.stt([m], a, y, 0.0, a, ALU.max, ALU.add)
        r = self.act([], rate, self.r("a_log"), ACT.Exp)
        m = self.stt([m, r], g, a, -1.0, rate.unsqueeze(1).to_broadcast([P, TT, 8]), ALU.mult, ALU.mult)
        g_done = m
        cum, whole = self.tiny(2, TT, 4), self.tiny(2, TT, 4)
        bank = self.banks.take()
        for dr in range(2):
            gd = g[:, :, dr * 4:dr * 4 + 4]
            self.mm([bank.free, g_done], bank.ap[:, dr * 16:dr * 16 + 16], self.c(f"cum{dr}"), gd, True, True)
            m = self.mm([], bank.ap[:, 32 + dr * 16:48 + dr * 16], self.c("ones64"), gd, True, True)
        m1 = self.copy([m], cum.rearrange("p a b c -> p (a b c)"), bank.ap[:, 0:32], "vector")
        m2 = self.copy([m], whole.rearrange("p a b c -> p (a b c)"), bank.ap[:, 32:64], "vector")
        bank.release(m2)
        k_scale, w_scale = self.tiny(2, TT, 4), self.tiny(2, TT, 4)
        m = self.tt([m1, m2], k_scale, whole, cum, ALU.subtract)
        k_scale_done = self.act([m], k_scale, k_scale, ACT.Exp)
        m = self.act([m1], w_scale, cum, ACT.Exp)
        for dr in range(2):
            m = self.tt([m, beta_done], w_scale[:, dr], w_scale[:, dr], beta[:, :, dr * 4:dr * 4 + 4], ALU.mult)
        scales = [k_scale_done, m, beta_done, m1]

        free_h = [q.last("tensor")]
        k_tok = hT[:, 0:4, :]
        v_tok = hT[:, 4:8, :]
        tok_done = {}
        for i in range(TT):
            for dst, off in ((k_tok, 4), (v_tok, 8)):
                bank = self.banks.take()
                for hd in range(4):
                    m = self.turn([bank.free, done[off + hd]], bank.ap[:, hd * P:(hd + 1) * P],
                                  qkvT[:, off + hd, i * P:(i + 1) * P], signal=hd == 3)
                m = self.copy([m, free_h], dst[:, i, :], bank.ap)
                bank.release(m)
                tok_done[off, i] = m

        turned = [q.last("tensor"), q.last("scalar"), q.last("vector")]
        self.work_at = 2 * DC * T + 12 * T + TT * QW
        o_acc = self.area(TT, QW)
        states = [self.area(4, P) for _ in range(2)]
        bufs = []
        while self.work_at + 512 <= self.WORK:
            bufs.append(self.area(512))
        bufs += [qkvT[:, 8 + i, :] for i in range(4)] + [mixed[:, 4 + i, :] for i in range(3)]
        pool = Rotation(bufs)
        for b in pool.buffers:
            b.free = turned
        state_done = [[self.q.do("gpsimd", [turned], lambda e, s=s: e.memset(s, 0.0))] for s in states]
        o_done = {}
        heads = lambda ap: ap.rearrange("p (h d) -> p h d", h=4)
        spread = lambda col: col.unsqueeze(2).to_broadcast([P, 4, P])
        over_heads = lambda c: c.unsqueeze(1).to_broadcast([P, 4, P])

        def per_head(after, pairs, out=None, bank=None, rows=slice(0, P)):
            bank = self.banks.take()
            for hd in range(4):
                lhsT, rhs = pairs(hd)
                m = self.mm([after, bank.free], bank.ap[:, hd * P:(hd + 1) * P], lhsT, rhs, True, True)
            return bank, m

        def unit(dr, i):
            tile = slice(i * P, (i + 1) * P)
            col = lambda t: t[:, dr, i, :]
            by_head = lambda b: (lambda hd: b.ap[:, hd * P:(hd + 1) * P])
            tt, ts, stt, act = self.tt, self.ts, self.stt, self.act
            g_col = g[:, i, dr * 4:dr * 4 + 4]
            b_col = beta[:, i, dr * 4:dr * 4 + 4]
            bg = pool.take()
            m = tt([g_done, bg.free], heads(bg.ap), over_heads(self.c(f"cum{dr}")), spread(g_col), ALU.mult)
            bank = self.banks.take()
            m = self.mm([m, bank.free], bank.ap, self.c("ones"), bg.ap, True, True)
            bg.release(m)
            yield
            eg, decay = pool.take(), pool.take()
            eg_done = act([m, eg.free], eg.ap, bank.ap, ACT.Exp)
            m = tt([eg_done, decay.free], heads(decay.ap), heads(bank.ap), over_heads(self.c(f"bar{dr}")), ALU.add)
            bank.release(m, eg_done)
            for hd in range(4):
                s = slice(hd * P, (hd + 1) * P)
                m = act([m, scales], decay.ap[:, s], decay.ap[:, s], ACT.Exp, bias=cum[:, dr, i, hd:hd + 1], scale=-1.0)
            decay_done = m
            yield
            kT = lambda hd: qkvT[:, 4 + hd, tile]
            qT = lambda hd: qkvT[:, hd, tile]
            kk, m_kk = per_head(done, lambda hd: (kT(hd), kT(hd)))
            qk, m_qk = per_head(done, lambda hd: (qT(hd), kT(hd)))
            L, QK = pool.take(), pool.take()
            yield
            m = tt([decay_done, m_qk, QK.free], QK.ap, qk.ap, decay.ap, ALU.mult)
            qk.release(m)
            qk_done = m
            for hd in range(4):
                s = slice(hd * P, (hd + 1) * P)
                m = stt([qk_done, scales], decay.ap[:, s], decay.ap[:, s], b_col[:, hd:hd + 1], self.c(f"strict{dr}"),
                        ALU.mult, ALU.mult)
            L_done = tt([m, m_kk, L.free], L.ap, kk.ap, decay.ap, ALU.mult)
            kk.release(L_done)
            decay.release(L_done)
            yield
            LT, QKT = pool.take(), pool.take()
            out = []
            for src, dst, ready in ((L, LT, L_done), (QK, QKT, qk_done)):
                bank = self.banks.take()
                for hd in range(4):
                    m = self.turn([ready, bank.free], bank.ap[:, hd * P:(hd + 1) * P], src.ap[:, hd * P:(hd + 1) * P],
                                  signal=hd == 3)
                if src is QK:
                    QK.release(m)
                m = self.copy([m, dst.free], dst.ap, bank.ap, "scalar")
                bank.release(m)
                out.append(m)
            LT_done, QKT_done = out
            qe, kd, vb, kb = (pool.take() for _ in range(4))
            qe_done = tt([eg_done, qe.free, done], heads(qe.ap), qkvT[:, 0:4, tile], heads(eg.ap), ALU.mult, "gpsimd")
            kd_done = tt([scales, kd.free, tok_done[4, i]], heads(kd.ap), heads(k_tok[:, i, :]), spread(col(k_scale)), ALU.mult, "gpsimd")
            vb_done = tt([scales, vb.free, tok_done[8, i]], heads(vb.ap), heads(v_tok[:, i, :]), spread(b_col), ALU.mult, "gpsimd")
            kb_done = tt([scales, kb.free, tok_done[4, i]], heads(kb.ap), heads(k_tok[:, i, :]), spread(col(w_scale)), ALU.mult, "gpsimd")
            yield
            N, NT, XT = (pool.take() for _ in range(3))
            in16, eye = over_heads(self.c("in16")), over_heads(self.c("ident"))
            mN = tt([L_done, N.free], heads(N.ap), heads(L.ap), in16, ALU.mult)
            mNT = tt([LT_done, NT.free], heads(NT.ap), heads(LT.ap), in16, ALU.mult)
            L.release(mN, LT_done)
            mXT = tt([mNT, XT.free], heads(XT.ap), eye, heads(NT.ap), ALU.subtract)
            power, powerT, mp, mpT = N, NT, mN, mNT
            for level in range(3):
                yield
                b1, m1 = per_head([mp, mpT], lambda hd: (by_head(powerT)(hd), by_head(power)(hd)))
                nxt = pool.take()
                n1 = self.copy([m1, nxt.free], nxt.ap, b1.ap, "vector")
                b1.release(n1)
                nxtT, n2 = None, None
                if level < 2:
                    b2, m1 = per_head([], lambda hd: (by_head(power)(hd), by_head(powerT)(hd)))
                    nxtT = pool.take()
                    n2 = self.copy([m1, nxtT.free], nxtT.ap, b2.ap, "scalar")
                    b2.release(n2)
                power.release(m1)
                powerT.release(m1, mXT)
                power, powerT, mp, mpT = nxt, nxtT, n1, n2
                yield
                bT, m2 = per_head([mp, mXT], lambda hd: (by_head(power)(hd), by_head(XT)(hd)))
                mXT = tt([m2], XT.ap, bT.ap, XT.ap, ALU.add)
                bT.release(mXT)
            power.release(m2)
            for join in ("join32", "join64"):
                yield
                X, J, W = pool.take(), pool.take(), pool.take()
                mJ = tt([LT_done, J.free], heads(J.ap), heads(LT.ap), over_heads(self.c(join)), ALU.mult, "gpsimd")
                bank = self.banks.take()
                for hd in range(4):
                    m = self.turn([mXT, bank.free], bank.ap[:, hd * P:(hd + 1) * P], by_head(XT)(hd), signal=hd == 3)
                mX = self.copy([m, X.free], X.ap, bank.ap, "scalar")
                bank.release(mX)
                yield
                b1, m1 = per_head([mJ, mX], lambda hd: (by_head(J)(hd), by_head(X)(hd)))
                J.release(m1)
                X.release(m1)
                mW = self.copy([m1, W.free], W.ap, b1.ap, "scalar")
                b1.release(mW)
                yield
                bT, m2 = per_head([mW], lambda hd: (by_head(W)(hd), by_head(XT)(hd)))
                mXT = tt([m2], XT.ap, XT.ap, bT.ap, ALU.subtract)
                bT.release(mXT)
                W.release(m2)
            LT.release(mJ, mNT)
            yield
            U, WT = pool.take(), pool.take()
            b1, m1 = per_head([mXT, vb_done], lambda hd: (by_head(XT)(hd), by_head(vb)(hd)))
            b2, m2 = per_head([kb_done], lambda hd: (by_head(kb)(hd), by_head(XT)(hd)))
            U_done = self.copy([m1, U.free], U.ap, b1.ap, "scalar")
            WT_done = self.copy([m2, WT.free], WT.ap, b2.ap, "vector")
            b1.release(U_done)
            b2.release(WT_done)
            XT.release(m2)
            vb.release(m2)
            kb.release(m2)
            yield
            S = states[dr]
            new = pool.take()
            o_bank = self.banks.take()
            for half in ((0, 1) if dr == 0 else (1, 0)):
                rows = slice(half * CHUNK, (half + 1) * CHUNK)
                end = half * CHUNK + (CHUNK - 1 if dr == 0 else 0)
                bank = self.banks.take()
                for hd in range(4):
                    lhs = WT.ap[:, hd * P + half * CHUNK:hd * P + (half + 1) * CHUNK]
                    m = self.mm([state_done[dr], WT_done, bank.free], bank.ap[rows, hd * P:(hd + 1) * P], lhs, S[:, hd, :], True, True)
                m_new = self.tt([m, U_done, new.free], new.ap[rows, :], U.ap[rows, :], bank.ap[rows, :], ALU.subtract)
                bank.release(m_new)
                yield
                for hd in range(4):
                    c = slice(hd * P + half * CHUNK, hd * P + (half + 1) * CHUNK)
                    out = o_bank.ap[rows, hd * P:(hd + 1) * P]
                    self.mm([qe_done, o_bank.free, QKT_done, m_new], out, qe.ap[:, c], S[:, hd, :], True, False)
                    m_o = self.mm([], out, QKT.ap[rows, c], new.ap[rows, hd * P:(hd + 1) * P], False, True)
                bank = self.banks.take()
                for hd in range(4):
                    m = self.mm([kd_done, bank.free], bank.ap[:, hd * P:(hd + 1) * P], kd.ap[rows, hd * P:(hd + 1) * P],
                                new.ap[rows, hd * P:(hd + 1) * P], True, True)
                ms = self.tt([m_o, eg_done, state_done[dr]], S, S, heads(eg.ap)[:, :, end:end + 1].to_broadcast([P, 4, P]), ALU.mult, "vector")
                ms = self.tt([ms, m], S, S, heads(bank.ap), ALU.add)
                bank.release(ms)
                state_done[dr] = [ms]
                yield
            for b in (WT, new, qe, QKT, kd):
                b.release(m)
            U.release(m_new)
            eg.release(ms, qe_done)
            first = i not in o_done
            if first:
                mo = self.copy([m_o], o_acc[:, i, :], o_bank.ap, "vector")
            else:
                mo = self.tt([m_o, o_done[i]], o_acc[:, i, :], o_acc[:, i, :], o_bank.ap, ALU.add)
            o_bank.release(mo)
            o_done[i] = mo

        for step in range(TT):
            running = [unit(0, step), unit(1, TT - 1 - step)]
            while running:
                for u in list(running):
                    try:
                        next(u)
                    except StopIteration:
                        running.remove(u)

        q.stage()
        sq = [pool.buffers[n].ap for n in range(2)]
        outs = Rotation([pool.buffers[n].ap for n in range(2, 4)])
        ss = self.tiny(TT, 4)
        for i in range(TT):
            m = self.act([], sq[i % 2], o_acc[:, i, :], ACT.Square) if i < 2 else \
                self.act([last_reduce[i - 2]], sq[i % 2], o_acc[:, i, :], ACT.Square)
            if i == 0:
                last_reduce = []
            m = self.reduce([m], ss[:, i, :], heads(sq[i % 2]), ALU.add)
            last_reduce.append(m)
        m = self.act([m], ss, ss, ACT.Sqrt, bias=self.c("eps"), scale=1.0 / P)
        inv = self.recip([m], ss, ss)
        for i in range(TT):
            b = outs.take()
            m = self.tt([inv, b.free], heads(b.ap), heads(o_acc[:, i, :]), spread(ss[:, i, :]), ALU.mult)
            m = self.tt([m], heads(b.ap), heads(b.ap), over_heads(self.r("dn_out_g")), ALU.mult)
            m = self.tt([m, z_done[i]], b.ap, b.ap, z[:, i, :], ALU.mult)
            self.turn_row(b, m, mixed, 4, i)
        self.residual_add(d["w_out_2"], mixed)

    def moe(self):
        d, q = self.dram, self.q
        entry = q.stage()
        self.work_at = 0
        x_tok = self.area(TT, D)
        in_slots = [self.ring[:, i * UP_W:(i + 1) * UP_W] for i in range(3)] + [self.area(UP_W)]
        down_slots = [self.area(DOWN_W) for _ in range(4)]
        hT = self.area(DC, T)
        self.rms_tmp = self.area(4, T)
        staging = Rotation([self.area(D) for _ in range(2)])
        h = self.rms(self.x_done, hT, self.v("ln2_g", 0, DC))

        def slots_of(aps, free, name):
            slots = Rotation(aps)
            for n, s in enumerate(slots.buffers):
                s.free, s.lane, s.over_lane = free[n], self.lane(f"{name}{n}_in"), self.lane(f"overflow_{name}{n}_in")
            return slots

        up_slots = slots_of(in_slots, [b.free for b in self.slabs.buffers] + [entry], "up")
        low_slots = slots_of(down_slots, [entry] * 4, "down")
        pieces = ((up_slots, 0, "w_gate"), (up_slots, DOWN_W, "w_up"), (low_slots, 0, "w_down"))

        def load_expert(e):
            w = up_slots.take(), low_slots.take()
            for slots, at, name in pieces:
                s = w[slots is low_slots]
                s.landed = s.lane.copy("sync", s.free, s.ap[:, at:at + DOWN_W], d[name][e * P:(e + 1) * P, :])
            return w

        def load_overflow(n, w_index, ready):
            w = up_slots.take(), low_slots.take()
            for slots, at, name in pieces:
                s = w[slots is low_slots]
                s.landed = s.over_lane.indirect([s.free, ready], out=s.ap[:, at:at + DOWN_W], out_offset=None,
                                                in_=d[name], in_offset=bass.IndirectOffsetOnAxis(ap=w_index[:, n:n + 1], axis=0),
                                                bounds_check=EXPERTS * P - 1, oob_is_err=False)
            return w

        router_lane = self.lane("router_in")
        wr = self.shaped(self.rms_tmp.rearrange("p a b -> p (a b)")[:, 0:DC * 72], (DC, 72))
        router_in = router_lane.copy("scalar", [h], wr, d["router_w"].rearrange("(k p) n -> p k n", p=P))
        tmp = staging.take()
        bank, logits, m = self.narrow(h, wr, router_in, 72, hT, tmp.ap[:, 0:T])
        tmp.release(m)
        lg = self.shaped(self.rms_tmp.rearrange("p a b -> p (a b)")[:, 640:640 + 288], (TT, 72))
        m = self.tt([m], lg, logits,
                    self.r("router_b").unsqueeze(1).to_broadcast([P, TT, 72]), ALU.add)
        bank.release(m)
        lg_done = m

        h_rows = self.nc.dram_tensor("h_rows", [PICKS, D], F32, kind="Internal").ap()
        y_rows = self.nc.dram_tensor("y_rows", [PICKS, D], F32, kind="Internal").ap()
        rows_lane = [self.lane(f"h_rows_out{i}") for i in range(2)]
        rows_out = []
        x_rows = []
        for i in range(TT):
            b = staging.take()
            marks = []
            for half in range(2):
                bank = self.banks.take()
                for j in range(4):
                    m = self.turn([h, bank.free], bank.ap[:, j * P:(j + 1) * P],
                                  hT[:, half * 4 + j, i * P:(i + 1) * P], signal=j == 3)
                m = self.copy([m, b.free], b.ap[:, half * 512:(half + 1) * 512], bank.ap, "scalar")
                bank.release(m)
                marks.append(m)
            for c in range(TOP_K):
                out = rows_lane[i % 2].copy("scalar", marks[:2], h_rows[c * T + i * P:c * T + (i + 1) * P, :], b.ap)
            b.release(out)
            rows_out.append(out)

        R = self.tiny
        gmax, gsum, m1c, m2c = R(TT), R(TT), R(TT), R(TT)
        t8, oh_g, ing, oh1, oh2 = R(TT, 8), R(TT, 8), R(TT, 8), R(TT, 8), R(TT, 8)
        cm = R(TT)
        gates = R(TOP_K, TT)
        wide = lambda c, n=8: c.unsqueeze(2).to_broadcast([P, TT, n])
        rev = self.c("rev8").unsqueeze(1).to_broadcast([P, TT, 8])
        tt, ts, red = self.tt, self.ts, self.reduce

        def first_max(m, src, top, out):
            m = red([m], top, src, ALU.max)
            m = tt([m], t8, src, wide(top), ALU.is_equal)
            m = tt([m], t8, t8, rev, ALU.mult)
            m = red([m], cm, t8, ALU.max)
            return tt([m], out, t8, wide(cm), ALU.is_equal)

        m = first_max(lg_done, lg[:, :, 0:8], gmax, oh_g)
        m = tt([m], t8, lg[:, :, 0:8], wide(gmax), ALU.subtract)
        m = self.act([m], t8, t8, ACT.Exp)
        m = red([m], gsum, t8, ALU.add)
        m = self.recip([m], gsum, gsum)
        big = self.shaped(self.rms_tmp.rearrange("p a b -> p (a b)")[:, 1024:1024 + 256], (TT, 64))
        el = lg[:, :, 8:72].rearrange("p i (g e) -> p i g e", g=8)
        big4 = big.rearrange("p i (g e) -> p i g e", g=8)
        m = tt([m], big4, el, oh_g.unsqueeze(3).to_broadcast([P, TT, 8, 8]), ALU.mult)
        m = red([m], ing, big.rearrange("p i (g e) -> p i e g", g=8), ALU.add)
        m = first_max(m, ing, m1c, oh1)
        m = self.stt([m], ing, oh1, NEG, ing, ALU.mult, ALU.add)
        m = first_max(m, ing, m2c, oh2)
        m = tt([m], m2c, m2c, m1c, ALU.subtract)
        m = self.act([m], m2c, m2c, ACT.Exp)
        m = ts([m], m1c, m2c, 1.0, ALU.add)
        m = self.recip([m], m1c, m1c)
        m = tt([m], gates[:, 0, :], m1c, gsum, ALU.mult)
        m = tt([m], gates[:, 1, :], gates[:, 0, :], m2c, ALU.mult)
        gates_done = m
        rest = self.area(3 * 512 + 1024)
        A = self.shaped(rest[:, 0:512], (PICK_TILES, EXPERTS))
        prod = self.shaped(rest[:, 512:1024], (PICK_TILES, EXPERTS))
        A_main = self.shaped(rest[:, 1024:1536], (PICK_TILES, EXPERTS))
        who = self.shaped(rest[:, 1536:2560], (PICK_TILES, P))
        for c, oh in enumerate((oh1, oh2)):
            for i in range(TT):
                m = tt([m], A[:, c * TT + i, :].rearrange("p (g e) -> p g e", g=8),
                       oh_g[:, i, :].unsqueeze(2).to_broadcast([P, 8, 8]),
                       oh[:, i, :].unsqueeze(1).to_broadcast([P, 8, 8]), ALU.mult)
        A_done = m
        bank = self.banks.take()
        for n in range(PICK_TILES):
            for j in range(n + 1):
                m = self.mm([A_done, bank.free], bank.ap[:, n * 64:(n + 1) * 64],
                            self.c("before") if j == n else self.c("ones"), A[:, j, :], j == 0, j == n)
        bank2 = self.banks.take()
        for n in range(PICK_TILES):
            m_c = self.mm([bank2.free], bank2.ap[0:64, 0:1], A[:, n, :], self.c("ones")[:, 0:1], n == 0, n == PICK_TILES - 1)
        rank, blk, off, who_e, q_blk = (R(PICK_TILES) for _ in range(5))
        m = tt([m], prod, bank.ap.rearrange("p (n e) -> p n e", n=PICK_TILES), A, ALU.mult)
        bank.release(m)
        m = red([m], rank, prod, ALU.add)
        over = R(MORE + 1)
        counts = R(1)
        m_x = self.copy([m_c], counts[0:64, :], bank2.ap[0:64, 0:1], "vector")
        bank2.release(m_x)
        m_x = ts([m_x], over[0:64, 0:MORE], self.c("caps", 64), counts[0:64, 0:1], ALU.is_lt)
        m_x = red([m_x], over[0:64, MORE:MORE + 1], over[0:64, 0:MORE], ALU.add)
        m_x = ts([m_x], who[0:64, 0, :], self.c("ones", 64), over[0:64, MORE:MORE + 1], ALU.mult)
        bank = self.banks.take()
        m_x = self.mm([m_x, bank.free], bank.ap[:, 0:64], who[0:64, 0, :], self.c("before", 64)[:, 0:64], True, True)
        spread_e = lambda ap: ap.unsqueeze(1).to_broadcast([P, PICK_TILES, EXPERTS])
        m = tt([m, m_x], prod, A, spread_e(bank.ap[:, 0:64]), ALU.mult)
        bank.release(m)
        m = red([m], off, prod, ALU.add)
        m = tt([m], prod, A, spread_e(self.c("expert")), ALU.mult)
        m = red([m], who_e, prod, ALU.add)
        scr = R(PICK_TILES, OVER)
        m = tt([m], scr[:, :, 0:MORE], rank.unsqueeze(2).to_broadcast([P, PICK_TILES, MORE]),
               self.c("caps").unsqueeze(1).to_broadcast([P, PICK_TILES, MORE]), ALU.is_ge)
        m = red([m], blk, scr[:, :, 0:MORE], ALU.add)
        m = self.stt([m], rank, blk, -float(CAP), rank, ALU.mult, ALU.add)
        main = R(PICK_TILES)
        m = ts([m], main, blk, 0.0, ALU.is_equal)
        m = tt([m], A_main, A, main.unsqueeze(2).to_broadcast([P, PICK_TILES, EXPERTS]), ALU.mult)
        m = tt([m], q_blk, off, blk, ALU.add)
        m = self.stt([m], main, main, -1.0, self.c("ones")[:, 0:8], ALU.mult, ALU.add)
        m = tt([m], q_blk, q_blk, main, ALU.mult)
        m = ts([m], q_blk, q_blk, -1.0, ALU.add)
        m = tt([m], scr, q_blk.unsqueeze(2).to_broadcast([P, PICK_TILES, OVER]),
               self.c("block").unsqueeze(1).to_broadcast([P, PICK_TILES, OVER]), ALU.is_equal)
        for n in range(PICK_TILES):
            m = ts([m, m_x], who[:, n, :], self.c("slot"), rank[:, n:n + 1], ALU.is_equal,
                   self.c("pick")[:, n:n + 1], ALU.mult)
        bank = self.banks.take()
        for n in range(PICK_TILES):
            self.mm([m, bank.free], bank.ap[:, 0:EXPERTS], who[:, n, :], A_main[:, n, :], n == 0, n == PICK_TILES - 1)
        for n in range(PICK_TILES):
            m_t = self.mm([], bank.ap[:, 64:64 + OVER], who[:, n, :], scr[:, n, :], n == 0, n == PICK_TILES - 1)
        zero = R(PICK_TILES)
        m = ts([m], zero, rank, 0.0, ALU.is_equal)
        m = tt([m], zero, zero, who_e, ALU.mult)
        for n in range(PICK_TILES):
            m = ts([m, m_t], who[:, n, :], self.c("ones"), zero[:, n:n + 1], ALU.mult)
        bank_e = self.banks.take()
        for n in range(PICK_TILES):
            m_e = self.mm([m, bank_e.free], bank_e.ap[:, 0:OVER], who[:, n, :], scr[:, n, :], n == 0, n == PICK_TILES - 1)
        pairs = EXPERTS // 2 + OVER // 2
        val, none = R(pairs), R(pairs)
        for par in range(2):
            rows = slice(par * 64, par * 64 + 64)
            m = self.copy([m_t], val[rows, 0:32], bank.ap[rows, par:64:2], "vector")
            m = self.copy([m_t], val[rows, 32:40], bank.ap[rows, 64 + par:80:2], "vector")
        m = ts([m], none, val, 0.0, ALU.is_equal, FAR, ALU.mult)
        m = self.stt([m], val, val, -1.0, none, ALU.add, ALU.add)
        row_index = self.index[:, 0:pairs]
        m = self.copy([m], row_index, val, "vector")
        index_done = m
        v2, n2 = R(OVER), R(OVER)
        m = ts([m_e], n2, bank_e.ap[:, 0:OVER], 0.0, ALU.is_equal, FAR, ALU.mult)
        m = self.stt([m], v2, bank_e.ap[:, 0:OVER], float(P), n2, ALU.mult, ALU.add)
        bank.release(index_done)
        m = ts([m], v2, v2, self.c("part"), ALU.add)
        w_index = self.index[:, pairs:pairs + OVER]
        m = self.copy([m], w_index, v2, "vector")
        any_over = self.index[:, pairs + OVER:pairs + OVER + 1]
        w_index_done = m = self.copy([m], any_over, bank_e.ap[:, 0:1], "vector")
        bank_e.release(m)

        for i in range(TT):
            for half in range(2):
                bank = self.banks.take()
                for j in range(4):
                    m = self.turn([self.x_done, bank.free], bank.ap[:, j * P:(j + 1) * P],
                                  self.xT3[:, half * 4 + j, i * P:(i + 1) * P], signal=j == 3)
                x_rows.append(self.copy([m], x_tok[:, i, half * 512:(half + 1) * 512], bank.ap))
                bank.release(x_rows[-1])

        marks = q.stage()
        keep = self.work_at
        self.work_at = TT * D + UP_W + 4 * DOWN_W
        gathered = Rotation([self.area(D) for _ in range(3)])
        slot_T = Rotation([self.area(DC, P) for _ in range(2)])
        y_buf = Rotation([self.area(D) for _ in range(2)])
        hid = Rotation([self.area(4, DE) for _ in range(2)])
        y_lane = [self.lane(f"y_out{i}") for i in range(2)]
        g_lane = [self.lane(f"gather{i}") for i in range(3)]
        for n, b in enumerate(gathered.buffers):
            b.free = [q.do("gpsimd", [], lambda e, b=b: e.memset(b.ap, 0.0)), rows_out[-2], rows_out[-1]]
            b.lane = g_lane[n]
        for n, b in enumerate(y_buf.buffers):
            b.lane = y_lane[n]
        gather_of, turned_of, y_out = {}, {}, []

        def gather(pr):
            b = gathered.take()
            m = b.lane.indirect([b.free, index_done], out=b.ap, out_offset=None, in_=h_rows,
                                in_offset=bass.IndirectOffsetOnAxis(ap=row_index[:, pr:pr + 1], axis=0),
                                bounds_check=PICKS - 1, oob_is_err=False)
            gather_of[pr] = b, m

        def turn_slots(pr):
            b, landed = gather_of.pop(pr)
            s = slot_T.take()
            out = []
            for half in range(2):
                bank = self.banks.take()
                for j in range(4):
                    m = self.turn([landed, bank.free], bank.ap[:, j * P:(j + 1) * P],
                                  b.ap[:, half * 4 + j:D:DC], signal=j == 3)
                m = self.copy([m, s.free], s.ap[:, half * 4:half * 4 + 4, :], bank.ap.rearrange("p (a b) -> p a b", a=4),
                              "scalar" if half else "vector")
                bank.release(m)
                out.append(m)
            b.release(*out)
            turned_of[pr] = s, out

        def up(bank, s, ready, half, w):
            w = w[0]
            sides = w.ap[:, 0:2 * DC * DE].rearrange("p (s k n) -> p k s n", s=2, k=DC)
            for k in range(DC):
                m = self.mm([bank.free, w.landed, ready], bank.ap[half * CAP:(half + 1) * CAP, :],
                            s.ap[:, k, half * CAP:(half + 1) * CAP], sides[:, k], k == 0, k == DC - 1)
            w.release(m)
            return m

        def hidden_of(bank, m):
            b = hid.take()
            act, hT_ = b.ap.rearrange("p a b -> p (a b)")[:, 0:DE], b.ap.rearrange("p a b -> p (a b)")[:, DE:3 * DE]
            m = self.act([m, b.free], act, bank.ap[:, 0:DE], ACT.Silu)
            m = self.tt([m], act, act, bank.ap[:, DE:2 * DE], ALU.mult)
            bank.release(m)
            b.ready, b.turned = m, hT_
            return b

        def turn_hidden(b):
            bank = self.banks.take()
            act = b.ap.rearrange("p a b -> p (a b)")[:, 0:DE]
            for fc in range(2):
                m = self.turn([b.ready, bank.free], bank.ap[:, fc * P:(fc + 1) * P], act[:, fc:DE:2], signal=fc == 1)
            b.ready = self.copy([m], b.turned[:, 0:DE], bank.ap[:, 0:DE], "scalar")
            bank.release(b.ready)

        def down(banks, b, half, w):
            w = w[1]
            wd = self.shaped(w.ap, (2, D))
            for n in range(2):
                for fc in range(2):
                    m = self.mm([banks[0].free, banks[1].free, b.ready, w.landed], banks[n].ap[half * CAP:(half + 1) * CAP, :],
                                b.turned[:, fc * P + half * CAP:fc * P + (half + 1) * CAP],
                                wd[:, fc, n * 512:(n + 1) * 512], fc == 0, fc == 1)
            w.release(m)
            return m

        def finish(pr, b, weights):
            banks = [self.banks.take() for _ in range(2)]
            for half in range(2):
                m = down(banks, b, half, weights[half])
            b.release(m)
            y = y_buf.take()
            out = []
            for n in range(2):
                mc = self.copy([m, y.free], y.ap[:, n * 512:(n + 1) * 512], banks[n].ap, "scalar" if n else "vector")
                banks[n].release(mc)
                out.append(mc)
            done = y.lane.indirect(out, out=y_rows, out_offset=bass.IndirectOffsetOnAxis(ap=row_index[:, pr:pr + 1], axis=0),
                                   in_=y.ap, in_offset=None, bounds_check=PICKS - 1, oob_is_err=False)
            y.release(done)
            y_out.append(done)

        def run_pairs(first, last, load):
            for pr in (first, first + 1):
                gather(pr)
            turn_slots(first)
            pending = None
            for pr in range(first, last):
                if pr + 2 < last:
                    gather(pr + 2)
                s, ready = turned_of.pop(pr)
                weights = [load(2 * pr), load(2 * pr + 1)]
                bank = self.banks.take()
                up(bank, s, ready, 0, weights[0])
                if pending:
                    finish(*pending)
                if pr + 1 < last:
                    turn_slots(pr + 1)
                m = up(bank, s, ready, 1, weights[1])
                s.release(m)
                b = hidden_of(bank, m)
                pending = (pr, b, weights)
                turn_hidden(b)
            finish(*pending)

        main_pairs = EXPERTS // 2
        run_pairs(0, main_pairs, load_expert)
        q.stage()
        q.guard(any_over[0:1, :])
        for n, b in enumerate(y_buf.buffers):
            b.lane = self.lane(f"overflow_y_out{n}")
        for n, b in enumerate(gathered.buffers):
            b.lane = self.lane(f"overflow_gather{n}")
        main_out = y_out[-2:]
        run_pairs(main_pairs, main_pairs + OVER // 2, lambda n: load_overflow(n - EXPERTS, w_index, w_index_done))
        q.end_guard(self.nc, self.ctx, [b.free for b in y_buf.buffers])
        y_out = main_out

        q.wait("scalar", y_out)
        marks = q.stage()
        self.work_at = TT * D
        ys = [self.area(D) for _ in range(2 * TT)] if self.work_at + 2 * TT * D <= self.WORK else None
        lanes = [self.lane(f"y_in{i}") for i in range(TT)]
        out_lane = self.lane("out")
        for i in range(TT):
            for c in range(TOP_K):
                landed = lanes[i].copy("scalar", [marks], ys[2 * i + c], y_rows[c * T + i * P:c * T + (i + 1) * P, :])
            m = x_rows
            for c in range(TOP_K):
                m = [self.stt([landed, m, gates_done], x_tok[:, i, :], ys[2 * i + c], gates[:, c, i:i + 1], x_tok[:, i, :],
                              ALU.mult, ALU.add)]
            final = out_lane.copy("sync", m, d["out"][i * P:(i + 1) * P, :], x_tok[:, i, :])
        q.wait("sync", [final])


STAGES = ("block1_mixer", "block1_mlp", "block2_attention", "deltanet", "moe")


def build(nc, dram, stages=STAGES):
    with ExitStack() as ctx:
        k = Kernel(nc, ctx, dram)
        for s in stages:
            {"block1_mixer": k.block1_mixer, "block1_mlp": k.block1_mlp, "block2_attention": k.block2_attention,
             "deltanet": k.deltanet, "moe": k.moe}[s]()
        block = ctx.enter_context(nc.Block())
        k.q.play(block)
    return k


def pack(x):
    f = np.float32
    a = {k: np.asarray(v) for k, v in x.items()}
    flat = lambda n: a[n].reshape(-1)
    gain = lambda n: np.concatenate([flat(n), flat(n)])
    vec = np.concatenate([
        flat("mod_b"), flat("c"), flat("norm1_g"), flat("norm2_g"), flat("final_g"), flat("ln1_g_2"),
        flat("ln2_g_2"), flat("pool_scale"), flat("ffn_conv_b"), flat("ffn_conv_w"), flat("dn_conv_w_2"),
        gain("attn_q_norm_g_2"), gain("attn_k_norm_g_2")]).reshape(-1, P)
    vec = np.concatenate([vec, np.zeros((VEC_TILES * P - len(vec), P), f)])
    row = np.concatenate([
        flat("attn_out_norm_g_2"), flat("dn_out_norm_g_2"), flat("b_f"), flat("router_group_b_2"),
        flat("router_expert_b_2"), flat("dn_dt_bias_2"), flat("dn_a_log_2")])[None, :]
    rpb = a["attn_rpb_2"][0]
    side = GRID - WIN_W
    return {
        "x": a["x"][0], "mod_w": a["mod_w"][0], "w_in": a["w_in"][0], "w_out": a["w_out"][0],
        "ffn_up": a["ffn_up"][0], "ffn_down": a["ffn_down"][0], "pool_w": a["pool_w"][0],
        "w_in_2": a["w_in_2"][0], "w_out_2": a["w_out_2"][0],
        "router_w": np.concatenate([a["router_group_w_2"][0], a["router_expert_w_2"][0]], 1),
        "w_gate": a["expert_w_gate_2"].reshape(EXPERTS * P, DC * DE),
        "w_up": a["expert_w_up_2"].reshape(EXPERTS * P, DC * DE),
        "w_down": a["expert_w_down_2"].reshape(EXPERTS * P, 2 * D),
        "rpb": np.pad(rpb, ((0, 0), (0, 0), (side, side)))[:, :, ::-1],
        "channel_vectors": vec, "row_vectors": row,
        "constants": np.concatenate(list(constants().values()), 1),
    }


def kernel(**inputs):
    from concourse import bacc
    from concourse.bass_utils import run_bass_kernel_spmd

    arrays = {n: np.ascontiguousarray(v) for n, v in pack(inputs).items()}
    nc = bacc.Bacc("TRN2", target_bir_lowering=False, num_devices=1)
    dram = {n: nc.dram_tensor(f"{n}_dram", v.shape, mybir.dt.from_np(v.dtype), kind="ExternalInput").ap()
            for n, v in arrays.items()}
    dram["out"] = nc.dram_tensor("out_dram", (T, D), F32, kind="ExternalOutput").ap()
    build(nc, dram)
    r = run_bass_kernel_spmd(nc, [{f"{n}_dram": v for n, v in arrays.items()}], core_ids=[0])
    return r.results[0]["out_dram"].reshape(1, T, D)
```

```python
from contextlib import ExitStack

import numpy as np

import concourse.bass as bass
from concourse import mybir

ALU = mybir.AluOpType
ACT = mybir.ActivationFunctionType
AXIS_X = mybir.AxisListType.X
F32 = mybir.dt.float32
F32R = mybir.dt.float32r
U32 = mybir.dt.uint32

P = 128
D = 1024
DC = D // P
T = 512
TT = T // P
HEADS = 8
DH = 64
QW = HEADS * DH
POOL_WINDOWS = (2, 4, 8, 16)
FF = 2816
FC = FF // P
EPS = 1e-6
GRID = 64
ROWS = T // GRID
WIN_W = 16
WIN_H = 8
DN_HEADS = 4
DN_TAPS = 5
CHUNK = 64
GROUPS = 8
PER_GROUP = 8
EXPERTS = GROUPS * PER_GROUP
DE = 256
CAP = 64
TOP_K = 2
PICKS = TOP_K * T
PICK_TILES = PICKS // P
MORE = T // CAP - 1
OVER = 16
FAR = 1.0e6
NEG = -1.0e30

MOD_W = 2048
SLAB = 4096
SLABS = 3
DOWN_W = 2048
UP_W = 2 * DOWN_W

VEC = {}
_at = 0
for _name, _rows in (("mod_b", 48), ("c", DC), ("norm1_g", DC), ("norm2_g", DC), ("final_g", DC),
                     ("ln1_g", DC), ("ln2_g", DC), ("pool_scale", 4), ("conv_b", 2 * FC),
                     ("conv_w", 3 * 2 * FC), ("dn_conv_w", DN_TAPS * 12), ("q_gain", 1),
                     ("k_gain", 1)):
    VEC[_name] = (_at, _rows)
    _at += _rows
VEC_TILES = -(-_at // P)

ROW = {}
_at = 0
for _name, _cols in (("attn_out_g", QW), ("dn_out_g", P), ("b_f", HEADS), ("router_b", 72),
                     ("dt_bias", 8), ("a_log", 8)):
    ROW[_name] = (_at, _cols)
    _at += _cols
ROW_W = _at


def constants():
    i = np.arange(P)[:, None]
    j = np.arange(P)[None, :]
    same = i // CHUNK == j // CHUNK
    f = np.float32
    out = {
        "ident": (i == j).astype(f),
        "ones": np.ones((P, P), f),
        "ones64": same.astype(f),
        "upto": (i <= j).astype(f),
        "before": (i < j).astype(f),
        "causal": np.where(j <= i, 0, NEG).astype(f),
        "cum0": (same & (i <= j)).astype(f), "cum1": (same & (i >= j)).astype(f),
        "bar0": np.where(same & (j <= i), 0, -NEG).astype(f),
        "bar1": np.where(same & (j >= i), 0, -NEG).astype(f),
        "strict0": (same & (j < i)).astype(f), "strict1": (same & (j > i)).astype(f),
        "in16": (i // 16 == j // 16).astype(f),
        "join32": ((i // 32 == j // 32) & (i // 16 != j // 16)).astype(f),
        "join64": (same & (i // 32 != j // 32)).astype(f),
    }
    out["head_row"] = np.concatenate([np.repeat(i == h, P, 1) for h in range(HEADS)], 1).astype(f)
    t = np.arange(16)
    out["pool_count"] = np.tile(np.concatenate([1 / np.minimum(t + 1, w) for w in POOL_WINDOWS]), (P, 1)).astype(f)
    col, key = np.arange(P)[:, None] % GRID, np.arange(GRID)[None, :]
    first = np.clip(col - WIN_W // 2, 0, GRID - WIN_W)
    out["window"] = np.where((key >= first) & (key < first + WIN_W), 0, NEG).astype(f)[:, ::-1]
    out["rev8"] = np.tile(8 - np.arange(8), (P, 1)).astype(f)
    out["pick"] = (np.arange(PICK_TILES)[None, :] * P + i + 1).astype(f)
    out["slot"] = np.tile(np.arange(P) % CAP + 1, (P, 1)).astype(f)
    out["block"] = np.tile(np.arange(OVER), (P, 1)).astype(f)
    out["expert"] = np.tile(np.arange(EXPERTS) + 1, (P, 1)).astype(f)
    out["caps"] = np.tile((np.arange(MORE) + 1) * CAP, (P, 1)).astype(f)
    out["part"] = (i - P).astype(f)
    out["eps"] = np.full((P, 1), EPS, f)
    return out


CONST = {}
_at = 0
for _name, _table in constants().items():
    CONST[_name] = (_at, _table.shape[1])
    _at += _table.shape[1]
CONST_W = _at


class Queues:

    ENGINES = ("tensor", "vector", "scalar", "gpsimd", "sync")

    def __init__(self, nc, ctx):
        self.queue = {e: [] for e in self.ENGINES}
        self.done = {e: ctx.enter_context(nc.semaphore(f"{e}_done")) for e in self.ENGINES}
        self.count = dict.fromkeys(self.ENGINES, 0)
        self.waited = {e: {} for e in self.ENGINES}

    def wait(self, engine, marks):
        for mark in marks:
            if mark is None:
                continue
            if isinstance(mark, list):
                self.wait(engine, mark)
                continue
            sem, value = mark
            if self.waited[engine].get(sem.name, 0) < value:
                self.waited[engine][sem.name] = value
                self.queue[engine].append(lambda e, sem=sem, value=value: e.wait_ge(sem, value))

    def do(self, engine, after, instruction, signal=True):
        self.wait(engine, after)
        if not signal:
            self.queue[engine].append(instruction)
            return None
        sem = self.done[engine]
        self.count[engine] += 1
        self.queue[engine].append(lambda e: instruction(e).then_inc(sem, 1))
        return (sem, self.count[engine])

    def last(self, engine):
        return (self.done[engine], self.count[engine]) if self.count[engine] else None

    def stage(self):
        marks = [self.last(e) for e in ("tensor", "vector", "scalar", "gpsimd")]
        for e in ("tensor", "vector", "scalar", "gpsimd"):
            self.wait(e, marks)
        return marks

    def guard(self, value):
        self.before = {e: dict(w) for e, w in self.waited.items()}
        self.guards = {}
        for name in self.ENGINES[:4]:
            def begin(e, name=name):
                self.guards[name] = e.If(e.value_load(value) != 0)
                self.guards[name].__enter__()
            self.queue[name].append(begin)

    def end_guard(self, nc, ctx, marks):
        marks = marks + [self.last(e) for e in self.ENGINES[:4]]
        for name in self.ENGINES[:4]:
            self.wait(name, marks)
            self.queue[name].append(lambda e, name=name: self.guards[name].__exit__(None, None, None))
        self.waited = self.before
        for name in self.ENGINES[:4]:
            self.done[name] = ctx.enter_context(nc.semaphore(f"{name}_done_after"))
            self.count[name] = 1
            self.queue[name].append(lambda e, sem=self.done[name]: e.sem_inc(sem, 1))

    def play(self, block):
        for name in self.ENGINES:
            def run(engine, name=name):
                for step in self.queue[name]:
                    step(engine)
            {"tensor": block.tensor, "vector": block.vector, "scalar": block.scalar,
             "gpsimd": block.gpsimd, "sync": block.sync}[name](run)


class Buffer:

    def __init__(self, ap):
        self.ap, self.free, self.busy = ap, [], False

    def release(self, *marks):
        self.free, self.busy = list(marks), False


class Split:

    def __init__(self, hi, lo):
        self.hi, self.lo = hi, lo

    def __len__(self):
        return len(self.hi)


class PerChunk(list):

    @staticmethod
    def of(after, k):
        return after[k] if isinstance(after, PerChunk) else after


class Rotation:
    def __init__(self, aps):
        self.buffers, self.next = [Buffer(a) for a in aps], 0

    def take(self):
        for _ in self.buffers:
            b = self.buffers[self.next]
            self.next = (self.next + 1) % len(self.buffers)
            if not b.busy:
                b.busy = True
                return b
        raise ValueError("no buffer is free")


class Lane:

    def __init__(self, nc, ctx, q, name):
        self.q, self.sem, self.count = q, ctx.enter_context(nc.semaphore(name)), 0

    def copy(self, engine, after, out, in_):
        self.q.wait(engine, after)
        self.count += 16
        self.q.queue[engine].append(lambda e: e.dma_start(out, in_).then_inc(self.sem, 16))
        return (self.sem, self.count)

    def indirect(self, after, **how):
        self.q.wait("gpsimd", after)
        self.count += 16
        self.q.queue["gpsimd"].append(lambda e: e.indirect_dma_start(**how).then_inc(self.sem, 16))
        return (self.sem, self.count)


class Kernel:
    def __init__(self, nc, ctx, dram):
        self.nc, self.ctx, self.dram = nc, ctx, dram
        self.q = q = Queues(nc, ctx)

        def sbuf(name, cols, dtype=F32):
            return ctx.enter_context(nc.sbuf_tensor(name, [P, cols], dtype))

        self.const = sbuf("constants", CONST_W)
        self.vec = sbuf("channel_vectors", VEC_TILES * P)
        self.row = sbuf("row_vectors", ROW_W)
        self.small = sbuf("small", 1400)
        self.index = sbuf("indices", 64, U32)
        self.xT = sbuf("residual_T", DC * T)
        self.ring = sbuf("weight_ring", SLABS * SLAB)
        self.WORK = 30900
        with nc.sbuf_tensor("work", [P, self.WORK], F32) as self.work:
            pass
        self.roundeds = {}
        self.work_at = self.small_at = 0
        banks = [ctx.enter_context(nc.psum_tensor(f"bank{i}", [P, 512], F32)) for i in range(8)]
        self.banks = Rotation([b[:, :] for b in banks])
        self.slabs = Rotation([self.ring[:, i * SLAB:(i + 1) * SLAB] for i in range(SLABS)])
        self.slab_lanes = [Lane(nc, ctx, q, f"slab{i}_in") for i in range(SLABS)]
        self.lanes = 0
        self.flip = 0

    def lane(self, name):
        return Lane(self.nc, self.ctx, self.q, name)

    def area(self, *shape):
        n = int(np.prod(shape))
        ap = self.work[:, self.work_at:self.work_at + n]
        self.work_at += n
        assert self.work_at <= self.WORK, self.work_at
        return self.shaped(ap, shape)

    def rounded(self, n):
        at = self.work_at
        self.work_at += n
        assert self.work_at <= self.WORK, self.work_at
        if (at, n) not in self.roundeds:
            below = self.nc.sbuf_tensor(f"below_{at}_{n}", [P, at], F32) if at else ExitStack()
            with below:
                with self.nc.sbuf_tensor(f"rounded_{at}_{n}", [P, n], F32R) as self.roundeds[at, n]:
                    pass
        return self.roundeds[at, n][:, :]

    def area_split(self, chunks, n=T):
        halves = []
        for _ in range(2):
            halves.append(self.shaped(self.rounded(chunks * n), (chunks, n)))
        return Split([halves[0][:, k, :] for k in range(chunks)], [halves[1][:, k, :] for k in range(chunks)])

    def split_buffers(self, n):
        self.split_room = Rotation([(self.rounded(n), self.rounded(n)) for _ in range(3)])

    @staticmethod
    def shaped(ap, shape):
        if len(shape) == 2:
            return ap.rearrange("p (a b) -> p a b", a=shape[0])
        if len(shape) == 3:
            return ap.rearrange("p (a b c) -> p a b c", a=shape[0], b=shape[1])
        return ap

    def tiny(self, *shape):
        n = int(np.prod(shape))
        ap = self.small[:, self.small_at:self.small_at + n]
        self.small_at += n
        assert self.small_at <= 1400
        return self.shaped(ap, shape)

    def c(self, name, rows=P):
        at, n = CONST[name]
        return self.const[0:rows, at:at + n]

    def v(self, name, i=0, n=1):
        at = VEC[name][0] + i
        return self.vec[:, at:at + n]

    def r(self, name):
        at, n = ROW[name]
        return self.row[:, at:at + n]

    def mm(self, after, out, lhsT, rhs, start, stop, signal=None):
        signal = stop if signal is None else signal
        return self.q.do("tensor", after, lambda e: e.matmul(out, lhsT, rhs, start=start, stop=stop), signal)

    def turn(self, after, out, in_, signal=True):
        ident = self.c("ident")[0:in_.shape[0], 0:in_.shape[0]]
        return self.q.do("tensor", after, lambda e: e.transpose(out, in_, ident), signal)

    def act(self, after, out, in_, func, bias=0.0, scale=1.0, accum=None):
        more = {} if accum is None else {"accum_out": accum}
        if func == ACT.Copy:
            return self.q.do("scalar", after, lambda e: e.activation(out, in_, func, scale=scale, **more))
        return self.q.do("scalar", after,
                         lambda e: e.activation(out, in_, func, bias=bias, scale=scale, **more))

    def tt(self, after, out, a, b, op, engine="vector"):
        return self.q.do(engine, after, lambda e: e.tensor_tensor(out, a, b, op))

    def ts(self, after, out, a, s1, op0, s2=None, op1=None, engine="vector"):
        if op1 is None:
            return self.q.do(engine, after, lambda e: e.tensor_scalar(out, a, s1, None, op0))
        return self.q.do(engine, after, lambda e: e.tensor_scalar(out, a, s1, s2, op0, op1))

    def stt(self, after, out, a, s, b, op0, op1):
        return self.q.do("vector", after, lambda e: e.scalar_tensor_tensor(
            out=out, in0=a, scalar=s, in1=b, op0=op0, op1=op1))

    def reduce(self, after, out, in_, op, negate=False):
        return self.q.do("vector", after, lambda e: e.tensor_reduce(out, in_, AXIS_X, op, negate=negate))

    def copy(self, after, out, in_, engine=None):
        if engine is None:
            self.flip ^= 1
            engine = "vector" if self.flip else "scalar"
        if engine == "scalar":
            return self.act(after, out, in_, ACT.Copy)
        return self.q.do(engine, after, lambda e: e.tensor_copy(out, in_))

    def recip(self, after, out, in_):
        return self.q.do("vector", after, lambda e: e.reciprocal(out, in_))

    def slab(self, *parts):
        i = self.slabs.next
        b = self.slabs.take()
        for at, shape, source in parts:
            n = int(np.prod(shape))
            mark = self.slab_lanes[i].copy("sync", b.free, self.shaped(b.ap[:, at:at + n], shape), source)
        b.landed = mark
        return b

    def columns(self, weight, first, n=512):
        b = self.slab((0, (DC, n), weight.rearrange("(k p) n -> p k n", p=P)[:, :, first:first + n]))
        b.view = self.shaped(b.ap[:, 0:DC * n], (DC, n))
        return b

    def split_weights(self, view, landed):
        b = self.split_room.take()
        shape = tuple(view.shape[1:])
        n = int(np.prod(shape))
        hi, lo = (self.shaped(ap[:, 0:n], shape) for ap in b.ap)
        m1 = self.act([landed, b.free], hi, view, ACT.Copy)
        m2 = self.tt([m1], lo, view, hi.bitcast(F32), ALU.subtract)
        b.hi, b.lo, b.ready = hi, lo, m2
        return b

    def begin(self, pieces):
        return {n: self.split_piece(pieces[n]) for n in range(2)}

    def split_piece(self, piece):
        slab, view, last = piece[0:3]
        slab = slab()
        b = self.split_weights(view(slab), slab.landed)
        if last:
            slab.release(b.ready)
        return b

    def stream(self, pieces, splits=None, between=()):
        ahead = 2
        later = None
        between = list(between)
        splits = splits or {}
        for n in range(len(pieces) + ahead):
            if n < len(pieces) and (n >= ahead or n not in splits):
                splits[n] = self.split_piece(pieces[n])
            if n >= ahead:
                b = splits.pop(n - ahead)
                use, then = pieces[n - ahead][3:5]
                m = use(b)
                b.release(m)
                if later:
                    later()
                later = then(m) if then else None
                if between:
                    between.pop(0)()
        if later:
            later()

    def three_products(self, after, out, lhs, rhs, first, last, signal=None):
        self.mm(after, out, lhs[0], rhs[0], first, False)
        self.mm([], out, lhs[0], rhs[1], False, False)
        return self.mm([], out, lhs[1], rhs[0], False, last, last if signal is None else signal)

    def once(self, load):
        kept = []

        def get():
            if not kept:
                kept.append(load())
            return kept[0]
        return get

    def column_pieces(self, weight, first, src, after, finish, count=4):
        slab = self.once(lambda: self.columns(weight, first, count * P))
        out = []
        for j in range(count):
            def use(b, j=j):
                bank = self.banks.take()
                for k in range(len(src)):
                    m = self.three_products([bank.free, b.ready, PerChunk.of(after, k)], bank.ap, (b.hi[:, k, :], b.lo[:, k, :]),
                                            (src.hi[k], src.lo[k]), k == 0, k == len(src) - 1)
                self.bank_of_piece = bank
                return m
            out.append((slab, lambda s, j=j: s.view[:, :, j * P:(j + 1) * P], j == count - 1, use,
                        lambda m, j=j: finish(j, self.bank_of_piece, m)))
        return out

    def row_pieces(self, weight, first, src, after, finish):
        slab = self.once(lambda: self.columns(weight, first))
        banks = []
        out = []
        for c in range(DC // 2):
            def use(b, c=c):
                if c == 0:
                    banks.extend(self.banks.take() for _ in range(TT))
                for i in range(TT):
                    tile = slice(i * P, (i + 1) * P)
                    for kk in range(2):
                        k = 2 * c + kk
                        m = self.three_products([banks[i].free, b.ready, PerChunk.of(after, k)], banks[i].ap,
                                                (src.hi[k][:, tile], src.lo[k][:, tile]),
                                                (b.hi[:, kk, :], b.lo[:, kk, :]), k == 0, k == DC - 1,
                                                signal=i == TT - 1 and kk == 1)
                return m

            def then(m):
                for i in range(TT):
                    finish(i, banks[i], m)
            out.append((slab, lambda s, c=c: s.view[:, 2 * c:2 * c + 2, :], c == DC // 2 - 1, use,
                        then if c == DC // 2 - 1 else None))
        return out

    def split_result(self, hi, lo, bank, mark, scale=1.0, free=()):
        m = self.act([mark, list(free)], hi, bank.ap, ACT.Copy, scale=scale)
        m = self.stt([m], lo, bank.ap, scale, hi.bitcast(F32), ALU.mult, ALU.subtract)
        bank.release(m)
        return m

    def load_small(self):
        lane = self.lane("small_in")
        d = self.dram
        lane.copy("sync", [], self.const[:, :], d["constants"])
        stage = self.work[:, 0:VEC_TILES * P].rearrange("p (a b) -> p a b", b=P)
        lane.copy("sync", [], stage, d["channel_vectors"].rearrange("(a p) n -> p a n", p=P))
        self.small_in = lane.copy("sync", [], self.row[:, :],
                                  d["row_vectors"].to_broadcast([P, ROW_W]))
        bank = self.banks.take()
        for a in range(VEC_TILES):
            m = self.turn([self.small_in], bank.ap[:, a * P:(a + 1) * P], stage[:, a, :])
        self.vec_done = self.copy([m, self.small_in], self.vec[:, :], bank.ap[:, 0:VEC_TILES * P], "vector")
        bank.release(self.vec_done)

    def load_x(self):
        self.work_at = 4096
        lane = self.lane("x_in")
        x = self.area(TT, D)
        landed = lane.copy("sync", [], x, self.dram["x"].rearrange("(i p) d -> p i d", p=P))
        xT = self.shaped(self.xT[:, :], (DC, T))
        marks = []
        for k in range(DC):
            bank = self.banks.take()
            for i in range(TT):
                m = self.turn([landed, self.small_in, bank.free], bank.ap[:, i * P:(i + 1) * P],
                              x[:, i, k * P:(k + 1) * P], signal=i == TT - 1)
            marks.append(self.copy([m], xT[:, k, :], bank.ap))
            bank.release(marks[-1])
        self.xT3 = xT
        self.x_done = PerChunk(marks)

    def modulation_start(self):
        self.c_act = self.tiny(DC)
        self.c_done = self.act([self.vec_done], self.c_act, self.v("c", 0, DC), ACT.Silu)
        self.mod = self.tiny(48)

    def modulation(self, part, first, last):
        acc = self.mod_acc
        for s in range(first, last):
            w = self.slab((0, (2, MOD_W), self.dram["mod_w"].rearrange("(k p) n -> p k n", p=P)[
                :, 2 * s:2 * s + 2, part * MOD_W:(part + 1) * MOD_W]))
            view = self.shaped(w.ap, (2, MOD_W))
            for k in range(2):
                col = self.c_act[:, 2 * s + k:2 * s + k + 1]
                if s + k == 0:
                    m = self.ts([w.landed, self.c_done, self.mod_free], acc, view[:, 0, :], col, ALU.mult)
                else:
                    m = self.stt([w.landed, m if s + k > first else self.mod_last], acc, view[:, k, :], col, acc,
                                 ALU.mult, ALU.add)
            self.mod_last = m
            w.release(m)

    def modulation_sum(self, part):
        for g in range(4):
            bank = self.banks.take()
            for j in range(4):
                at = (4 * g + j) * P
                m = self.mm([self.mod_last, bank.free], bank.ap[:, j * P:(j + 1) * P], self.mod_acc[:, at:at + P],
                            self.c("ones"), True, True)
            col = part * 16 + g * 4
            done = self.tt([m, self.vec_done], self.mod[:, col:col + 4], bank.ap[:, 0:512:P],
                           self.v("mod_b", col, 4), ALU.add)
            bank.release(done)
        self.mod_free = m
        return done

    def narrow(self, after, weight, landed, n, src, tmp):
        bank = self.banks.take()
        if isinstance(src, Split):
            b = self.split_weights(weight, landed)
            for k in range(DC):
                m = self.three_products([bank.free, b.ready, PerChunk.of(after, k)], bank.ap[0:n, :], (b.hi[:, k, :], b.lo[:, k, :]),
                                        (src.hi[k], src.lo[k]), k == 0, k == DC - 1)
            b.release(m)
        else:
            for k in range(DC):
                m = self.mm([bank.free, landed, PerChunk.of(after, k)], bank.ap[0:n, :], weight[:, k, 0:n], src[:, k, :], k == 0, k == DC - 1)
        m = self.copy([m], tmp[0:n, :], bank.ap[0:n, :], "scalar")
        bank.release(m)
        bank = self.banks.take()
        for i in range(TT):
            m2 = self.turn([m, bank.free], bank.ap[:, i * n:(i + 1) * n], tmp[0:n, i * P:(i + 1) * P], signal=i == TT - 1)
        return bank, bank.ap[:, 0:TT * n].rearrange("p (i n) -> p i n", i=TT), m2

    def rms_start(self, after, meanwhile=None):
        squares = self.squares = Rotation([self.rms_tmp[:, i, :] for i in range(2)])
        bank = self.banks.take()
        for k in range(DC):
            s = squares.take()
            sq = self.act([PerChunk.of(after, k), s.free], s.ap, self.xT3[:, k, :], ACT.Square)
            m = self.mm([sq, bank.free, self.small_in], bank.ap, self.c("ones"), s.ap, k == 0, k == DC - 1, signal=True)
            s.release(m)
        self.begun = meanwhile() if meanwhile else None
        root = self.act([m, self.small_in], self.rms_tmp[:, 2, :], bank.ap, ACT.Sqrt, bias=self.c("eps"), scale=1.0 / D)
        bank.release(root)
        return self.recip([root], self.rms_tmp[:, 3, :], self.rms_tmp[:, 2, :])

    def rms_finish(self, inv, after, out, gain, shift=None, marks=None):
        marks = PerChunk() if marks is None else marks
        if isinstance(out, Split):
            ys = Rotation([self.rms_tmp[:, i, :] for i in range(3)])
            scaled = {}
            for k in range(DC + 1):
                if k < DC:
                    y = ys.take()
                    scaled[k] = y, self.stt([inv, after, y.free], y.ap, self.xT3[:, k, :], gain[:, k:k + 1],
                                            self.rms_tmp[:, 3, :], ALU.mult, ALU.mult)
                if k > 0:
                    (y, m), c = scaled.pop(k - 1), k - 1
                    if shift is None:
                        m = self.copy([m], out.hi[c], y.ap, "scalar")
                        m = self.tt([m], out.lo[c], y.ap, out.hi[c].bitcast(F32), ALU.subtract)
                    else:
                        m = self.act([m], out.hi[c], y.ap, ACT.Identity, bias=shift[:, c:c + 1])
                        m = self.stt([m], out.lo[c], y.ap, shift[:, c:c + 1], out.hi[c].bitcast(F32), ALU.add, ALU.subtract)
                    y.release(m)
                    marks.append(m)
            return marks
        for k in range(DC):
            marks.append(self.stt([inv, after], out[:, k, :], self.xT3[:, k, :], gain[:, k:k + 1],
                                  self.rms_tmp[:, 3, :], ALU.mult, ALU.mult))
        return marks

    def rms(self, after, out, gain, shift=None, more=(), pieces=None, marks=None):
        inv = self.rms_start(after, (lambda: self.begin(pieces)) if pieces else None)
        return self.rms_finish(inv, [after, list(more)], out, gain, shift, marks)

    def gain_of(self, after, scale_at, norm):
        g = self.tiny(DC)
        return g, self.stt([after], g, self.mod[:, scale_at:scale_at + DC], 1.0, self.v(norm, 0, DC), ALU.add, ALU.mult)

    def attend(self, qT, kT, v, width, logits, out_row, ready, outs):
        n_buf = 3
        probs = Rotation([self.area(T) for _ in range(n_buf)])
        turned = Rotation([self.area(T) for _ in range(n_buf)])
        neg_max = self.tiny(TT, HEADS)
        total = self.tiny(TT, HEADS)
        inverse = self.tiny(TT, HEADS)
        state = {}

        def scores(i, h):
            w = width(i)
            rows = slice(64 * (h % 2), 64 * (h % 2) + 64)
            bank = self.banks.take()
            m = self.mm([bank.free, ready], bank.ap[:, 0:w], qT[rows, h // 2, i * P:(i + 1) * P],
                        kT[rows, h // 2, 0:w], True, True)
            p = probs.take()
            m = logits(i, h, bank, m, p)
            m = self.reduce([m], neg_max[:, i, h:h + 1], p.ap[:, 0:w], ALU.max, negate=True)
            m = self.act([m], p.ap[:, 0:w], p.ap[:, 0:w], ACT.Exp, bias=neg_max[:, i, h:h + 1],
                         accum=total[:, i, h:h + 1])
            state[i, h] = [p, m]

        def transposed(i, h):
            w = width(i)
            p, m = state[i, h]
            bank = self.banks.take()
            t = turned.take()
            for j in range(w // P):
                mark = self.turn([m, bank.free], bank.ap[:, j * P:(j + 1) * P], p.ap[:, j * P:(j + 1) * P],
                                 signal=j == w // P - 1)
            p.release(mark)
            mark = self.copy([mark, t.free], t.ap[:, 0:w], bank.ap[:, 0:w])
            bank.release(mark)
            state[i, h] = [t, mark, m]

        def values(i, h):
            t, mark, exp = state.pop((i, h))
            if h == 0:
                state["o"] = self.banks.take()
            o = state["o"]
            for j in range(width(i) // P):
                for half in range(2):
                    m = self.mm([mark, ready, o.free], o.ap[half * DH:(half + 1) * DH, h * DH:(h + 1) * DH],
                                t.ap[:, j * P + half * DH:j * P + (half + 1) * DH],
                                v[:, j, h * DH:(h + 1) * DH], j == 0, j == width(i) // P - 1)
            t.release(m)
            if h == HEADS - 1:
                inv = self.recip([exp], inverse[:, i, :], total[:, i, :])
                b = outs.take()
                o3 = o.ap.rearrange("p (h d) -> p h d", h=HEADS)
                m = self.tt([m, inv, b.free], b.ap.rearrange("p (h d) -> p h d", h=HEADS), o3,
                            inverse[:, i, :].unsqueeze(2).to_broadcast([P, HEADS, DH]), ALU.mult)
                o.release(m)
                out_row(i, b, m)

        units = [(i, h) for i in range(TT) for h in range(HEADS)]
        for n in range(len(units) + 2):
            if n < len(units):
                scores(*units[n])
            if 1 <= n <= len(units):
                transposed(*units[n - 1])
            if n >= 2:
                values(*units[n - 2])

    def turn_row(self, b, mark, mixed, first, i):
        bank = self.banks.take()
        for j in range(4):
            m = self.turn([mark, bank.free], bank.ap[:, j * P:(j + 1) * P], b.ap[:, j * P:(j + 1) * P], signal=j == 3)
        b.release(m)
        tile = slice(i * P, (i + 1) * P)
        for j in range(4):
            r = self.act([m], mixed.hi[first + j][:, tile], bank.ap[:, j * P:(j + 1) * P], ACT.Copy)
        for j in range(4):
            r = self.tt([r], mixed.lo[first + j][:, tile], bank.ap[:, j * P:(j + 1) * P],
                        mixed.hi[first + j][:, tile].bitcast(F32), ALU.subtract)
        bank.release(r)
        self.mixed_marks.append(r)

    def block1_mixer(self):
        d, q = self.dram, self.q
        self.load_small()
        self.modulation_start()
        self.load_x()
        split_at, self.work_at = 0, 6 * DC * P
        hT_at = self.work_at
        hT = self.area_split(DC)
        self.rms_tmp = self.area(4, T)
        self.mod_acc, self.mod_free = self.area(MOD_W), None
        self.modulation(0, 0, 3)
        inv = self.rms_start(self.x_done)
        self.modulation(0, 3, 4)
        wf_lane = self.lane("wf_in")
        wf = self.tiny(DC, HEADS)
        wf_in = wf_lane.copy("scalar", [], wf, d["w_in"].rearrange("(k p) n -> p k n", p=P)[:, :, 3 * QW:3 * QW + HEADS])
        q.stage()
        areas_at, self.work_at = self.work_at, split_at
        self.split_buffers(DC * P)
        self.work_at = areas_at
        qT, kT, v = self.area(4, T), self.area(4, T), self.area(TT, QW)
        pooled = self.area_split(4)
        u_bufs = [self.area(T) for _ in range(3)]
        minus_F = self.area(T)

        w_in = d["w_in"]
        ready = []

        def keep_columns(out, scale):
            def finish(j, bank, m):
                m = self.act([m], out[:, j, :], bank.ap, ACT.Copy, scale=scale)
                bank.release(m)
                ready.append(m)
            return finish

        def keep_v(i, bank, m):
            m = self.copy([m], v[:, i, :], bank.ap)
            bank.release(m)
            ready.append(m)

        h = PerChunk()
        q_pieces = self.column_pieces(w_in, 0, hT, h, keep_columns(qT, DH ** -0.5))
        q_begun = self.begin(q_pieces)
        mod_a = self.modulation_sum(0)
        gain, gain_done = self.gain_of(mod_a, DC, "norm1_g")
        self.rms_finish(inv, [self.x_done, gain_done], hT, gain, self.mod[:, 0:DC], h)
        modulate = lambda part, s: lambda: self.modulation(part, s, s + 1)
        self.stream(q_pieces, q_begun)
        self.stream(self.column_pieces(w_in, QW, hT, h, keep_columns(kT, 1.0)), None, [modulate(1, s) for s in range(4)])
        v_pieces = self.row_pieces(w_in, 2 * QW, hT, h, keep_v)
        v_begun = self.begin(v_pieces)

        bank, logit, m = self.narrow(h, wf, wf_in, HEADS, hT, minus_F)
        y, a, log_f, F = self.tiny(TT, 8), self.tiny(TT, 8), self.tiny(TT, 8), self.tiny(TT, 8)
        m = self.tt([m], y, logit, self.r("b_f").unsqueeze(1).to_broadcast([P, TT, 8]), ALU.add)
        bank.release(m)
        e = self.softplus_part([m], a, y)
        log_f_done = self.stt([e], log_f, y, 0.0, a, ALU.min, ALU.subtract)
        def sum_b():
            self.mod_b_done = self.modulation_sum(1)
        self.stream(v_pieces, v_begun, [sum_b] + [modulate(2, s) for s in range(3)])
        bank = self.banks.take()
        for i in range(TT):
            for j in range(i + 1):
                c = self.c("upto") if j == i else self.c("ones")
                self.mm([bank.free, log_f_done], bank.ap[:, i * 8:i * 8 + 8], c, log_f[:, j, :], j == 0, j == i)
        F_done = self.copy([q.last("tensor")], F, bank.ap[:, 0:32].rearrange("p (i h) -> p i h", i=TT), "vector")
        bank.release(F_done)
        bank = self.banks.take()
        for i in range(TT):
            for j in range(i + 1):
                c = self.c("upto") if j == i else self.c("ones")
                self.mm([bank.free, log_f_done], bank.ap[0:8, i * P:(i + 1) * P], log_f[:, j, :], c, j == 0, j == i)
        rows_done = self.act([q.last("tensor")], minus_F[0:8, :], bank.ap[0:8, :], ACT.Copy, scale=-1.0)
        bank.release(rows_done)
        self.mixed_marks = []
        pool_lane = self.lane("pool_w_in")
        pool_w = self.shaped(self.rms_tmp.rearrange("p a b -> p (a b)")[:, 0:4 * P], (4, P))
        pool_in = pool_lane.copy("scalar", [h], pool_w, d["pool_w"].rearrange("g c d -> c g d"))
        counts = self.c("pool_count").rearrange("p (g n) -> p g n", g=4)
        u_free = []
        waiting = []

        def pool(g, bank, m):
            if waiting:
                waiting.pop()()
            window = POOL_WINDOWS[g]
            u, s, s2 = u_bufs
            m = u_done = self.copy([m, list(u_free)], u, bank.ap, "scalar")
            bank.release(m)
            src, reach = u, 1
            while reach < window:
                dst = s2 if src is s else s
                m1 = self.tt([m], dst[:, reach:], src[:, reach:], src[:, :T - reach], ALU.add)
                m2 = self.copy([m], dst[:, 0:reach], src[:, 0:reach], "vector")
                m, src, reach = [m1, m2], dst, 2 * reach
            other = s2 if src is s else s
            m = self.stt([m, u_done], other, src, 1.0 / window, u, ALU.mult, ALU.subtract)
            m = self.tt([m], other[:, 0:16], src[:, 0:16], counts[:, g, :], ALU.mult)
            m = self.tt([m], other[:, 0:16], other[:, 0:16], u[:, 0:16], ALU.subtract)

            def own_map(m=m, other=other):
                bank = self.banks.take()
                m = self.mm([m, pool_in, bank.free], bank.ap, pool_w[:, g, :], other, True, True)
                u_free[:] = [m]
                self.mixed_marks.append(self.split_result(pooled.hi[g], pooled.lo[g], bank, m, self.v("pool_scale", g)))
            waiting.append(own_map)

        self.stream(self.column_pieces(w_in, 3 * QW + HEADS, hT, h, pool), None, [modulate(2, 3)])
        self.mod_b_done = self.modulation_sum(2)
        waiting.pop()()

        q.stage()
        self.work_at = hT_at
        attended = self.area_split(4)
        mixed = Split(attended.hi + pooled.hi, attended.lo + pooled.lo)
        F_rows = self.area(HEADS, T)
        for hd in range(HEADS):
            bank = self.banks.take()
            m = self.mm([bank.free, rows_done], bank.ap, self.c("head_row", 8)[:, hd * P:(hd + 1) * P],
                        minus_F[0:8, :], True, True)
            done = self.copy([m], F_rows[:, hd, :], bank.ap)
            bank.release(done)
            ready.append(done)
        ready.append(F_done)

        def logits(i, hd, bank, m, p):
            n = (i + 1) * P
            m = self.stt([m, ready, p.free], p.ap[:, 0:n], bank.ap[:, 0:n], F[:, i, hd:hd + 1],
                         F_rows[:, hd, 0:n], ALU.add, ALU.add)
            bank.release(m)
            return self.tt([m], p.ap[:, i * P:n], p.ap[:, i * P:n], self.c("causal"), ALU.add)

        out_pieces = self.residual_pieces(d["w_out"], mixed, self.mod[:, 2 * DC:3 * DC])
        out_begun = self.begin(out_pieces)
        self.attend(qT, kT, v, lambda i: (i + 1) * P, logits,
                    lambda i, b, m: self.turn_row(b, m, mixed, 0, i), ready,
                    Rotation([self.area(QW) for _ in range(2)]))

        self.stream(out_pieces, out_begun)

    def softplus_part(self, after, out, y):
        m = self.act(after, out, y, ACT.Abs)
        m = self.act([m], out, out, ACT.Exp, scale=-1.0)
        return self.act([m], out, out, ACT.Ln, bias=self.c("ones")[:, 0:1])

    def residual_pieces(self, weight, mixed, gate=None):
        self.x_done = PerChunk()

        def add(k, bank, m):
            x = self.xT3[:, k, :]
            if gate is None:
                m = self.tt([m], x, bank.ap, x, ALU.add)
            else:
                m = self.stt([m, self.mod_b_done], x, bank.ap, gate[:, k:k + 1], x, ALU.mult, ALU.add)
            bank.release(m)
            self.x_done.append(m)

        return (self.column_pieces(weight, 0, mixed, self.mixed_marks, add)
                + self.column_pieces(weight, 512, mixed, self.mixed_marks, lambda j, bank, m: add(4 + j, bank, m)))

    def block1_mlp(self):
        d, q = self.dram, self.q
        q.stage()
        self.work_at = 0
        HC = FC // 2
        self.split_buffers(HC * P)
        hT_at = self.work_at
        hT = self.area_split(DC)
        hidden = self.area_split(HC)
        self.rms_tmp = self.area(4, T)
        gain, gain_done = self.gain_of(self.mod_b_done, 4 * DC, "norm2_g")
        h = PerChunk()
        convs = Rotation([self.rms_tmp[:, i, :] for i in range(4)])
        up = d["ffn_up"].rearrange("(k p) n -> p k n", p=P)
        down = d["ffn_down"].rearrange("(k p) n -> p k n", p=P)
        last_down = []

        def up_pieces(first, count, marks):
            n = count * P

            def load():
                w = self.slab((0, (DC, n), up[:, :, first * P:first * P + n]),
                              (DC * n, (DC, n), up[:, :, FF + first * P:FF + first * P + n]))
                w.views = [self.shaped(w.ap[:, i * DC * n:(i + 1) * DC * n], (DC, n)) for i in range(2)]
                return w
            slab = self.once(load)
            out = []
            for j in range(count):
                pair = []
                for side in range(2):
                    ch = side * FC + first + j

                    def use(b):
                        bank = self.bank_of_piece = self.banks.take()
                        for k in range(DC):
                            m = self.three_products([bank.free, b.ready, h[k]], bank.ap, (b.hi[:, k, :], b.lo[:, k, :]),
                                                    (hT.hi[k], hT.lo[k]), k == 0, k == DC - 1)
                        return m

                    def then(m, ch=ch, pair=pair, side=side, c_out=(first + j) % HC):
                        bank, c = self.bank_of_piece, convs.take()
                        tap = [self.v("conv_w", t * 2 * FC + ch) for t in range(3)]
                        m = self.act([m, c.free], c.ap, bank.ap, ACT.Identity, bias=self.v("conv_b", ch), scale=tap[2])
                        m = self.stt([m], c.ap[:, 1:], bank.ap[:, 0:T - 1], tap[1], c.ap[:, 1:], ALU.mult, ALU.add)
                        m = self.stt([m], c.ap[:, 2:], bank.ap[:, 0:T - 2], tap[0], c.ap[:, 2:], ALU.mult, ALU.add)
                        bank.release(m)
                        if side == 0:
                            m = self.act([m], c.ap, c.ap, ACT.Silu)
                        pair.append((c, m))
                        if side == 1:
                            (cg, mg), (cv, mv) = pair
                            m = self.tt([mg, mv], cv.ap, cg.ap, cv.ap, ALU.mult, "gpsimd")
                            cg.release(m)
                            m = self.act([m, list(last_down)], hidden.hi[c_out], cv.ap, ACT.Copy)
                            m = self.tt([m], hidden.lo[c_out], cv.ap, hidden.hi[c_out].bitcast(F32), ALU.subtract)
                            cv.release(m)
                            marks.append(m)
                    out.append((slab, lambda s, j=j, side=side: s.views[side][:, :, j * P:(j + 1) * P],
                                j == count - 1 and side == 1, use, then))
            return out

        def down_piece(half, k, marks):
            def load():
                w = self.slab((0, (HC, P), down[:, half * HC:(half + 1) * HC, k * P:(k + 1) * P]))
                w.view = self.shaped(w.ap[:, 0:HC * P], (HC, P))
                return w

            def use(b):
                bank = self.bank_of_piece = self.banks.take()
                for c in range(HC):
                    m = self.three_products([bank.free, b.ready, marks], bank.ap, (b.hi[:, c, :], b.lo[:, c, :]),
                                            (hidden.hi[c], hidden.lo[c]), c == 0, c == HC - 1)
                last_down[:] = [m]
                return m

            def then(m):
                bank, x = self.bank_of_piece, self.xT3[:, k, :]
                m = self.stt([m, self.x_done[k]], x, bank.ap, self.mod[:, 5 * DC + k:5 * DC + k + 1], x, ALU.mult, ALU.add)
                bank.release(m)
                self.x_done[k] = m
            return (self.once(load), lambda s: s.view, True, use, then)

        pieces = []
        for half in range(2):
            marks = []
            at = half * HC
            while at < (half + 1) * HC:
                n = min(2, (half + 1) * HC - at)
                pieces += up_pieces(at, n, marks)
                at += n
            pieces += [down_piece(half, k, marks) for k in range(DC)]
        self.rms(self.x_done, hT, gain, self.mod[:, 3 * DC:4 * DC], [gain_done], pieces, h)
        for c in convs.buffers:
            c.free = h
        self.stream(pieces, self.begun)
        self.rms_tmp = self.shaped(self.work[:, hT_at:hT_at + 4 * T], (4, T))
        self.x_done = self.rms(self.x_done, self.xT3, self.v("final_g", 0, DC))

    def head_norm(self, after, out, src, ones, n, gain, scale=None, eps_inside=True):
        t = self.norm_tmp.take()
        m = self.act([after, t.free], t.ap[:, 0, :], src, ACT.Square)
        bank = self.banks.take()
        m = self.mm([m, bank.free], bank.ap, ones, t.ap[:, 0, :], True, True)
        m = self.act([m], t.ap[:, 1, :], bank.ap, ACT.Sqrt, bias=self.c("eps"), scale=1.0 / n)
        bank.release(m)
        m = self.recip([m], t.ap[:, 1, :], t.ap[:, 1, :])
        m = self.stt([m], out, src, gain, t.ap[:, 1, :], ALU.mult, ALU.mult)
        t.release(m)
        return m

    def block2_attention(self):
        d, q = self.dram, self.q
        entry = q.stage()
        self.work_at = 0
        self.hT2 = hT = self.area_split(DC)
        self.mixed_at = self.work_at
        mixed = self.mixed2 = self.area_split(4)
        qT, kT, v = self.area(4, T), self.area(4, T), self.area(TT, QW)
        raws = Rotation([self.area(T) for _ in range(2)])
        shared_at = self.work_at
        self.split_buffers(DC * P)
        self.rms_tmp = self.area(4, T)
        self.norm_tmp = Rotation([self.area(2, T) for _ in range(2)])
        h = self.h2 = PerChunk()
        w_in = d["w_in_2"]
        ready = []
        q_gain = self.tiny(1)
        gain_done = self.ts([self.vec_done], q_gain, self.v("q_gain"), DH ** -0.5, ALU.mult)

        def normed(out, gain):
            def finish(j, bank, m):
                raw = raws.take()
                c = self.copy([m, raw.free], raw.ap, bank.ap)
                bank.release(c)

                def norm():
                    done = self.head_norm([c, gain_done], out[:, j, :], raw.ap, self.c("ones64"), DH, gain)
                    raw.release(done)
                    ready.append(done)
                return norm
            return finish

        def keep_v(i, bank, m):
            m = self.copy([m], v[:, i, :], bank.ap)
            bank.release(m)
            ready.append(m)

        pieces = (self.column_pieces(w_in, 0, hT, h, normed(qT, q_gain))
                  + self.column_pieces(w_in, QW, hT, h, normed(kT, self.v("k_gain")))
                  + self.row_pieces(w_in, 2 * QW, hT, h, keep_v))
        self.rms(self.x_done, hT, self.v("ln1_g", 0, DC), pieces=pieces, marks=h)
        self.stream(pieces, self.begun)

        n_m = 2 * WIN_H - 2
        entry = q.stage()
        self.work_at = shared_at
        table = [self.area(n_m, GRID) for _ in range(HEADS)]
        table_done = []
        rpb = d["rpb"]
        landed = {}
        for hd in range(HEADS):
            lane = self.lane(f"rpb{hd}_in")
            for r2 in range(2):
                in_ = rpb[hd, 1 - r2:1 - r2 + n_m, :]
                source = bass.AP(in_.tensor, in_.offset, [[1, GRID], [2 * GRID - 1, n_m], [1, GRID]])
                landed[hd] = lane.copy("sync", entry, table[hd][r2 * GRID:(r2 + 1) * GRID, :, :],
                                   source)
        for hd in range(HEADS):
            table_done.append(self.tt([landed[hd]], table[hd], table[hd],
                                      self.c("window").unsqueeze(1).to_broadcast([P, n_m, GRID]), ALU.add, "gpsimd"))

        def logits(i, hd, bank, m, p):
            at = table[hd][:, 6 - 2 * i:6 - 2 * i + ROWS, :]
            forwards = bass.AP(at.tensor, at.offset + GRID - 1, [list(at.ap[0]), [GRID, ROWS], [-1, GRID]])
            by_row = lambda ap: ap.rearrange("p (r c) -> p r c", r=ROWS)
            m = self.tt([m, table_done[hd], p.free], by_row(p.ap), by_row(bank.ap), forwards, ALU.add)
            bank.release(m)
            return m

        square, stats = self.area(QW), self.tiny(TT, 3)
        self.mixed_marks = []
        last = []

        def out_row(i, b, m):
            m = self.act([m] + last, square, b.ap, ACT.Square, accum=stats[:, i, 0:1])
            last[:] = [m]
            m = self.act([m], stats[:, i, 1:2], stats[:, i, 0:1], ACT.Sqrt, bias=self.c("eps"), scale=1.0 / QW)
            m = self.recip([m], stats[:, i, 2:3], stats[:, i, 1:2])
            m = self.stt([m], b.ap, b.ap, stats[:, i, 2:3], self.r("attn_out_g"), ALU.mult, ALU.mult)
            self.turn_row(b, m, mixed, 0, i)

        self.attend(qT, kT, v, lambda i: T, logits, out_row, ready, raws)

    def deltanet(self):
        d, q = self.dram, self.q
        q.stage()
        hT, h = self.hT2, self.h2
        self.work_at = self.mixed_at + 2 * 4 * T
        qkvT = self.area(12, T)
        z = self.area(TT, QW)
        free_at = self.work_at
        self.split_buffers(DC * P)
        self.norm_tmp = Rotation([self.area(2, T) for _ in range(2)])
        convs = Rotation([self.area(T) for _ in range(3)])
        w_in = d["w_in_2"]
        base = 3 * QW
        done = {}

        def conv(ch, bank, m):
            c = convs.take()
            tap = [self.v("dn_conv_w", t * 12 + ch) for t in range(DN_TAPS)]
            m = self.act([m, c.free], c.ap, bank.ap, ACT.Copy, scale=tap[2])
            for t in (0, 1, 3, 4):
                s_ = t - DN_TAPS // 2
                to = slice(max(0, -s_), T - max(0, s_))
                of = slice(max(0, s_), T - max(0, -s_))
                m = self.stt([m], c.ap[:, to], bank.ap[:, of], tap[t], c.ap[:, to], ALU.mult, ALU.add)
            bank.release(m)
            m = self.act([m], qkvT[:, ch, :], c.ap, ACT.Silu)
            c.release(m)
            done[ch] = m

        z_done = {}

        def keep_z(i, bank, m):
            m = self.act([m], z[:, i, :], bank.ap, ACT.Silu)
            bank.release(m)
            by_head = z[:, i, :].rearrange("p (h d) -> p h d", h=4)
            z_done[i] = self.tt([m], by_head, by_head, self.r("dn_out_g").unsqueeze(1).to_broadcast([P, 4, P]),
                                ALU.mult, "gpsimd")

        pieces = []
        for s in range(3):
            pieces += self.column_pieces(w_in, base + s * 512, hT, h, lambda j, bank, m, s=s: conv(4 * s + j, bank, m))
        g = beta = cum = whole = k_scale = w_scale = scales = g_done = beta_done = k_scale_done = None

        def gates():
            nonlocal g, beta, cum, whole, k_scale, w_scale, scales, g_done, beta_done, k_scale_done
            lane = self.lane("gates_in")
            wg = self.tiny(DC, 16)
            gates_in = lane.copy("scalar", [], wg, w_in.rearrange("(k p) n -> p k n", p=P)[:, :, base + 4 * 512:base + 4 * 512 + 16])
            tmp = convs.take()
            bank, ab, m = self.narrow([h, tmp.free], wg, gates_in, 16, hT, tmp.ap)
            tmp.release(m)
            y, a, g, beta = (self.tiny(TT, 8) for _ in range(4))
            rate = self.tiny(8)
            m1 = self.tt([m], y, ab[:, :, 0:8], self.r("dt_bias").unsqueeze(1).to_broadcast([P, TT, 8]), ALU.add)
            m2 = self.act([m1], beta, ab[:, :, 8:16], ACT.Exp, scale=-1.0)
            bank.release(m1, m2)
            m2 = self.ts([m2], beta, beta, 1.0, ALU.add)
            beta_done = self.recip([m2], beta, beta)
            m = self.softplus_part([m1], a, y)
            m = self.stt([m], a, y, 0.0, a, ALU.max, ALU.add)
            r = self.act([], rate, self.r("a_log"), ACT.Exp)
            m = self.stt([m, r], g, a, -1.0, rate.unsqueeze(1).to_broadcast([P, TT, 8]), ALU.mult, ALU.mult)
            g_done = m
            yield
            cum, whole = self.tiny(2, TT, 4), self.tiny(2, TT, 4)
            bank = self.banks.take()
            for dr in range(2):
                gd = g[:, :, dr * 4:dr * 4 + 4]
                self.mm([bank.free, g_done], bank.ap[:, dr * 16:dr * 16 + 16], self.c(f"cum{dr}"), gd, True, True)
                m = self.mm([], bank.ap[:, 32 + dr * 16:48 + dr * 16], self.c("ones64"), gd, True, True)
            m1 = self.copy([m], cum.rearrange("p a b c -> p (a b c)"), bank.ap[:, 0:32], "vector")
            m2 = self.copy([m], whole.rearrange("p a b c -> p (a b c)"), bank.ap[:, 32:64], "vector")
            bank.release(m2)
            k_scale, w_scale = self.tiny(2, TT, 4), self.tiny(2, TT, 4)
            m = self.tt([m1, m2], k_scale, whole, cum, ALU.subtract)
            k_scale_done = self.act([m], k_scale, k_scale, ACT.Exp)
            m = self.act([m1], w_scale, cum, ACT.Exp)
            for dr in range(2):
                m = self.tt([m, beta_done], w_scale[:, dr], w_scale[:, dr], beta[:, :, dr * 4:dr * 4 + 4], ALU.mult)
            scales = [k_scale_done, m, beta_done, m1]

        def norm(ch):
            done[ch] = self.head_norm(done[ch], qkvT[:, ch, :], qkvT[:, ch, :], self.c("ones"), 1.0,
                                      float(P) ** -0.5 if ch < 4 else 1.0)
        between = [lambda: next(gate_steps, None)] + [lambda: None] * 15
        for n, chunks in ((12, (0, 1, 2)), (13, (3, 4, 5)), (14, (6, 7))):
            between[n] = lambda chunks=chunks: [norm(ch) for ch in chunks]
        pieces += self.row_pieces(w_in, base + 3 * 512, hT, h, keep_z)
        begun = self.begin(pieces)
        gate_steps = gates()
        next(gate_steps)
        self.stream(pieces, begun, between)
        done = [done[ch] for ch in range(12)]

        free_h = [q.last("tensor")]
        k_tok = self.shaped(self.work[:, 0:4 * T], (4, T))
        v_tok = self.shaped(self.work[:, 4 * T:8 * T], (4, T))
        tok_done = {}
        for i in range(TT):
            for dst, off in ((k_tok, 4), (v_tok, 8)):
                bank = self.banks.take()
                for hd in range(4):
                    m = self.turn([bank.free, done[off + hd]], bank.ap[:, hd * P:(hd + 1) * P],
                                  qkvT[:, off + hd, i * P:(i + 1) * P], signal=hd == 3)
                m = self.copy([m, free_h], dst[:, i, :], bank.ap)
                bank.release(m)
                tok_done[off, i] = m

        turned = [q.last("tensor"), q.last("scalar"), q.last("vector")]
        self.work_at = 8 * T
        o_acc = self.area(TT, QW)
        states = [self.area(4, P) for _ in range(2)]
        bufs = [self.area(512) for _ in range(2)]
        self.work_at = free_at
        while self.work_at + 512 <= self.WORK:
            bufs.append(self.area(512))
        bufs += [qkvT[:, 8 + i, :] for i in range(4)]
        pool = Rotation(bufs)
        for b in pool.buffers:
            b.free = turned
        state_done = [[self.q.do("gpsimd", [turned], lambda e, s=s: e.memset(s, 0.0))] for s in states]
        o_done = {}
        heads = lambda ap: ap.rearrange("p (h d) -> p h d", h=4)
        spread = lambda col: col.unsqueeze(2).to_broadcast([P, 4, P])
        over_heads = lambda c: c.unsqueeze(1).to_broadcast([P, 4, P])

        def per_head(after, pairs, out=None, bank=None, rows=slice(0, P)):
            bank = self.banks.take()
            for hd in range(4):
                lhsT, rhs = pairs(hd)
                m = self.mm([after, bank.free], bank.ap[:, hd * P:(hd + 1) * P], lhsT, rhs, True, True)
            return bank, m

        def unit(dr, i):
            tile = slice(i * P, (i + 1) * P)
            col = lambda t: t[:, dr, i, :]
            by_head = lambda b: (lambda hd: b.ap[:, hd * P:(hd + 1) * P])
            tt, ts, stt, act = self.tt, self.ts, self.stt, self.act
            g_col = g[:, i, dr * 4:dr * 4 + 4]
            b_col = beta[:, i, dr * 4:dr * 4 + 4]
            bg = pool.take()
            m = tt([g_done, bg.free], heads(bg.ap), over_heads(self.c(f"cum{dr}")), spread(g_col), ALU.mult)
            bank = self.banks.take()
            m = self.mm([m, bank.free], bank.ap, self.c("ones"), bg.ap, True, True)
            bg.release(m)
            yield
            eg, decay = pool.take(), pool.take()
            eg_done = act([m, eg.free], eg.ap, bank.ap, ACT.Exp)
            m = tt([eg_done, decay.free], heads(decay.ap), heads(bank.ap), over_heads(self.c(f"bar{dr}")), ALU.add)
            bank.release(m, eg_done)
            for hd in range(4):
                s = slice(hd * P, (hd + 1) * P)
                m = act([m, scales], decay.ap[:, s], decay.ap[:, s], ACT.Exp, bias=cum[:, dr, i, hd:hd + 1], scale=-1.0)
            decay_done = m
            yield
            kT = lambda hd: qkvT[:, 4 + hd, tile]
            qT = lambda hd: qkvT[:, hd, tile]
            kk, m_kk = per_head(done, lambda hd: (kT(hd), kT(hd)))
            qk, m_qk = per_head(done, lambda hd: (qT(hd), kT(hd)))
            L, QK = pool.take(), pool.take()
            yield
            m = tt([decay_done, m_qk, QK.free], QK.ap, qk.ap, decay.ap, ALU.mult)
            qk.release(m)
            qk_done = m
            for hd in range(4):
                s = slice(hd * P, (hd + 1) * P)
                m = stt([qk_done, scales], decay.ap[:, s], decay.ap[:, s], b_col[:, hd:hd + 1], self.c(f"strict{dr}"),
                        ALU.mult, ALU.mult)
            L_done = tt([m, m_kk, L.free], L.ap, kk.ap, decay.ap, ALU.mult)
            kk.release(L_done)
            decay.release(L_done)
            yield
            LT, QKT = pool.take(), pool.take()
            out = []
            for src, dst, ready in ((L, LT, L_done), (QK, QKT, qk_done)):
                bank = self.banks.take()
                for hd in range(4):
                    m = self.turn([ready, bank.free], bank.ap[:, hd * P:(hd + 1) * P], src.ap[:, hd * P:(hd + 1) * P],
                                  signal=hd == 3)
                if src is QK:
                    QK.release(m)
                m = self.copy([m, dst.free], dst.ap, bank.ap, "scalar")
                bank.release(m)
                out.append(m)
            LT_done, QKT_done = out
            qe, kd, vb, kb = (pool.take() for _ in range(4))
            qe_done = tt([eg_done, qe.free, done], heads(qe.ap), qkvT[:, 0:4, tile], heads(eg.ap), ALU.mult, "gpsimd")
            kd_done = tt([scales, kd.free, tok_done[4, i]], heads(kd.ap), heads(k_tok[:, i, :]), spread(col(k_scale)), ALU.mult, "gpsimd")
            vb_done = tt([scales, vb.free, tok_done[8, i]], heads(vb.ap), heads(v_tok[:, i, :]), spread(b_col), ALU.mult, "gpsimd")
            kb_done = tt([scales, kb.free, tok_done[4, i]], heads(kb.ap), heads(k_tok[:, i, :]), spread(col(w_scale)), ALU.mult, "gpsimd")
            yield
            N, NT, XT = (pool.take() for _ in range(3))
            in16, eye = over_heads(self.c("in16")), over_heads(self.c("ident"))
            mN = tt([L_done, N.free], heads(N.ap), heads(L.ap), in16, ALU.mult)
            mNT = tt([LT_done, NT.free], heads(NT.ap), heads(LT.ap), in16, ALU.mult)
            L.release(mN, LT_done)
            mXT = tt([mNT, XT.free], heads(XT.ap), eye, heads(NT.ap), ALU.subtract)
            power, powerT, mp, mpT = N, NT, mN, mNT
            for level in range(3):
                yield
                b1, m1 = per_head([mp, mpT], lambda hd: (by_head(powerT)(hd), by_head(power)(hd)))
                nxt = pool.take()
                n1 = self.copy([m1, nxt.free], nxt.ap, b1.ap, "vector")
                b1.release(n1)
                nxtT, n2 = None, None
                if level < 2:
                    b2, m1 = per_head([], lambda hd: (by_head(power)(hd), by_head(powerT)(hd)))
                    nxtT = pool.take()
                    n2 = self.copy([m1, nxtT.free], nxtT.ap, b2.ap, "scalar")
                    b2.release(n2)
                power.release(m1)
                powerT.release(m1, mXT)
                power, powerT, mp, mpT = nxt, nxtT, n1, n2
                yield
                bT, m2 = per_head([mp, mXT], lambda hd: (by_head(power)(hd), by_head(XT)(hd)))
                mXT = tt([m2], XT.ap, bT.ap, XT.ap, ALU.add)
                bT.release(mXT)
            power.release(m2)
            for join in ("join32", "join64"):
                yield
                X, J, W = pool.take(), pool.take(), pool.take()
                mJ = tt([LT_done, J.free], heads(J.ap), heads(LT.ap), over_heads(self.c(join)), ALU.mult, "gpsimd")
                bank = self.banks.take()
                for hd in range(4):
                    m = self.turn([mXT, bank.free], bank.ap[:, hd * P:(hd + 1) * P], by_head(XT)(hd), signal=hd == 3)
                mX = self.copy([m, X.free], X.ap, bank.ap, "scalar")
                bank.release(mX)
                yield
                b1, m1 = per_head([mJ, mX], lambda hd: (by_head(J)(hd), by_head(X)(hd)))
                J.release(m1)
                X.release(m1)
                mW = self.copy([m1, W.free], W.ap, b1.ap, "scalar")
                b1.release(mW)
                yield
                bT, m2 = per_head([mW], lambda hd: (by_head(W)(hd), by_head(XT)(hd)))
                mXT = tt([m2], XT.ap, XT.ap, bT.ap, ALU.subtract)
                bT.release(mXT)
                W.release(m2)
            LT.release(mJ, mNT)
            yield
            U, WT = pool.take(), pool.take()
            b1, m1 = per_head([mXT, vb_done], lambda hd: (by_head(XT)(hd), by_head(vb)(hd)))
            b2, m2 = per_head([kb_done], lambda hd: (by_head(kb)(hd), by_head(XT)(hd)))
            U_done = self.copy([m1, U.free], U.ap, b1.ap, "scalar")
            WT_done = self.copy([m2, WT.free], WT.ap, b2.ap, "vector")
            b1.release(U_done)
            b2.release(WT_done)
            XT.release(m2)
            vb.release(m2)
            kb.release(m2)
            yield
            S = states[dr]
            new = pool.take()
            o_bank = self.banks.take()
            for half in ((0, 1) if dr == 0 else (1, 0)):
                rows = slice(half * CHUNK, (half + 1) * CHUNK)
                end = half * CHUNK + (CHUNK - 1 if dr == 0 else 0)
                bank = self.banks.take()
                for hd in range(4):
                    lhs = WT.ap[:, hd * P + half * CHUNK:hd * P + (half + 1) * CHUNK]
                    m = self.mm([state_done[dr], WT_done, bank.free], bank.ap[rows, hd * P:(hd + 1) * P], lhs, S[:, hd, :], True, True)
                m_new = self.tt([m, U_done, new.free], new.ap[rows, :], U.ap[rows, :], bank.ap[rows, :], ALU.subtract)
                bank.release(m_new)
                yield
                for hd in range(4):
                    c = slice(hd * P + half * CHUNK, hd * P + (half + 1) * CHUNK)
                    out = o_bank.ap[rows, hd * P:(hd + 1) * P]
                    self.mm([qe_done, o_bank.free, QKT_done, m_new], out, qe.ap[:, c], S[:, hd, :], True, False)
                    m_o = self.mm([], out, QKT.ap[rows, c], new.ap[rows, hd * P:(hd + 1) * P], False, True)
                bank = self.banks.take()
                for hd in range(4):
                    m = self.mm([kd_done, bank.free], bank.ap[:, hd * P:(hd + 1) * P], kd.ap[rows, hd * P:(hd + 1) * P],
                                new.ap[rows, hd * P:(hd + 1) * P], True, True)
                ms = self.tt([m_o, eg_done, state_done[dr]], S, S, heads(eg.ap)[:, :, end:end + 1].to_broadcast([P, 4, P]), ALU.mult, "vector")
                ms = self.tt([ms, m], S, S, heads(bank.ap), ALU.add)
                bank.release(ms)
                state_done[dr] = [ms]
                yield
            for b in (WT, new, qe, QKT, kd):
                b.release(m)
            U.release(m_new)
            eg.release(ms, qe_done)
            first = i not in o_done
            if first:
                mo = self.copy([m_o], o_acc[:, i, :], o_bank.ap, "vector")
            else:
                mo = self.tt([m_o, o_done[i]], o_acc[:, i, :], o_acc[:, i, :], o_bank.ap, ALU.add)
            o_bank.release(mo)
            o_done[i] = mo

        for step in range(TT):
            running = [unit(0, step), unit(1, TT - 1 - step)]
            while running:
                for u in list(running):
                    try:
                        next(u)
                    except StopIteration:
                        running.remove(u)

        q.stage()
        self.work_at = 0
        got = self.area_split(4)
        mixed = Split(self.mixed2.hi + got.hi, self.mixed2.lo + got.lo)
        sq = [qkvT[:, n, :] for n in range(2)]
        outs = Rotation([qkvT[:, n, :] for n in range(2, 4)])
        self.work_at = free_at
        self.split_buffers(DC * P)
        out_pieces = self.residual_pieces(d["w_out_2"], mixed)
        out_begun = self.begin(out_pieces)
        ss = self.tiny(TT, 4)
        reduced = []
        for i in range(TT):
            m = self.act(reduced[i - 2:i - 1] if i > 1 else [], sq[i % 2], o_acc[:, i, :], ACT.Square)
            reduced.append(self.reduce([m], ss[:, i, :], heads(sq[i % 2]), ALU.add))
        inverse = []
        for i in range(TT):
            m = self.act([reduced[i]], ss[:, i, :], ss[:, i, :], ACT.Sqrt, bias=self.c("eps"), scale=1.0 / P)
            inverse.append(self.recip([m], ss[:, i, :], ss[:, i, :]))
        for i in range(TT):
            b = outs.take()
            for hd in range(4):
                cols = slice(hd * P, (hd + 1) * P)
                m = self.stt([inverse[i], z_done[i], b.free], b.ap[:, cols], o_acc[:, i, cols], ss[:, i, hd:hd + 1],
                             z[:, i, cols], ALU.mult, ALU.mult)
            self.turn_row(b, m, mixed, 4, i)
        self.stream(out_pieces, out_begun)

    def hot_places(self, at):
        keep, self.work_at = self.work_at, at
        places = [self.rounded(TT * 4 * CAP) for _ in range(2)]
        self.work_at = keep
        return places

    def moe(self):
        d, q = self.dram, self.q
        entry = q.stage()
        self.work_at = 0
        hT = self.area(DC, T)
        x_tok = self.shaped(self.work[:, 0:TT * D], (TT, D))
        in_slots = [self.ring[:, i * UP_W:(i + 1) * UP_W] for i in range(3)] + [self.area(UP_W)]
        down_slots = [self.area(DOWN_W) for _ in range(4)]
        h_tok = [self.shaped(self.rounded(TT * D), (TT, DC, P)) for _ in range(2)]
        hot_at = self.work_at
        self.rms_tmp = self.area(4, T)
        keep_at = self.work_at
        wr = self.area(DC, 72)
        ones_r, before_r = self.rounded(P), self.rounded(P)
        A = self.shaped(self.rounded(PICK_TILES * EXPERTS), (PICK_TILES, EXPERTS))
        prod = self.area(PICK_TILES, EXPERTS)
        who_at = self.work_at
        who = self.shaped(self.rounded(PICK_TILES * P), (PICK_TILES, P))
        tmp = self.work[:, who_at:who_at + T]
        blocks = self.shaped(self.rounded(PICK_TILES * (EXPERTS + OVER)), (PICK_TILES, EXPERTS + OVER))
        end_at = self.work_at
        self.work_at = max(end_at, keep_at + 2 * D + 2 * 3 * DE)
        place = self.area(TT, EXPERTS + OVER)
        router_in = self.lane("router_in").copy("scalar", [entry], wr, d["router_w"].rearrange("(k p) n -> p k n", p=P))
        h = self.rms(self.x_done, hT, self.v("ln2_g", 0, DC))

        def slots_of(aps, free, name):
            slots = Rotation(aps)
            for n, s in enumerate(slots.buffers):
                s.free, s.lane, s.over_lane = free[n], self.lane(f"{name}{n}_in"), self.lane(f"overflow_{name}{n}_in")
            return slots

        up_slots = slots_of(in_slots, [b.free for b in self.slabs.buffers] + [entry], "up")
        low_slots = slots_of(down_slots, [entry] * 4, "down")

        def load_up(e):
            s = up_slots.take()
            for at, name in ((0, "w_gate"), (DOWN_W, "w_up")):
                s.landed = s.lane.copy("sync", s.free, s.ap[:, at:at + DOWN_W], d[name][e * P:(e + 1) * P, :])
            return s

        def load_down(e):
            s = low_slots.take()
            s.landed = s.lane.copy("sync", s.free, s.ap, d["w_down"][e * P:(e + 1) * P, :])
            return s

        first_up = [load_up(e) for e in range(3)]
        first_down = [load_down(0)]
        first_up.append(load_up(3))
        first_down += [load_down(e) for e in range(1, 4)]

        def load_expert(e):
            if e < len(first_up):
                return first_up[e], first_down[e]
            return load_up(e), load_down(e)

        def load_overflow(n, w_index, ready):
            w = up_slots.take(), low_slots.take()
            for slots, at, name in ((up_slots, 0, "w_gate"), (up_slots, DOWN_W, "w_up"), (low_slots, 0, "w_down")):
                s = w[slots is low_slots]
                s.landed = s.over_lane.indirect([s.free, ready], out=s.ap[:, at:at + DOWN_W], out_offset=None,
                                                in_=d[name], in_offset=bass.IndirectOffsetOnAxis(ap=w_index[:, n:n + 1], axis=0),
                                                bounds_check=EXPERTS * P - 1, oob_is_err=False)
            return w

        bank, logits, m = self.narrow(h, wr, router_in, 72, hT, tmp)
        router_turned = m
        lg = self.shaped(self.rms_tmp.rearrange("p a b -> p (a b)")[:, 640:640 + 288], (TT, 72))
        m = self.tt([m, h], lg, logits,
                    self.r("router_b").unsqueeze(1).to_broadcast([P, TT, 72]), ALU.add)
        bank.release(m)
        lg_done = m
        m = self.act([entry], ones_r, self.c("ones"), ACT.Copy)
        rounded_in = self.act([entry], before_r, self.c("before"), ACT.Copy)

        y_rows = self.nc.dram_tensor("y_rows", [PICKS, D], F32, kind="Internal").ap()
        rows_done, x_rows = [], []
        evacuate = []

        def turn_h(n):
            i, half = n // 2, n % 2
            bank = self.banks.take()
            for j in range(4):
                m = self.turn([h, bank.free], bank.ap[:, j * P:(j + 1) * P],
                              hT[:, half * 4 + j, i * P:(i + 1) * P], signal=j == 3)
            src = bank.ap.rearrange("p (q k) -> p k q", k=DC)
            hi, lo = (part[:, i, :, half * 64:half * 64 + 64] for part in h_tok)
            m = self.act([m], hi, src, ACT.Copy)
            evacuate.append((bank, lo, src, hi, m))

        def rest_of_h():
            for bank, lo, src, hi, m in evacuate:
                m = self.tt([m], lo, src, hi.bitcast(F32), ALU.subtract)
                bank.release(m)
                rows_done.append(m)
            evacuate.clear()

        for n in range(6):
            turn_h(n)

        R = self.tiny
        gmax, gsum, m1c, m2c = R(TT), R(TT), R(TT), R(TT)
        t8, oh_g, ing, oh1, oh2 = R(TT, 8), R(TT, 8), R(TT, 8), R(TT, 8), R(TT, 8)
        cm = R(TT)
        gates = R(TOP_K, TT)
        wide = lambda c, n=8: c.unsqueeze(2).to_broadcast([P, TT, n])
        rev = self.c("rev8").unsqueeze(1).to_broadcast([P, TT, 8])
        tt, ts, red = self.tt, self.ts, self.reduce

        def first_max(m, src, top, out):
            m = red([m], top, src, ALU.max)
            m = tt([m], t8, src, wide(top), ALU.is_equal)
            m = tt([m], t8, t8, rev, ALU.mult)
            m = red([m], cm, t8, ALU.max)
            return tt([m], out, t8, wide(cm), ALU.is_equal)

        m = first_max(lg_done, lg[:, :, 0:8], gmax, oh_g)
        group = R(TT, 8)
        m = group_done = tt([m], group, lg[:, :, 0:8], wide(gmax), ALU.subtract)
        big = self.shaped(self.rms_tmp.rearrange("p a b -> p (a b)")[:, 1024:1024 + 256], (TT, 64))
        el = lg[:, :, 8:72].rearrange("p i (g e) -> p i g e", g=8)
        big4 = big.rearrange("p i (g e) -> p i g e", g=8)
        m = tt([m], big4, el, oh_g.unsqueeze(3).to_broadcast([P, TT, 8, 8]), ALU.mult)
        m = red([m], ing, big.rearrange("p i (g e) -> p i e g", g=8), ALU.add)
        m = first_max(m, ing, m1c, oh1)
        m = self.stt([m], ing, oh1, NEG, ing, ALU.mult, ALU.add)
        m = first_max(m, ing, m2c, oh2)
        tops_done = m

        def gate():
            m = self.act([group_done], group, group, ACT.Exp)
            m = red([m], gsum, group, ALU.add)
            mg = self.recip([m], gsum, gsum)
            m = tt([tops_done], m2c, m2c, m1c, ALU.subtract)
            m = self.act([m], m2c, m2c, ACT.Exp)
            m = ts([m], m1c, m2c, 1.0, ALU.add)
            m = self.recip([m], m1c, m1c)
            m = tt([m, mg], gates[:, 0, :], m1c, gsum, ALU.mult)
            return tt([m], gates[:, 1, :], gates[:, 0, :], m2c, ALU.mult)

        for c, oh in enumerate((oh1, oh2)):
            for i in range(TT):
                m = tt([m], A[:, c * TT + i, :].rearrange("p (g e) -> p g e", g=8),
                       oh_g[:, i, :].unsqueeze(2).to_broadcast([P, 8, 8]),
                       oh[:, i, :].unsqueeze(1).to_broadcast([P, 8, 8]), ALU.mult)
        A_done = m
        bank = self.banks.take()
        flat_A = A.rearrange("p n e -> p (n e)")
        self.mm([A_done, rounded_in, bank.free], bank.ap, before_r, flat_A, True, False)
        for n in range(1, PICK_TILES):
            m_rank = self.mm([], bank.ap[:, n * EXPERTS:], ones_r, flat_A[:, 0:(PICK_TILES - n) * EXPERTS], False, n == PICK_TILES - 1)
        rest_of_h()
        for n in range(6, 8):
            turn_h(n)
        bank2 = self.banks.take()
        for n in range(PICK_TILES):
            m_c = self.mm([bank2.free], bank2.ap[0:64, 0:1], A[:, n, :].bitcast(F32), self.c("ones")[:, 0:1], n == 0, n == PICK_TILES - 1)
        rank, blk, off, who_e, q_blk = (R(PICK_TILES) for _ in range(5))
        A32 = A.bitcast(F32)
        m = tt([m_rank], prod, bank.ap.rearrange("p (n e) -> p n e", n=PICK_TILES), A32, ALU.mult)
        bank.release(m)
        m = red([m], rank, prod, ALU.add)
        m = tt([m], prod[:, :, 0:MORE], rank.unsqueeze(2).to_broadcast([P, PICK_TILES, MORE]),
               self.c("caps").unsqueeze(1).to_broadcast([P, PICK_TILES, MORE]), ALU.is_ge)
        m = red([m], blk, prod[:, :, 0:MORE], ALU.add)
        m = self.stt([m], rank, blk, -float(CAP), rank, ALU.mult, ALU.add)
        main = R(PICK_TILES)
        m = ts([m], main, blk, 0.0, ALU.is_equal)
        m = tt([m], blocks[:, :, 0:EXPERTS], A32, main.unsqueeze(2).to_broadcast([P, PICK_TILES, EXPERTS]), ALU.mult)
        rank1 = R(PICK_TILES)
        m = ts([m], rank1, rank, 1.0, ALU.add)

        def place_of(m, cols):
            n = cols.stop - cols.start
            b32 = blocks.bitcast(F32)[:, :, cols]
            t = prod[:, 0:TT, 0:n]
            spread = lambda c: rank1[:, c * TT:(c + 1) * TT].unsqueeze(2).to_broadcast([P, TT, n])
            m = tt([m], place[:, :, cols], b32[:, 0:TT, :], spread(0), ALU.mult)
            m = tt([m], t, b32[:, TT:2 * TT, :], spread(1), ALU.mult)
            return tt([m], place[:, :, cols], place[:, :, cols], t, ALU.add)

        m = place_done = place_of(m, slice(0, EXPERTS))
        hot = Rotation([self.shaped(ap, (TT, 4, CAP)) for ap in self.hot_places(hot_at)])
        slot_T = Rotation([self.shaped(self.xT[:, i * 2048:(i + 1) * 2048], (DC, 4 * CAP)) for i in range(2)])
        hot_of, turned_of = {}, {}

        placed = [place_done]

        def choose(quad):
            b = hot.take()
            for i in range(TT):
                m = tt([placed, b.free], b.ap[:, i],
                       self.c("slot")[:, 0:CAP].unsqueeze(1).to_broadcast([P, 4, CAP]),
                       place[:, i, 4 * quad:4 * quad + 4].unsqueeze(2).to_broadcast([P, 4, CAP]), ALU.is_equal)
            hot_of[quad] = b, m

        choose(0)
        rest_of_h()
        for i in range(TT):
            for half in range(2):
                bank = self.banks.take()
                for j in range(4):
                    m = self.turn([self.x_done, bank.free], bank.ap[:, j * P:(j + 1) * P],
                                  self.xT3[:, half * 4 + j, i * P:(i + 1) * P], signal=j == 3)
                x_rows.append(self.copy([m], x_tok[:, i, half * 512:(half + 1) * 512], bank.ap, "scalar"))
                bank.release(x_rows[-1])

        pairs = EXPERTS // 2 + OVER // 2
        row_index = self.index[:, 0:pairs]
        w_index = self.index[:, pairs:pairs + OVER]
        any_over = self.index[:, pairs + OVER:pairs + OVER + 1]

        def find_picks():
            over = R(MORE + 1)
            counts = R(1)
            m_x = self.copy([m_c], counts[0:64, :], bank2.ap[0:64, 0:1], "vector")
            bank2.release(m_x)
            m_x = ts([m_x], over[0:64, 0:MORE], self.c("caps", 64), counts[0:64, 0:1], ALU.is_lt)
            m_x = red([m_x], over[0:64, MORE:MORE + 1], over[0:64, 0:MORE], ALU.add)
            m_x = ts([m_x, router_turned], tmp[0:64, 0:P], self.c("ones", 64), over[0:64, MORE:MORE + 1], ALU.mult)
            yield
            bank = self.banks.take()
            m_x = self.mm([m_x, bank.free], bank.ap[:, 0:64], tmp[0:64, 0:P], self.c("before", 64)[:, 0:64], True, True)
            spread_e = lambda ap: ap.unsqueeze(1).to_broadcast([P, PICK_TILES, EXPERTS])
            m = tt([place_done, m_x], prod, A32, spread_e(bank.ap[:, 0:64]), ALU.mult)
            bank.release(m)
            m = red([m], off, prod, ALU.add)
            m = tt([m], prod, A32, spread_e(self.c("expert")), ALU.mult)
            m = red([m], who_e, prod, ALU.add)
            scr = blocks[:, :, EXPERTS:]
            m = tt([m], q_blk, off, blk, ALU.add)
            m = self.stt([m], main, main, -1.0, self.c("ones")[:, 0:8], ALU.mult, ALU.add)
            m = tt([m], q_blk, q_blk, main, ALU.mult)
            m = ts([m], q_blk, q_blk, -1.0, ALU.add)
            m = slots_done = tt([m], scr, q_blk.unsqueeze(2).to_broadcast([P, PICK_TILES, OVER]),
                   self.c("block").unsqueeze(1).to_broadcast([P, PICK_TILES, OVER]), ALU.is_equal)
            over_placed = place_of(slots_done, slice(EXPERTS, EXPERTS + OVER))
            m = over_placed
            placed.append(over_placed)
            for n in range(PICK_TILES):
                m = ts([m, m_x], who[:, n, :], self.c("slot"), rank1[:, n:n + 1], ALU.is_equal,
                       self.c("pick")[:, n:n + 1], ALU.mult)
            yield
            bank = self.banks.take()
            for n in range(PICK_TILES):
                m_t = self.mm([m, bank.free], bank.ap[:, 0:EXPERTS + OVER], who[:, n, :], blocks[:, n, :], n == 0, n == PICK_TILES - 1)
            zero = R(PICK_TILES)
            m = ts([m], zero, rank, 0.0, ALU.is_equal)
            m = tt([m], zero, zero, who_e, ALU.mult)
            for n in range(PICK_TILES):
                m = ts([m, m_t], who[:, n, :], self.c("ones"), zero[:, n:n + 1], ALU.mult)
            yield
            bank_e = self.banks.take()
            for n in range(PICK_TILES):
                m_e = self.mm([m, bank_e.free], bank_e.ap[:, 0:OVER], who[:, n, :], scr[:, n, :], n == 0, n == PICK_TILES - 1)
            val, none = R(pairs), R(pairs)
            for par in range(2):
                rows = slice(par * 64, par * 64 + 64)
                m = self.copy([m_t], val[rows, 0:32], bank.ap[rows, par:64:2], "vector")
                m = self.copy([m_t], val[rows, 32:40], bank.ap[rows, 64 + par:80:2], "vector")
            m = ts([m], none, val, 0.0, ALU.is_equal, FAR, ALU.mult)
            m = self.stt([m], val, val, -1.0, none, ALU.add, ALU.add)
            m = self.copy([m], row_index, val, "vector")
            self.index_done = m
            v2, n2 = R(OVER), R(OVER)
            m = ts([m_e], n2, bank_e.ap[:, 0:OVER], 0.0, ALU.is_equal, FAR, ALU.mult)
            m = self.stt([m], v2, bank_e.ap[:, 0:OVER], float(P), n2, ALU.mult, ALU.add)
            bank.release(m)
            m = ts([m], v2, v2, self.c("part"), ALU.add)
            m = self.copy([m], w_index, v2, "vector")
            self.w_index_done = m = self.copy([m], any_over, bank_e.ap[:, 0:1], "vector")
            bank_e.release(m)
            for b in y_buf.buffers + hid.buffers[1:]:
                b.free = [m_e, m]
            self.gates_done = gate()
            yield

        self.work_at = keep_at
        hid = Rotation([self.area(3 * DE) for _ in range(2)])
        y_buf = Rotation([self.area(D) for _ in range(2)])
        hid.buffers[0].free = [m_c]
        for b in slot_T.buffers:
            b.free = x_rows
        for n, b in enumerate(y_buf.buffers):
            b.lane = self.lane(f"y_out{n}")
        y_out = []

        def gather(quad, half):
            b, chosen = hot_of[quad]
            if half == 0:
                turned_of[quad] = slot_T.take(), []
            s, out = turned_of[quad]
            for k in range(4 * half, 4 * half + 4, 2):
                bank = self.banks.take()
                for kk in range(2):
                    for part in range(2):
                        for i in range(TT):
                            m = self.mm([bank.free, chosen, rows_done], bank.ap[:, kk * 256:(kk + 1) * 256],
                                        h_tok[part][:, i, k + kk, :], b.ap[:, i].rearrange("p a b -> p (a b)"),
                                        part + i == 0, part == 1 and i == TT - 1)
                m = self.copy([m, s.free], s.ap[:, k:k + 2, :], bank.ap.rearrange("p (a b) -> p a b", a=2),
                              "scalar" if (k // 2) % 2 else "vector")
                bank.release(m)
                out.append(m)
            if half:
                b.release(*out)

        def up(bank, s, ready, block, w):
            half, at, w = block % 2, block % 4 * CAP, w[0]
            sides = w.ap[:, 0:2 * DC * DE].rearrange("p (s k n) -> p k s n", s=2, k=DC)
            for k in range(DC):
                m = self.mm([bank.free, w.landed, ready], bank.ap[half * CAP:(half + 1) * CAP, :],
                            s.ap[:, k, at:at + CAP], sides[:, k], k == 0, k == DC - 1)
            w.release(m)
            return m

        def hidden_of(bank, m):
            b = hid.take()
            act, hT_ = b.ap[:, 0:DE], b.ap[:, DE:3 * DE]
            m = self.act([m, b.free], act, bank.ap[:, 0:DE], ACT.Silu)
            m = self.tt([m], act, act, bank.ap[:, DE:2 * DE], ALU.mult)
            bank.release(m)
            b.ready, b.turned = m, hT_
            return b

        def turn_hidden(b):
            bank = self.banks.take()
            act = b.ap[:, 0:DE]
            for fc in range(2):
                m = self.turn([b.ready, bank.free], bank.ap[:, fc * P:(fc + 1) * P], act[:, fc:DE:2], signal=fc == 1)
            b.ready = self.copy([m], b.turned[:, 0:DE], bank.ap[:, 0:DE], "scalar")
            bank.release(b.ready)

        def down(banks, b, half, w):
            w = w[1]
            wd = self.shaped(w.ap, (2, D))
            for n in range(2):
                for fc in range(2):
                    m = self.mm([banks[0].free, banks[1].free, b.ready, w.landed], banks[n].ap[half * CAP:(half + 1) * CAP, :],
                                b.turned[:, fc * P + half * CAP:fc * P + (half + 1) * CAP],
                                wd[:, fc, n * 512:(n + 1) * 512], fc == 0, fc == 1)
            w.release(m)
            return m

        def finish(pr, b, weights):
            banks = [self.banks.take() for _ in range(2)]
            for half in range(2):
                m = down(banks, b, half, weights[half])
            b.release(m)
            y = y_buf.take()
            out = []
            for n in range(2):
                mc = self.copy([m, y.free], y.ap[:, n * 512:(n + 1) * 512], banks[n].ap, "scalar" if n else "vector")
                banks[n].release(mc)
                out.append(mc)
            done = y.lane.indirect([out, self.index_done], out=y_rows, out_offset=bass.IndirectOffsetOnAxis(ap=row_index[:, pr:pr + 1], axis=0),
                                   in_=y.ap, in_offset=None, bounds_check=PICKS - 1, oob_is_err=False)
            y.release(done)
            y_out.append(done)

        def run_pairs(first, last, load, meanwhile=iter(())):
            quads = (first // 2, last // 2)
            if quads[0] not in hot_of:
                choose(quads[0])
            for half in range(2):
                next(meanwhile, None)
                gather(quads[0], half)
            pending = None
            for pr in range(first, last):
                quad, odd = pr // 2, pr % 2
                if not odd and quad + 1 < quads[1]:
                    choose(quad + 1)
                s, ready = turned_of[quad]
                weights = [load(2 * pr), load(2 * pr + 1)]
                bank = self.banks.take()
                up(bank, s, ready, 2 * pr, weights[0])
                next(meanwhile, None)
                if pending:
                    finish(*pending)
                if quad + 1 < quads[1]:
                    gather(quad + 1, odd)
                next(meanwhile, None)
                m = up(bank, s, ready, 2 * pr + 1, weights[1])
                next(meanwhile, None)
                if odd:
                    s.release(m)
                b = hidden_of(bank, m)
                pending = (pr, b, weights)
                turn_hidden(b)
                next(meanwhile, None)
            finish(*pending)

        main_pairs = EXPERTS // 2
        run_pairs(0, main_pairs, load_expert, find_picks())
        q.stage()
        q.guard(any_over[0:1, :])
        for n, b in enumerate(y_buf.buffers):
            b.lane = self.lane(f"overflow_y_out{n}")
        main_out = y_out[-2:]
        run_pairs(main_pairs, main_pairs + OVER // 2, lambda n: load_overflow(n - EXPERTS, w_index, self.w_index_done))
        q.end_guard(self.nc, self.ctx, [b.free for b in y_buf.buffers])
        y_out = main_out

        q.wait("scalar", y_out)
        marks = q.stage()
        self.work_at = TT * D
        ys = [self.area(D) for _ in range(2 * TT)] if self.work_at + 2 * TT * D <= self.WORK else None
        lanes = [self.lane(f"y_in{i}") for i in range(TT)]
        out_lane = self.lane("out")
        for i in range(TT):
            for c in range(TOP_K):
                landed = lanes[i].copy("scalar", [marks], ys[2 * i + c], y_rows[c * T + i * P:c * T + (i + 1) * P, :])
            m = x_rows
            for c in range(TOP_K):
                m = [self.stt([landed, m, self.gates_done], x_tok[:, i, :], ys[2 * i + c], gates[:, c, i:i + 1], x_tok[:, i, :],
                              ALU.mult, ALU.add)]
            final = out_lane.copy("sync", m, d["out"][i * P:(i + 1) * P, :], x_tok[:, i, :])
        q.wait("sync", [final])


STAGES = ("block1_mixer", "block1_mlp", "block2_attention", "deltanet", "moe")


def build(nc, dram, stages=STAGES):
    with ExitStack() as ctx:
        k = Kernel(nc, ctx, dram)
        for s in stages:
            {"block1_mixer": k.block1_mixer, "block1_mlp": k.block1_mlp, "block2_attention": k.block2_attention,
             "deltanet": k.deltanet, "moe": k.moe}[s]()
        block = ctx.enter_context(nc.Block())
        k.q.play(block)
    return k


def pack(x):
    f = np.float32
    a = {k: np.asarray(v) for k, v in x.items()}
    flat = lambda n: a[n].reshape(-1)
    gain = lambda n: np.concatenate([flat(n), flat(n)])
    vec = np.concatenate([
        flat("mod_b"), flat("c"), flat("norm1_g"), flat("norm2_g"), flat("final_g"), flat("ln1_g_2"),
        flat("ln2_g_2"), flat("pool_scale"), flat("ffn_conv_b"), flat("ffn_conv_w"), flat("dn_conv_w_2"),
        gain("attn_q_norm_g_2"), gain("attn_k_norm_g_2")]).reshape(-1, P)
    vec = np.concatenate([vec, np.zeros((VEC_TILES * P - len(vec), P), f)])
    row = np.concatenate([
        flat("attn_out_norm_g_2"), flat("dn_out_norm_g_2"), flat("b_f"), flat("router_group_b_2"),
        flat("router_expert_b_2"), flat("dn_dt_bias_2"), flat("dn_a_log_2")])[None, :]
    rpb = a["attn_rpb_2"][0]
    side = GRID - WIN_W
    return {
        "x": a["x"][0], "mod_w": a["mod_w"][0], "w_in": a["w_in"][0], "w_out": a["w_out"][0],
        "ffn_up": a["ffn_up"][0], "ffn_down": a["ffn_down"][0], "pool_w": a["pool_w"][0],
        "w_in_2": a["w_in_2"][0], "w_out_2": a["w_out_2"][0],
        "router_w": np.concatenate([a["router_group_w_2"][0], a["router_expert_w_2"][0]], 1),
        "w_gate": a["expert_w_gate_2"].reshape(EXPERTS * P, DC * DE),
        "w_up": a["expert_w_up_2"].reshape(EXPERTS * P, DC * DE),
        "w_down": a["expert_w_down_2"].reshape(EXPERTS * P, 2 * D),
        "rpb": np.pad(rpb, ((0, 0), (0, 0), (side, side)))[:, :, ::-1],
        "channel_vectors": vec, "row_vectors": row,
        "constants": np.concatenate(list(constants().values()), 1),
    }


def kernel(**inputs):
    from concourse import bacc
    from concourse.bass_utils import run_bass_kernel_spmd

    arrays = {n: np.ascontiguousarray(v) for n, v in pack(inputs).items()}
    nc = bacc.Bacc("TRN2", target_bir_lowering=False, num_devices=1)
    dram = {n: nc.dram_tensor(f"{n}_dram", v.shape, mybir.dt.from_np(v.dtype), kind="ExternalInput").ap()
            for n, v in arrays.items()}
    dram["out"] = nc.dram_tensor("out_dram", (T, D), F32, kind="ExternalOutput").ap()
    build(nc, dram)
    r = run_bass_kernel_spmd(nc, [{f"{n}_dram": v for n, v in arrays.items()}], core_ids=[0])
    return r.results[0]["out_dram"].reshape(1, T, D)
```
